# Optimizing a Trainium2 kernel written in Bass

```python
import math
import jax
import jax.numpy as jnp
from jax import lax
import numpy as np

D_MODEL = 2048
BATCH = 1
SEQ = 256
DEPTH = 1

A_HEADS = 8
A_DQK = 64
A_DV = 2 * A_DQK
B_HEADS = 16
B_GROUPS = 4
B_HPG = B_HEADS // B_GROUPS
B_DH = 64
CMP_LEN = 32
CMP_STRIDE = 16
CMP_HIDDEN = 256
SEL_BLOCK = 64
SEL_TOPN = 16
WINDOW = 512
N_NSA_BRANCH = 3
MEM_TOKENS = 256
M_HEADS = 4
M_DH = 256
REL_BUCKETS = 32
REL_MAX_DIST = 1024
PEER_HEADS = 8
PEER_NKEYS = 128
PEER_DKEY = 256
PEER_TOPK = 16
PEER_EXPERTS = PEER_NKEYS * PEER_NKEYS
N_BRANCH = 3
MIX_W = 1024
IN_WIDTHS = (A_HEADS * 2 * A_DQK, A_HEADS * 2 * A_DQK, A_HEADS * A_DV, B_HEADS * B_DH, N_NSA_BRANCH * 2 * B_GROUPS * B_DH, N_NSA_BRANCH * B_HEADS, M_HEADS * M_DH, N_BRANCH * D_MODEL)
C_IN = sum(IN_WIDTHS)
Q_BLOCK = 128
PEER_CHUNK = 128
LN_EPS = 1e-5
FORCE = 1e9
ALPHA = (2 * DEPTH) ** 0.25
BETA = (8 * DEPTH) ** -0.25

kernel_name = 'hybrid_diffattn_nsa_mem_peer_deepnorm'

def lambda_init(layer_idx):
    return 0.8 - 0.6 * math.exp(-0.3 * layer_idx)

def layer_norm(x, g, b):
    xf = x.astype(jnp.float32)
    mu = jnp.mean(xf, axis=-1, keepdims=True)
    var = jnp.mean(jnp.square(xf - mu), axis=-1, keepdims=True)
    return ((xf - mu) * lax.rsqrt(var + LN_EPS) * g + b).astype(x.dtype)

def rms_norm(x, g):
    xf = x.astype(jnp.float32)
    return (xf * lax.rsqrt(jnp.mean(jnp.square(xf), axis=-1, keepdims=True) + LN_EPS) * g).astype(x.dtype)

def masked_softmax(s, mask):
    s = jnp.where(mask, s.astype(jnp.float32), -jnp.inf)
    m = jnp.max(s, axis=-1, keepdims=True)
    m = jnp.where(jnp.isfinite(m), m, 0.0)
    e = jnp.where(mask, jnp.exp(s - m), 0.0)
    return e / jnp.maximum(jnp.sum(e, axis=-1, keepdims=True), 1e-30)

def rel_bucket(dist):
    n = jnp.maximum(dist, 0)
    max_exact = REL_BUCKETS // 2
    nf = jnp.maximum(n, 1).astype(jnp.float32)
    large = max_exact + (jnp.log(nf / max_exact) / math.log(REL_MAX_DIST / max_exact) * (REL_BUCKETS - max_exact)).astype(jnp.int32)
    large = jnp.minimum(large, REL_BUCKETS - 1)
    return jnp.where(n < max_exact, n, large)

def group_bias(tab_g, bkt):
    return jnp.moveaxis(tab_g[:, bkt], 0, 1)

def gather_blocks(blocks, idx):
    g = jax.vmap(jax.vmap(lambda kb, i: kb[i]))(blocks, idx)
    return g.reshape(idx.shape[0], idx.shape[1], idx.shape[2], -1, blocks.shape[-1])

def diff_attention(q, k, v, lam_params, subln_g, rel_tab, lam_init):
    B, T = q.shape[:2]
    nb = T // Q_BLOCK
    qh = q.transpose(0, 2, 3, 1, 4)
    kh = k.transpose(0, 2, 3, 1, 4)
    vh = v.transpose(0, 2, 1, 3)
    q_blocks = jnp.moveaxis(qh.reshape(B, A_HEADS, 2, nb, Q_BLOCK, A_DQK), 3, 0)
    lp = lam_params.astype(jnp.float32)
    lam = jnp.exp(jnp.sum(lp[0] * lp[1])) - jnp.exp(jnp.sum(lp[2] * lp[3])) + lam_init
    kpos = jnp.arange(T)
    scale = A_DQK ** -0.5

    def block(args):
        q_blk, i = args
        qpos = i * Q_BLOCK + jnp.arange(Q_BLOCK)
        dist = qpos[:, None] - kpos[None, :]
        bias = jnp.moveaxis(rel_tab[rel_bucket(dist)], -1, 0)
        s = jnp.einsum('bhmqd,bhmkd->bhmqk', q_blk, kh).astype(jnp.float32) * scale + bias[:, None]
        p = masked_softmax(s, dist >= 0)
        w = p[:, :, 0] - lam * p[:, :, 1]
        return jnp.einsum('bhqk,bhkd->bhqd', w.astype(vh.dtype), vh)

    o = lax.map(block, (q_blocks, jnp.arange(nb)))
    o = jnp.moveaxis(o, 0, 2).reshape(B, A_HEADS, T, A_DV).transpose(0, 2, 1, 3)
    o = rms_norm(o, subln_g) * (1.0 - lam_init)
    return o.reshape(B, T, A_HEADS * A_DV)

def nsa_attention(q, kv, gate_logits, cmp_pe, cmp_w1, cmp_w2, rel_tab):
    B, T = q.shape[:2]
    nb = T // Q_BLOCK
    n_sel = T // SEL_BLOCK
    n_top = min(SEL_TOPN, n_sel)
    n_c = (T - CMP_LEN) // CMP_STRIDE + 1
    scale = B_DH ** -0.5
    tpos = jnp.arange(T)
    qh = q.reshape(B, T, B_GROUPS, B_HPG, B_DH).transpose(0, 2, 3, 1, 4)
    kv = kv.transpose(2, 3, 0, 4, 1, 5)

    cidx = jnp.arange(n_c)[:, None] * CMP_STRIDE + jnp.arange(CMP_LEN)[None, :]

    def compress(raw, pe, w1, w2):
        blk = raw[:, :, cidx] + pe
        return jax.nn.gelu(blk.reshape(B, B_GROUPS, n_c, CMP_LEN * B_DH) @ w1) @ w2

    k_cmp = compress(kv[0, 0], cmp_pe[0], cmp_w1[0], cmp_w2[0])
    v_cmp = compress(kv[0, 1], cmp_pe[1], cmp_w1[1], cmp_w2[1])
    c_end = jnp.arange(n_c) * CMP_STRIDE + CMP_LEN - 1
    s_c = jnp.einsum('bghtd,bgcd->bghtc', qh, k_cmp).astype(jnp.float32) * scale
    p_c = masked_softmax(s_c, c_end[None, :] <= tpos[:, None])
    o_cmp = jnp.einsum('bghtc,bgcd->bghtd', p_c.astype(v_cmp.dtype), v_cmp)

    overlap = jax.nn.one_hot(cidx // SEL_BLOCK, n_sel, dtype=jnp.float32).mean(axis=1)
    imp = jnp.einsum('bghtc,cj->bgtj', p_c, overlap)
    blk_ids = jnp.arange(n_sel)[None, :]
    cur = (tpos // SEL_BLOCK)[:, None]
    forced = (blk_ids == 0) | (blk_ids == cur) | (blk_ids == cur - 1)
    future = blk_ids * SEL_BLOCK > tpos[:, None]
    imp = jnp.where(forced, FORCE, jnp.where(future, -FORCE, imp))
    _, sel_idx = lax.top_k(imp, n_top)

    ks_blocks = kv[1, 0].reshape(B, B_GROUPS, n_sel, SEL_BLOCK, B_DH)
    vs_blocks = kv[1, 1].reshape(B, B_GROUPS, n_sel, SEL_BLOCK, B_DH)
    pad = ((0, 0), (0, 0), (WINDOW, 0), (0, 0))
    k_wp = jnp.pad(kv[2, 0], pad)
    v_wp = jnp.pad(kv[2, 1], pad)
    tab_g = rel_tab.T.reshape(B_GROUPS, B_HPG, REL_BUCKETS)

    q_blocks = jnp.moveaxis(qh.reshape(B, B_GROUPS, B_HPG, nb, Q_BLOCK, B_DH), 3, 0)
    sel_blocks = jnp.moveaxis(sel_idx.reshape(B, B_GROUPS, nb, Q_BLOCK, n_top), 2, 0)

    def block(args):
        q_blk, sel_b, i = args
        q0 = i * Q_BLOCK
        qpos = q0 + jnp.arange(Q_BLOCK)
        kg = gather_blocks(ks_blocks, sel_b)
        vg = gather_blocks(vs_blocks, sel_b)
        kpos = (sel_b[..., None] * SEL_BLOCK + jnp.arange(SEL_BLOCK)).reshape(B, B_GROUPS, Q_BLOCK, -1)
        dist = qpos[:, None] - kpos
        bias = jax.vmap(group_bias, in_axes=(0, 1), out_axes=1)(tab_g, rel_bucket(dist))
        s = jnp.einsum('bghqd,bgqkd->bghqk', q_blk, kg).astype(jnp.float32) * scale + bias
        p = masked_softmax(s, (dist >= 0)[:, :, None])
        o_sel = jnp.einsum('bghqk,bgqkd->bghqd', p.astype(vg.dtype), vg)
        kw = lax.dynamic_slice_in_dim(k_wp, q0, WINDOW + Q_BLOCK, axis=2)
        vw = lax.dynamic_slice_in_dim(v_wp, q0, WINDOW + Q_BLOCK, axis=2)
        kpos_w = q0 - WINDOW + jnp.arange(WINDOW + Q_BLOCK)
        dist_w = qpos[:, None] - kpos_w[None, :]
        mask_w = (dist_w >= 0) & (dist_w < WINDOW) & (kpos_w >= 0)[None, :]
        bias_w = jnp.moveaxis(rel_tab[rel_bucket(dist_w)], -1, 0).reshape(B_GROUPS, B_HPG, Q_BLOCK, -1)
        s_w = jnp.einsum('bghqd,bgkd->bghqk', q_blk, kw).astype(jnp.float32) * scale + bias_w
        p_w = masked_softmax(s_w, mask_w)
        o_win = jnp.einsum('bghqk,bgkd->bghqd', p_w.astype(vw.dtype), vw)
        return o_sel, o_win

    o_sel, o_win = lax.map(block, (q_blocks, sel_blocks, jnp.arange(nb)))

    def unblock(o):
        return jnp.moveaxis(o, 0, 3).reshape(B, B_GROUPS, B_HPG, T, B_DH)

    g = jax.nn.sigmoid(gate_logits.astype(jnp.float32)).astype(q.dtype)
    g = g.reshape(B, T, N_NSA_BRANCH, B_GROUPS, B_HPG).transpose(2, 0, 3, 4, 1)[..., None]
    o = g[0] * o_cmp + g[1] * unblock(o_sel) + g[2] * unblock(o_win)
    return o.transpose(0, 3, 1, 2, 4).reshape(B, T, B_HEADS * B_DH)

def memory_attention(q, mem, w_kv):
    B, T = q.shape[:2]
    qh = q.reshape(B, T, M_HEADS, M_DH)
    kv = (mem @ w_kv).reshape(B, mem.shape[1], 2, M_HEADS, M_DH)
    s = jnp.einsum('bthd,bmhd->bhtm', qh, kv[:, :, 0]).astype(jnp.float32) * (M_DH ** -0.5)
    p = jax.nn.softmax(s, axis=-1)
    o = jnp.einsum('bhtm,bmhd->bthd', p.astype(kv.dtype), kv[:, :, 1])
    return o.reshape(B, T, M_HEADS * M_DH)

def peer_ffn(x, w_q, sub_keys, u_tab, v_tab):
    B, T, D = x.shape
    n_tok = B * T
    xf = x.reshape(n_tok, D)
    q = (xf @ w_q).reshape(n_tok, PEER_HEADS, 2, PEER_DKEY // 2)
    s = jnp.einsum('nhcd,hckd->nhck', q, sub_keys).astype(jnp.float32)
    s_top, i_top = lax.top_k(s, PEER_TOPK)
    comb = (s_top[:, :, 0, :, None] + s_top[:, :, 1, None, :]).reshape(n_tok, PEER_HEADS, -1)
    cand = (i_top[:, :, 0, :, None] * PEER_NKEYS + i_top[:, :, 1, None, :]).reshape(n_tok, PEER_HEADS, -1)
    s_fin, pos = lax.top_k(comb, PEER_TOPK)
    experts = jnp.take_along_axis(cand, pos, axis=-1)
    gate = jax.nn.softmax(s_fin, axis=-1)
    nc = n_tok // PEER_CHUNK

    def chunk(args):
        xc, ec, gc = args
        hid = jax.nn.gelu(jnp.einsum('cd,chkd->chk', xc, u_tab[ec]).astype(jnp.float32))
        return jnp.einsum('chk,chkd->cd', (gc * hid).astype(v_tab.dtype), v_tab[ec])

    out = lax.map(chunk, (xf.reshape(nc, PEER_CHUNK, D), experts.reshape(nc, PEER_CHUNK, PEER_HEADS, PEER_TOPK), gate.reshape(nc, PEER_CHUNK, PEER_HEADS, PEER_TOPK)))
    return out.reshape(B, T, D)

def setup_inputs(seed: int = 0) -> dict:
    key = jax.random.key(seed)
    ks = jax.random.split(key, 20)
    f32 = jnp.float32
    nrm = lambda k, shape, sc: jax.random.normal(k, shape, f32) * sc
    return {
        'x': nrm(ks[0], (BATCH, SEQ, D_MODEL), 1.0),
        'mem': nrm(ks[1], (BATCH, MEM_TOKENS, D_MODEL), 1.0),
        'w_in': nrm(ks[2], (DEPTH, D_MODEL, C_IN), D_MODEL ** -0.5),
        'diff_lambda': nrm(ks[3], (DEPTH, 4, A_DQK), 0.1),
        'diff_subln': 1.0 + nrm(ks[4], (DEPTH, A_DV), 0.02),
        'cmp_pe': nrm(ks[5], (DEPTH, 2, CMP_LEN, B_DH), 0.1),
        'cmp_w1': nrm(ks[6], (DEPTH, 2, CMP_LEN * B_DH, CMP_HIDDEN), (CMP_LEN * B_DH) ** -0.5),
        'cmp_w2': nrm(ks[7], (DEPTH, 2, CMP_HIDDEN, B_DH), CMP_HIDDEN ** -0.5),
        'w_mem_kv': nrm(ks[8], (DEPTH, D_MODEL, 2 * M_HEADS * M_DH), D_MODEL ** -0.5),
        'w_branch': nrm(ks[9], (DEPTH, N_BRANCH, MIX_W, D_MODEL), MIX_W ** -0.5),
        'w_out': nrm(ks[10], (DEPTH, D_MODEL, D_MODEL), BETA * D_MODEL ** -0.5),
        'ln1_g': 1.0 + nrm(ks[11], (DEPTH, D_MODEL), 0.02),
        'ln1_b': nrm(ks[12], (DEPTH, D_MODEL), 0.02),
        'peer_wq': nrm(ks[13], (DEPTH, D_MODEL, PEER_HEADS * PEER_DKEY), D_MODEL ** -0.5),
        'peer_keys': nrm(ks[14], (DEPTH, PEER_HEADS, 2, PEER_NKEYS, PEER_DKEY // 2), (PEER_DKEY // 2) ** -0.5),
        'peer_u': nrm(ks[15], (DEPTH, PEER_EXPERTS, D_MODEL), D_MODEL ** -0.5),
        'peer_v': nrm(ks[16], (DEPTH, PEER_EXPERTS, D_MODEL), BETA),
        'ln2_g': 1.0 + nrm(ks[17], (DEPTH, D_MODEL), 0.02),
        'ln2_b': nrm(ks[18], (DEPTH, D_MODEL), 0.02),
        'rel_bias': nrm(ks[19], (REL_BUCKETS, A_HEADS + B_HEADS), 0.3),
    }

def reference(x, mem, w_in, diff_lambda, diff_subln, cmp_pe, cmp_w1, cmp_w2, w_mem_kv, w_branch, w_out, ln1_g, ln1_b, peer_wq, peer_keys, peer_u, peer_v, ln2_g, ln2_b, rel_bias):
    split_at = np.cumsum(IN_WIDTHS)[:-1].tolist()
    for l in range(DEPTH):
        B, T, _ = x.shape
        h = x @ w_in[l]
        a_q, a_k, a_v, b_q, b_kv, b_g, m_q, merge = jnp.split(h, split_at, axis=-1)
        o_a = diff_attention(a_q.reshape(B, T, A_HEADS, 2, A_DQK), a_k.reshape(B, T, A_HEADS, 2, A_DQK), a_v.reshape(B, T, A_HEADS, A_DV), diff_lambda[l], diff_subln[l], rel_bias[:, :A_HEADS], lambda_init(l))
        o_b = nsa_attention(b_q.reshape(B, T, B_HEADS, B_DH), b_kv.reshape(B, T, N_NSA_BRANCH, 2, B_GROUPS, B_DH), b_g.reshape(B, T, N_NSA_BRANCH, B_HEADS), cmp_pe[l], cmp_w1[l], cmp_w2[l], rel_bias[:, A_HEADS:])
        o_m = memory_attention(m_q, mem, w_mem_kv[l])
        branches = jnp.stack([o_a, o_b, o_m], axis=2)
        up = jnp.einsum('btnc,ncd->btnd', branches, w_branch[l])
        gates = jax.nn.sigmoid(merge.astype(jnp.float32)).astype(x.dtype).reshape(B, T, N_BRANCH, D_MODEL)
        y = jnp.sum(gates * up, axis=2) @ w_out[l]
        x = layer_norm(ALPHA * x + y, ln1_g[l], ln1_b[l])
        x = layer_norm(ALPHA * x + peer_ffn(x, peer_wq[l], peer_keys[l], peer_u[l], peer_v[l]), ln2_g[l], ln2_b[l])
    return x


_drawn_inputs = setup_inputs


def setup_inputs(seed=0):
    import zlib

    import numpy as np

    out = dict(_drawn_inputs(seed))
    spreads = {}
    factors = {'diff_lambda': 4.764, 'diff_subln': 2.971, 'ln2_g': 2.823, 'ln2_b': 2.841}
    for name, (base, spread) in spreads.items():
        noise = np.random.default_rng([zlib.crc32(name.encode()), seed]).standard_normal(out[name].shape)
        drawn = base * np.exp(spread * noise) if base else spread * noise
        out[name] = jnp.asarray(drawn.astype(out[name].dtype))
    for name, factor in factors.items():
        out[name] = (out[name] * factor).astype(out[name].dtype)
    return out
```

```python
import math
from contextlib import ExitStack

import numpy as np

import concourse.bass as bass
from concourse import mybir

F32 = mybir.dt.float32
U32 = mybir.dt.uint32
ALU = mybir.AluOpType
ACT = mybir.ActivationFunctionType
AX = mybir.AxisListType

P = 128
T = 256
NT = T // P
D = 2048
DC = D // P
A_HEADS, A_DQK, A_DV = 8, 64, 128
B_HEADS, B_GROUPS, B_DH = 16, 4, 64
B_HPG = B_HEADS // B_GROUPS
CMP_LEN, CMP_STRIDE, CMP_HIDDEN = 32, 16, 256
N_CMP = (T - CMP_LEN) // CMP_STRIDE + 1
M_HEADS, M_DH = 4, 256
BUCKETS, MAX_DIST = 32, 1024
HEADS = A_HEADS + B_HEADS
MIX_C = 1024 // P
PEER_HEADS, NKEYS, TOPK = 8, 128, 16
PICKS = PEER_HEADS * TOPK
LN_EPS = 1e-5
ALPHA = 2.0 ** 0.25
BETA_LAM = 0.8 - 0.6
NEG = -1e30

RING = 4
PHASES = [("mem_k", 8), ("mem_v", 8), ("qk", 40), ("v", 12), ("cmp_w1", 4), ("merge", 48),
          ("w_out", 16), ("wq", 16), ("u", NKEYS), ("v_tab", NKEYS)]
BASE = {}
_n = 0
for _name, _count in PHASES:
    BASE[_name] = _n
    _n += _count
CHUNKS = _n
CW = 2048
assert all(c % RING == 0 for _, c in PHASES)

Q_A, Q_B, Q_M, K_A, K_SEL, K_WIN, RAW_K, RAW_V = 0, 8, 16, 24, 32, 34, 36, 38
V_A, V_SEL, V_WIN, NV_W = 0, 1024, 1280, 1536

SB = 52736
O_RING = 0
O_XT = O_RING + RING * CW
O_S = O_XT + DC * T
O_MISC = O_S + 4096
O_H = O_MISC + 3584
O_QK = O_H
O_RAWP = O_QK + 40 * T
O_KM = O_RAWP + 2 * B_GROUPS * T
O_NV = O_KM + 8 * T
O_MV = O_NV + NT * NV_W
O_BIAS = O_MV + NT * 1024
O_OT = O_BIAS + HEADS * T
O_LEFT = O_OT + 24 * T
assert O_LEFT + 1024 == O_H + NKEYS * T == SB


def rel_buckets():
    n = np.arange(T)
    nf = np.maximum(n, 1).astype(np.float32)
    half = BUCKETS // 2
    large = half + (np.log(nf / np.float32(half)) / np.float32(math.log(MAX_DIST / half))
                    * np.float32(BUCKETS - half)).astype(np.int32)
    return np.where(n < half, n, np.minimum(large, BUCKETS - 1))


def build(nc, x, x_t, mem_t, stream, w_gate, w_branch, tab, buckets_rev, lam, subln, pe_cols, w2,
          keys_t, ln1_g, ln1_b, ln2_g, ln2_b, identity, flip, cmp_mask, iotas, out):
    ctx = ExitStack()
    with ctx:
        def sem(name):
            return ctx.enter_context(nc.semaphore(name))

        arena = ctx.enter_context(nc.sbuf_tensor("arena", [P, SB], F32))
        ps = ctx.enter_context(nc.psum_tensor("ps", [P, 8, 512], F32))
        bias_rows = nc.dram_tensor("bias_rows", [HEADS, 384], F32, kind="Internal")
        x1_dram = nc.dram_tensor("x1_dram", [P, NT * D], F32, kind="Internal")

        def at(off, n, parts=P):
            return arena[0:parts, off:off + n]

        ring = [at(O_RING + s * CW, CW) for s in range(RING)]
        xt = at(O_XT, DC * T).rearrange("p (c t) -> p c t", c=DC)
        memt = at(O_OT, DC * T).rearrange("p (c t) -> p c t", c=DC)
        qk = at(O_QK, 40 * T).rearrange("p (c t) -> p c t", c=40)
        rawp = at(O_RAWP, 2 * B_GROUPS * T).rearrange("p (k g t) -> p k g t", k=2, g=B_GROUPS)
        km = at(O_KM, 8 * T).rearrange("p (c t) -> p c t", c=8)
        nv = at(O_NV, NT * NV_W).rearrange("p (t n) -> p t n", t=NT)
        mv = at(O_MV, NT * 1024).rearrange("p (t n) -> p t n", t=NT)
        bias = at(O_BIAS, HEADS * T).rearrange("p (h k) -> p h k", h=HEADS)
        ot = at(O_OT, 24 * T).rearrange("p (c t) -> p c t", c=24)
        hank_a = at(O_S, 16 * T)
        hank_b = at(O_RAWP, 8 * T)
        pc = at(O_S, NT * 1024).rearrange("p (t c n) -> p t c n", t=NT, c=8)
        pct = at(O_RAWP, 8 * T).rearrange("p (c t) -> p c t", c=8)
        pt = [at(O_S + 2048 + 512 * i, 512) for i in range(2)]
        ee = [at(O_S + 3072 + 512 * i, 512) for i in range(2)] + [at(O_LEFT, 512)]
        m = O_MISC
        ident = at(m, P)
        ones = at(m + 128, P)
        iota = at(m + 256, P)
        stage = [at(m + 384 + 256 * i, T) for i in range(2)]
        gates = at(m + 896, NT * 48).rearrange("p (t n) -> p t n", t=NT)
        small = m + 992
        nmx = [at(small + 4 * i, 2) for i in range(3)]
        mxs = [at(small + 12 + 4 * i, 2) for i in range(3)]
        sums = [at(small + 24 + 4 * i, 2) for i in range(3)]
        rec = [at(small + 36 + 4 * i, 2) for i in range(3)]
        lam_sb = at(small + 48, 1)
        lam_tmp = at(small + 49, 4)
        subln_sb = at(small + 53, 1)
        bn = at(small + 56, 48).rearrange("p (t c s) -> p t c s", t=NT, c=4)
        mean_var = at(small + 104, 4).rearrange("p (t s) -> p t s", t=NT)
        rstd = at(small + 108, 2)
        eps_sb = at(small + 110, 1)
        w = small + 112
        flip_sb = at(w, P)
        wgate_sb = at(w + 128, DC * 48).rearrange("p (c n) -> p c n", c=DC)
        lam_in = at(w + 896, 256)
        pe_sb = at(w + 1152, 32).rearrange("p (k l) -> p k l", k=2)
        cmask = at(w + 1184, 60).rearrange("p (k t n) -> p k t n", k=2, t=NT)
        tab_sb = at(w + 1244, HEADS, BUCKETS)
        rows_sb = at(w + 1268, 384, HEADS)
        brev_sb = at(w + 1652, T, BUCKETS)
        w2_sb = at(w + 1268, 256).rearrange("p (k h n) -> p k h n", k=2, h=2)
        assert w + 1908 <= O_H
        hid = at(O_LEFT + 512, 2 * 2 * 60).rearrange("p (k h n) -> p k h n", k=2, h=2)
        hid_pe = at(O_LEFT + 752, 4).rearrange("p (k h) -> p k h", k=2)
        kbd = at(O_QK + RAW_K * T, 256).rearrange("p (j n) -> p j n", j=2)
        vbd = at(O_QK + RAW_K * T + 256, 256).rearrange("p (j n) -> p j n", j=2)
        cst = at(O_LEFT + 768, 64).rearrange("p (a b) -> p a b", a=4)
        rms = at(O_S + 2048, 2048)
        yt = at(O_S, DC * T).rearrange("p (c t) -> p c t", c=DC)
        yt_flat = at(O_S, DC * T)
        wb = [at(O_QK + 1024 * s, 1024).rearrange("p (c n) -> p c n", c=MIX_C) for s in range(RING)]
        gate_t = [at(O_LEFT + 256 * i, T) for i in range(2)]
        prod_t = [at(O_LEFT + 512 + 256 * i, T) for i in range(2)]
        xn = at(O_QK + 4096, NT * D).rearrange("p (t n) -> p t n", t=NT)
        gb = at(O_NV, 2 * D).rearrange("p (k n) -> p k n", k=2)
        pq = at(O_H + 28672, DC * T).rearrange("p (c t) -> p c t", c=DC)
        keys = at(O_H + 26624, DC * NKEYS).rearrange("p (c n) -> p c n", c=DC)
        sc = at(O_S, NT * D).rearrange("p (t n) -> p t n", t=NT)
        hx = at(O_H, NKEYS * T).rearrange("p (j t) -> p j t", j=NKEYS)
        vals = at(w, 256).rearrange("p (h c k) -> p h c k", h=PEER_HEADS, c=2)
        idx_u = at(w + 256, 256).bitcast(U32)
        idx_f = at(w + 512, 256).rearrange("p (h c k) -> p h c k", h=PEER_HEADS, c=2)
        comb = at(w + 768, 256)
        comb2 = at(w + 1024, 256)
        seg = at(w + 1024, P)
        fin = at(w + 1280, PICKS)
        pos_u = at(w + 1408, PICKS).bitcast(U32)
        pab_u = at(w + 1536, PICKS).bitcast(U32)
        pab_f = at(w + 1664, PICKS)
        picked = [at(O_XT + 0 * P, P)] * 0
        den = at(w + 1792, 16)
        nat = at(O_H + 24576, NT * 3 * P).rearrange("p (t k n) -> p t k n", t=NT, k=3)
        pick_t = at(w + 1024, 3 * T).rearrange("p (k t) -> p k t", k=3)
        hot = at(O_S, 2 * 2 * 4 * P).rearrange("p (b k a n) -> p b k a n", b=2, k=2, a=4)
        x1n = at(O_S, NT * D).rearrange("p (t n) -> p t n", t=NT)
        gb2 = at(O_XT, 2 * D).rearrange("p (k n) -> p k n", k=2)

        s_ring = [sem(f"chunk_landed_{s}") for s in range(RING)]
        s_xt, s_mem, s_first, s_wg, s_w2 = (sem(n) for n in (
            "x_t_landed", "mem_t_landed", "constants_landed", "gate_weights_landed", "w2_landed"))
        s_small = sem("small_inputs_landed")
        s_wb = [sem(f"branch_weights_landed_{s}") for s in range(RING)]
        s_xn, s_gb, s_x1s, s_keys, s_x1l, s_gb2, s_out = (sem(n) for n in (
            "x_landed", "ln1_params_landed", "x1_stored", "keys_landed", "x1_reloaded",
            "ln2_params_landed", "out_stored"))
        s_chunk = sem("chunk_used")
        s_evac = sem("projection_evacuated")
        s_rows, s_rowc, s_rowd, s_hank, s_flip, s_bias = (sem(n) for n in (
            "bias_rows_ready", "bias_rows_copied", "bias_rows_stored", "hankel_landed",
            "bias_flipped", "bias_copied"))
        s_bg, s_gates = sem("gate_logits_ready"), sem("gates_ready")
        s_raw, s_hid, s_hidc, s_w2mm, s_bd = (sem(n) for n in (
            "raw_paired", "cmp_hidden_ready", "cmp_hidden_copied", "cmp_kv_ready", "cmp_kv_copied"))
        s_cs, s_csx, s_cex, s_cp, s_ct, s_ctc = (sem(n) for n in (
            "cmp_scores_ready", "cmp_scores_shifted", "cmp_exp_done", "cmp_probs_ready",
            "cmp_probs_transposed", "cmp_probs_t_copied"))
        s_sc, s_st1, s_exp, s_p, s_tr, s_ptc, s_pv, s_oev = (sem(n) for n in (
            "scores_ready", "scores_biased", "exp_done", "probs_ready", "probs_transposed",
            "probs_t_copied", "values_mixed", "mixed_copied"))
        s_lam, s_lame = sem("lambda_sums_ready"), sem("lambda_exp_done")
        s_sq, s_ss, s_rt, s_da = (sem(n) for n in (
            "squares_ready", "square_sums_ready", "rms_root_ready", "diff_heads_scaled"))
        s_gmm, s_umm, s_gsig, s_mul, s_yacc = (sem(n) for n in (
            "merge_logits_ready", "branch_up_ready", "merge_gate_ready", "gated_product_ready",
            "gated_sum_ready"))
        s_stage, s_y = sem("weights_staged"), sem("wide_product_used_stage")
        s_v = sem("vector_chain")
        s_a = sem("scalar_chain")
        s_lnv, s_lnr, s_x1, s_x1t, s_x1tc = (sem(n) for n in (
            "variance_ready", "deviation_ready", "x1_ready", "x1_transposed", "x1_t_copied"))
        s_ps, s_psc, s_tke, s_tkx, s_nat, s_natt, s_pick = (sem(n) for n in (
            "key_scores_ready", "key_scores_copied", "topk_shifted", "topk_exp_done",
            "picks_ready", "picks_transposed", "picks_t_copied"))
        s_hot, s_g, s_w = sem("one_hots_ready"), sem("gate_matrix_ready"), sem("expert_weights_ready")
        s_lnv2, s_lnr2, s_fin = sem("variance2_ready"), sem("deviation2_ready"), sem("out_ready")

        maps = [("diff", h, mm, 0) for h in range(A_HEADS) for mm in range(2)]
        maps += [("nsa", c, br, half) for c in range(8) for br in range(2) for half in range(2)]
        maps += [("mem", h, 0, 0) for h in range(M_HEADS)]
        NM = len(maps)
        unit_of, units = {}, []
        for k, (kind, _, b, _) in enumerate(maps):
            if kind != "diff" or b == 1:
                unit_of[k] = len(units)
                units.append(k)
        jobs = [k for k, (kind, _, b, half) in enumerate(maps)
                if kind == "mem" or (kind == "diff" and b == 1) or (kind == "nsa" and b == 1 and half == 1)]
        job_of = {k: j for j, k in enumerate(jobs)}

        def job_at(k):
            return next(j for j, last in enumerate(jobs) if last >= k)

        block = ctx.enter_context(nc.Block())

        @block.sync
        def _(sp):
            sp.dma_start(arena[:, O_OT:O_OT + DC * T], mem_t).then_inc(s_mem, 16)
            for s in range(RING):
                sp.dma_start(ring[s], stream[s]).then_inc(s_ring[s], 16)
            with sp.Fori(1, CHUNKS // RING) as i:
                for s in range(RING):
                    sp.wait_ge(s_chunk, i * RING + (s + 1 - RING))
                    sp.dma_start(ring[s], stream[i * RING + s]).then_inc(s_ring[s], 16)
            for t in range(NT):
                sp.wait_ge(s_fin, t + 1)
                sp.dma_start(out[0, t * P:(t + 1) * P, :], x1n[:, t, :]).then_inc(s_out, 16)
            sp.wait_ge(s_out, NT * 16)

        @block.gpsimd
        def _(pool):
            pool.memset(ones, 1.0)
            pool.memset(eps_sb, LN_EPS).then_inc(s_first, 1)
            pool.wait_ge(s_pv, len(units))
            for s in range(RING):
                pool.dma_start(wb[s], w_branch[s]).then_inc(s_wb[s], 16)
            pool.dma_start(xn, x.rearrange("b (t p) n -> p (b t) n", p=P)).then_inc(s_xn, 16)
            pool.dma_start(gb[:, 0, :], ln1_g.to_broadcast([P, D])).then_inc(s_gb, 16)
            pool.dma_start(gb[:, 1, :], ln1_b.to_broadcast([P, D])).then_inc(s_gb, 16)
            with pool.Fori(1, 48 // RING) as i:
                for s in range(RING):
                    pool.wait_ge(s_umm, i * RING + (s + 1 - RING))
                    pool.dma_start(wb[s], w_branch[i * RING + s]).then_inc(s_wb[s], 16)
            pool.wait_ge(s_yacc, 48)
            pool.dma_start(keys, keys_t).then_inc(s_keys, 16)
            pool.wait_ge(s_x1, NT)
            pool.dma_start(x1_dram.ap(), xn.rearrange("p t n -> p (t n)")).then_inc(s_x1s, 16)
            pool.wait_ge(s_chunk, BASE["v_tab"])
            pool.dma_start(gb2[:, 0, :], ln2_g.to_broadcast([P, D])).then_inc(s_gb2, 16)
            pool.dma_start(gb2[:, 1, :], ln2_b.to_broadcast([P, D])).then_inc(s_gb2, 16)
            pool.wait_ge(s_g, T // 4)
            pool.wait_ge(s_x1s, 16)
            pool.dma_start(x1n.rearrange("p t n -> p (t n)"), x1_dram.ap()).then_inc(s_x1l, 16)

        @block.scalar
        def _(act):
            chain = [0]

            def link(ins):
                chain[0] += 1
                ins.then_inc(s_a, 1)
                act.wait_ge(s_a, chain[0])

            act.dma_start(arena[:, O_XT:O_XT + DC * T], x_t).then_inc(s_xt, 16)
            for dst, src in ((ident, identity), (iota, iotas), (flip_sb, flip),
                             (tab_sb, tab), (brev_sb, buckets_rev)):
                act.dma_start(dst, src).then_inc(s_small, 16)
            act.dma_start(wgate_sb, w_gate).then_inc(s_wg, 16)
            for dst, src in ((lam_in, lam.to_broadcast([P, 256])),
                             (subln_sb, subln), (pe_sb, pe_cols), (cmask, cmp_mask)):
                act.dma_start(dst, src).then_inc(s_wg, 16)
            act.wait_ge(s_rows, 1)
            act.activation(rows_sb[:, 0:T], ps[0:HEADS, 7, 0:T], ACT.Copy).then_inc(s_rowc, 1)
            act.wait_ge(s_rowc, 2)
            act.dma_start(bias_rows.ap(), rows_sb).then_inc(s_rowd, 16)
            act.wait_ge(s_rowd, 16)
            act.dma_start(hank_a, bass.AP(bias_rows, 0, [[1, P], [384, 16], [1, T]])).then_inc(s_hank, 16)
            act.dma_start(hank_b, bass.AP(bias_rows, 16 * 384, [[1, P], [384, 8], [1, T]])).then_inc(s_hank, 16)
            act.dma_start(w2_sb, w2).then_inc(s_w2, 16)

            act.sem_inc(s_evac, 2)

            def evac_t(name, first, n, dst, scale):
                g0 = BASE[name] + first
                with act.Fori(0, n // RING) as i:
                    for s in range(RING):
                        act.wait_ge(s_chunk, i * RING + (g0 + s + 1))
                        act.activation(dst[:, bass.ds((i * RING + s) * T + first * T, T)],
                                       ps[:, s % 2, 0:T], ACT.Copy, scale=scale).then_inc(s_evac, 1)

            def evac_n(name, n, dst, width):
                g0 = BASE[name]
                with act.Fori(0, n // RING) as i:
                    for s in range(RING):
                        act.wait_ge(s_chunk, i * RING + (g0 + s + 1))
                        act.activation(dst[:, :, bass.ds((i * RING + s) * P, P)],
                                       ps[:, s % 2, 0:T].rearrange("p (t n) -> p t n", t=NT),
                                       ACT.Copy).then_inc(s_evac, 1)

            evac_t("mem_k", 0, 8, at(O_KM, 8 * T), 1.0)
            evac_n("mem_v", 8, mv, 1024)
            qk_flat = at(O_QK, 40 * T)
            evac_t("qk", 0, 16, qk_flat, A_DQK ** -0.5)
            evac_t("qk", 16, 8, qk_flat, M_DH ** -0.5)
            evac_t("qk", 24, 16, qk_flat, 1.0)
            evac_n("v", 12, nv, NV_W)
            act.wait_ge(s_bg, 1)
            act.activation(gates, ps[:, 7, 0:96].rearrange("p (t n) -> p t n", t=NT),
                           ACT.Sigmoid).then_inc(s_gates, 1)
            for q in range(12):
                act.wait_ge(s_flip, q + 1)
                act.activation(at(O_BIAS + 512 * q, 512), ps[:, 4 + q % 2, :], ACT.Copy).then_inc(s_bias, 1)
            act.wait_ge(s_lam, 1)
            act.activation(lam_tmp[:, 2:4], lam_tmp[:, 0:2], ACT.Exp).then_inc(s_lame, 1)
            act.wait_ge(s_hid, 1)
            link(act.activation(hid_pe, ps[:, 4, 0:4].rearrange("p (k h) -> p k h", k=2), ACT.Copy))
            for kv in range(2):
                for hh in range(2):
                    last = act.activation(hid[:, kv, hh, :], ps[:, kv, hh * 64:hh * 64 + 60],
                                          ACT.Gelu_apprx_tanh, bias=hid_pe[:, kv, hh:hh + 1])
            last.then_inc(s_hidc, 1)
            act.wait_ge(s_w2mm, 1)
            act.wait_ge(s_bd, 1)
            for g in range(B_GROUPS):
                j, e = g // 2, g % 2
                act.activation(kbd[64 * e:64 * e + 64, j, 64 * e:64 * e + N_CMP],
                               ps[0:64, 5, g * N_CMP:(g + 1) * N_CMP], ACT.Copy)
                last = act.activation(vbd[64 * e:64 * e + N_CMP, j, 64 * e:64 * e + 64],
                                      ps[0:N_CMP, 6, g * 64:(g + 1) * 64], ACT.Copy)
            last.then_inc(s_bd, 1)
            act.wait_ge(s_csx, 1)
            act.activation(pc.rearrange("p t c n -> p (t c n)"), pc.rearrange("p t c n -> p (t c n)"),
                           ACT.Exp).then_inc(s_cex, 1)
            for q in range(4):
                act.wait_ge(s_ct, q + 1)
                act.activation(at(O_RAWP + 512 * q, 512), ps[:, q, :], ACT.Copy).then_inc(s_ctc, 1)

            def exp(k):
                kind = maps[k][0]
                e = ee[k % 3]
                act.wait_ge(s_st1, k + 1)
                if kind == "mem":
                    if k >= 3:
                        act.wait_ge(s_tr, unit_of[k - 3] + 1)
                    parts = [(e[:, t * T:(t + 1) * T], ps[:, k % 3, t * T:(t + 1) * T]) for t in range(NT)]
                else:
                    parts = [(e[:, 0:P],) * 2, (e[:, P:3 * P],) * 2]
                for t, (dst, src) in enumerate(parts):
                    last = act.activation(dst, src, ACT.Exp, bias=nmx[k % 3][:, t:t + 1],
                                          accum_out=sums[k % 3][:, t:t + 1])
                last.then_inc(s_exp, 1)

            def pt_copy(k):
                u = unit_of[k]
                wid = 512 if maps[k][0] == "mem" else 384
                act.wait_ge(s_tr, u + 1)
                if u >= 2:
                    act.wait_ge(s_pv, u - 1)
                act.activation(pt[u % 2][:, 0:wid], ps[:, 3 + u % 2, 0:wid], ACT.Copy).then_inc(s_ptc, 1)

            def o_copy(k):
                kind, c = maps[k][0], maps[k][1]
                j = job_of[k]
                act.wait_ge(s_pv, unit_of[k] + 1)
                b = 5 + j % 2
                if kind == "mem":
                    act.activation(at(O_OT + (16 + 2 * c) * T, 512), ps[:, b, :], ACT.Copy).then_inc(s_oev, 1)
                else:
                    first = 0 if kind == "diff" else 8
                    act.activation(ot[:, first + c, :], ps[:, b, 0:T], ACT.Copy).then_inc(s_oev, 1)

            for k in range(-1, NM + 1):
                if k + 1 < NM:
                    exp(k + 1)
                if k in unit_of:
                    pt_copy(k)
                if k - 1 in job_of:
                    o_copy(k - 1)
            act.wait_ge(s_ss, 1)
            for q in range(4):
                last = act.activation(rms[:, 512 * q:512 * q + 512], ps[:, q, :], ACT.Sqrt,
                                      bias=eps_sb, scale=1.0 / A_DV)
            last.then_inc(s_rt, 1)
            with act.Fori(0, 48 // RING) as i:
                for s in range(RING):
                    act.wait_ge(s_gmm, i * RING + s + 1)
                    act.wait_ge(s_mul, i * RING + s + 1)
                    act.activation(gate_t[s % 2], ps[:, s % 2, 0:T], ACT.Sigmoid).then_inc(s_gsig, 1)

            def stage_in(src, n, done, ready):
                with act.Fori(0, n // RING) as i:
                    for s in range(RING):
                        act.wait_ge(s_y, i * RING + (done + s + 1))
                        act.activation(stage[s % 2], src[:, bass.ds((i * RING + s) * T, T)],
                                       ACT.Copy).then_inc(s_stage, 1)

            act.wait_ge(s_yacc, 48)
            stage_in(yt_flat, 16, 0, None)
            act.wait_ge(s_lnv, 1)
            act.activation(rstd, mean_var[:, :, 1], ACT.Sqrt, bias=eps_sb).then_inc(s_lnr, 1)
            for q in range(8):
                act.wait_ge(s_x1t, q + 1)
                act.activation(at(O_XT + 512 * q, 512), ps[:, q % 4, :], ACT.Copy).then_inc(s_x1tc, 1)
            g0 = BASE["wq"]
            with act.Fori(0, 16 // RING) as i:
                for s in range(RING):
                    act.wait_ge(s_chunk, i * RING + (g0 + s + 1))
                    act.activation(at(O_H + 28672, DC * T)[:, bass.ds((i * RING + s) * T, T)],
                                   ps[:, 4 + s % 2, 0:T], ACT.Copy).then_inc(s_evac, 1)
            for q in range(8):
                act.wait_ge(s_ps, q + 1)
                act.activation(at(O_S + 512 * q, 512), ps[:, q % 4, :], ACT.Copy).then_inc(s_psc, 1)
            def experts(first, n):
                g1 = BASE["u"] + first
                with act.Fori(0, n // RING) as i:
                    for s in range(RING):
                        act.wait_ge(s_chunk, i * RING + (g1 + s + 1))
                        act.activation(at(O_H, NKEYS * T)[:, bass.ds((i * RING + (s + first)) * T, T)],
                                       ps[:, 4 + s % 2, 0:T], ACT.Gelu_apprx_tanh).then_inc(s_evac, 1)

            act.wait_ge(s_x1s, 16)
            experts(0, NKEYS // 2)
            act.wait_ge(s_tke, 1)
            act.activation(nat[:, :, 2, :], nat[:, :, 2, :], ACT.Exp).then_inc(s_tkx, 1)
            for q in range(3):
                act.wait_ge(s_natt, q + 1)
                act.activation(pick_t[:, q, :], ps[:, q, 0:T], ACT.Copy).then_inc(s_pick, 1)
            experts(NKEYS // 2, NKEYS // 2)
            act.wait_ge(s_w, 2 + T // 4)
            stage_in(at(O_H, NKEYS * T), NKEYS, 16, None)
            act.wait_ge(s_lnv2, 1)
            act.activation(rstd, mean_var[:, :, 1], ACT.Sqrt, bias=eps_sb).then_inc(s_lnr2, 1)

        @block.tensor
        def _(pe):
            def ring_t():
                return [r.rearrange("p (c n) -> p c n", c=DC) for r in ring]

            def columns_stationary(name, n, moving, bank0):
                g0 = BASE[name]
                e0 = evac_index[name]
                with pe.Fori(0, n // RING) as i:
                    for s in range(RING):
                        r = ring_t()[s]
                        pe.wait_ge(s_ring[s], i * 16 + (g0 // RING + 1) * 16)
                        pe.wait_ge(s_evac, i * RING + (e0 + s + 1))
                        for c in range(DC):
                            last = pe.matmul(ps[:, bank0 + s % 2, 0:T], r[:, c, :], moving[:, c, :],
                                             start=c == 0, stop=c == DC - 1)
                        last.then_inc(s_chunk, 1)

            def tokens_stationary(name, n, stationary):
                g0 = BASE[name]
                e0 = evac_index[name]
                with pe.Fori(0, n // RING) as i:
                    for s in range(RING):
                        r = ring_t()[s]
                        pe.wait_ge(s_ring[s], i * 16 + (g0 // RING + 1) * 16)
                        pe.wait_ge(s_evac, i * RING + (e0 + s + 1))
                        for t in range(NT):
                            for c in range(DC):
                                last = pe.matmul(ps[:, s % 2, t * P:(t + 1) * P],
                                                 stationary[:, c, t * P:(t + 1) * P], r[:, c, :],
                                                 start=c == 0, stop=c == DC - 1)
                        last.then_inc(s_chunk, 1)

            evac_index = {"mem_k": 0, "mem_v": 8, "qk": 16, "v": 56, "wq": 68, "u": 84}

            pe.wait_ge(s_small, 5 * 16)
            pe.wait_ge(s_first, 1)
            pe.matmul(ps[0:HEADS, 7, 0:T], tab_sb, brev_sb, start=True, stop=True).then_inc(s_rows, 1)
            pe.wait_ge(s_mem, 16)
            columns_stationary("mem_k", 8, memt, 0)
            tokens_stationary("mem_v", 8, memt)
            pe.wait_ge(s_xt, 16)
            pe.wait_ge(s_wg, 5 * 16)
            pe.wait_ge(s_rowc, 2)
            for t in range(NT):
                for c in range(DC):
                    last = pe.matmul(ps[:, 7, t * 48:(t + 1) * 48], xt[:, c, t * P:(t + 1) * P],
                                     wgate_sb[:, c, :], start=c == 0, stop=c == DC - 1)
            last.then_inc(s_bg, 1)
            columns_stationary("qk", 40, xt, 0)
            tokens_stationary("v", 12, xt)
            pe.wait_ge(s_hank, 32)
            for q in range(12):
                if q >= 2:
                    pe.wait_ge(s_bias, q - 1)
                src = hank_a[:, q * 512:(q + 1) * 512] if q < 8 else hank_b[:, (q - 8) * 512:(q - 7) * 512]
                pe.matmul(ps[:, 4 + q % 2, :], flip_sb, src, start=True, stop=True).then_inc(s_flip, 1)
            for s in range(RING):
                pe.wait_ge(s_ring[s], (BASE["cmp_w1"] // RING + 1) * 16)
            pe.wait_ge(s_raw, 1)
            pe.wait_ge(s_evac, 2 + 68)
            pe.wait_ge(s_bias, 12)
            for kv in range(2):
                for hh in range(2):
                    for l2 in range(16):
                        w1 = ring[2 * kv + l2 // 8].rearrange("p (l n) -> p l n", l=8)[:, l2 % 8, hh * P:(hh + 1) * P]
                        mov = rawp[:, kv, :, 2 * l2:2 * l2 + 16 * (N_CMP - 1) + 1:16]
                        pe.matmul(ps[:, kv, hh * 64:hh * 64 + 60].rearrange("p (g c) -> p g c", g=4),
                                  w1, mov, start=l2 == 0, stop=l2 == 15)
            for kv in range(2):
                for hh in range(2):
                    for l2 in range(16):
                        w1 = ring[2 * kv + l2 // 8].rearrange("p (l n) -> p l n", l=8)[:, l2 % 8, hh * P:(hh + 1) * P]
                        last = pe.matmul(ps[:, 4, 2 * kv + hh:2 * kv + hh + 1], w1,
                                         pe_sb[:, kv, l2:l2 + 1], start=l2 == 0, stop=l2 == 15)
            last.then_inc(s_hid, 1)
            pe.wait_ge(s_hid, 1)
            pe.sem_inc(s_chunk, 4)
            pe.wait_ge(s_hidc, 1)
            pe.wait_ge(s_w2, 16)
            for hh in range(2):
                pe.matmul(ps[0:64, 5, 0:60], w2_sb[:, 0, hh, :], hid[:, 0, hh, :], start=hh == 0, stop=hh == 1)
            for g in range(B_GROUPS):
                for hh in range(2):
                    last = pe.matmul(ps[0:N_CMP, 6, g * 64:(g + 1) * 64],
                                     hid[:, 1, hh, g * N_CMP:(g + 1) * N_CMP], w2_sb[:, 1, hh, :],
                                     start=hh == 0, stop=hh == 1)
            last.then_inc(s_w2mm, 1)
            pe.wait_ge(s_bd, 2)
            for t in range(NT):
                for c in range(8):
                    b = 2 * t + c // 4
                    last = pe.matmul(ps[:, b, (c % 4) * P:(c % 4 + 1) * P],
                                     qk[:, Q_B + c, t * P:(t + 1) * P], kbd[:, c // 4, :], start=True, stop=True)
            last.then_inc(s_cs, 1)
            pe.wait_ge(s_cp, 1)
            for c in range(8):
                for t in range(NT):
                    last = pe.transpose(ps[:, c // 2, (c % 2) * T + t * P:(c % 2) * T + (t + 1) * P],
                                        pc[:, t, c, :], ident)
                if c % 2:
                    last.then_inc(s_ct, 1)

            def scores(k):
                kind, c, br, half = maps[k]
                if k >= 3:
                    pe.wait_ge(s_exp, k - 2)
                else:
                    pe.wait_ge(s_ctc, 4)
                b = k % 3
                if kind == "mem":
                    for t in range(NT):
                        for d in range(2):
                            last = pe.matmul(ps[:, b, t * T:(t + 1) * T], qk[:, Q_M + 2 * c + d, t * P:(t + 1) * P],
                                             km[:, 2 * c + d, :], start=d == 0, stop=d == 1)
                else:
                    if kind == "diff":
                        q, kk, h0 = qk[:, Q_A + c, :], qk[:, K_A + c, :], 64 * br
                    else:
                        q, kk, h0 = qk[:, Q_B + c, :], qk[:, (K_SEL, K_WIN)[br] + c // 4, :], 64 * half
                    pe.matmul(ps[:, b, 0:P], q[h0:h0 + 64, 0:P], kk[h0:h0 + 64, 0:P], start=True, stop=True)
                    last = pe.matmul(ps[:, b, P:3 * P], q[h0:h0 + 64, P:T], kk[h0:h0 + 64, 0:T],
                                     start=True, stop=True)
                last.then_inc(s_sc, 1)

            def transposes(k):
                u = unit_of[k]
                pe.wait_ge(s_p, u + 1)
                if u >= 2:
                    pe.wait_ge(s_ptc, u - 1)
                e, b = ee[k % 3], 3 + u % 2
                if maps[k][0] == "mem":
                    pairs = [(t * T + kb * P, kb * T + t * P) for t in range(NT) for kb in range(2)]
                else:
                    pairs = [(i * P, i * P) for i in range(3)]
                for a, z in pairs:
                    last = pe.transpose(ps[:, b, z:z + P], e[:, a:a + P], ident)
                last.then_inc(s_tr, 1)

            def mix(k):
                kind, c, br, half = maps[k]
                u, j = unit_of[k], job_at(k)
                b = 5 + j % 2
                pe.wait_ge(s_ptc, u + 1)
                if j >= 2:
                    pe.wait_ge(s_oev, j - 1)
                p_t = pt[u % 2]
                if kind == "mem":
                    for dd in range(2):
                        for kb in range(2):
                            last = pe.matmul(ps[:, b, dd * T:(dd + 1) * T],
                                             mv[:, kb, c * 256 + dd * P:c * 256 + (dd + 1) * P],
                                             p_t[:, kb * T:(kb + 1) * T], start=kb == 0, stop=kb == 1)
                elif kind == "diff":
                    v = nv[:, :, V_A + c * P:V_A + (c + 1) * P]
                    pe.matmul(ps[:, b, 0:T], v[:, 0, :], p_t[:, 0:T], start=True, stop=False)
                    last = pe.matmul(ps[:, b, P:T], v[:, 1, :], p_t[:, T:T + P], start=False, stop=True)
                else:
                    if br == 0 and half == 0:
                        pe.matmul(ps[:, b, 0:T], vbd[:, c // 4, :], pct[:, c, :], start=True, stop=False,
                                  skip_group_check=True)
                    g = 2 * (c // 4) + half
                    v = nv[:, :, (V_SEL, V_WIN)[br] + g * 64:(V_SEL, V_WIN)[br] + (g + 1) * 64]
                    h0 = 64 * half
                    pe.matmul(ps[h0:h0 + 64, b, 0:T], v[:, 0, :], p_t[:, 0:T], start=False, stop=False,
                              skip_group_check=True)
                    last = pe.matmul(ps[h0:h0 + 64, b, P:T], v[:, 1, :], p_t[:, T:T + P], start=False,
                                     stop=br == 1, skip_group_check=True)
                last.then_inc(s_pv, 1)

            scores(0)
            scores(1)
            for k in range(NM + 1):
                if k + 2 < NM:
                    scores(k + 2)
                if k in unit_of:
                    transposes(k)
                if k - 1 in unit_of:
                    mix(k - 1)
            for h in range(A_HEADS):
                if h == 0:
                    pe.wait_ge(s_sq, 1)
                last = pe.matmul(ps[:, h // 2, (h % 2) * T:(h % 2 + 1) * T], ones,
                                 at(O_BIAS + h * T, T), start=True, stop=True)
            last.then_inc(s_ss, 1)
            pe.wait_ge(s_da, 1)
            pe.wait_ge(s_oev, len(jobs))
            g0 = BASE["merge"] // RING
            ot_flat = at(O_OT, 24 * T)
            for n in range(3):
                with pe.Fori(0, 4) as i:
                    for s in range(RING):
                        r = ring_t()[s]
                        pe.wait_ge(s_ring[s], i * 16 + (g0 + 4 * n + 1) * 16)
                        pe.wait_ge(s_gsig, i * RING + (16 * n + s + 1))
                        for c in range(DC):
                            last = pe.matmul(ps[:, s % 2, 0:T], r[:, c, :], xt[:, c, :],
                                             start=c == 0, stop=c == DC - 1)
                        last.then_inc(s_gmm, 1)
                        pe.wait_ge(s_wb[s], i * 16 + (4 * n + 1) * 16)
                        pe.wait_ge(s_mul, i * RING + (16 * n + s + 1))
                        for c in range(MIX_C):
                            last = pe.matmul(ps[:, 2 + s % 2, 0:T], wb[s][:, c, :], ot[:, 8 * n + c, :],
                                             start=c == 0, stop=c == MIX_C - 1)
                        last.then_inc(s_umm, 1)
                        pe.wait_ge(s_umm, i * RING + (16 * n + s + 1))
                        pe.sem_inc(s_chunk, 1)

            def wide(name, n, y0):
                g0 = BASE[name] // RING
                def body(i, s, first, last_one):
                    pe.wait_ge(s_ring[s], i * 16 + (g0 + 1) * 16)
                    pe.wait_ge(s_stage, i * RING + (y0 + s + 1))
                    for t in range(NT):
                        for q in range(4):
                            last = pe.matmul(ps[:, 4 * t + q, :], stage[s % 2][:, t * P:(t + 1) * P],
                                             ring[s][:, q * 512:(q + 1) * 512], start=first, stop=last_one,
                                             skip_group_check=True)
                    last.then_inc(s_chunk, 1)
                    pe.wait_ge(s_chunk, i * RING + (BASE[name] + s + 1))
                    pe.sem_inc(s_y, 1)
                for s in range(RING):
                    body(0, s, s == 0, False)
                with pe.Fori(1, n // RING - 1) as i:
                    for s in range(RING):
                        body(i, s, False, False)
                for s in range(RING):
                    body(n // RING - 1, s, False, s == RING - 1)

            pe.wait_ge(s_mul, 2 + 48)
            pe.wait_ge(s_gsig, 2 + 48)
            wide("w_out", 16, 0)
            pe.wait_ge(s_x1, NT)
            for c in range(DC):
                if c >= 8 and c % 2 == 0:
                    pe.wait_ge(s_x1tc, c // 2 - 3)
                for t in range(NT):
                    last = pe.transpose(ps[:, (c // 2) % 4, (c % 2) * T + t * P:(c % 2) * T + (t + 1) * P],
                                        xn[:, t, c * P:(c + 1) * P], ident)
                if c % 2:
                    last.then_inc(s_x1t, 1)
            pe.wait_ge(s_x1tc, 8)
            columns_stationary("wq", 16, xt, 4)
            pe.wait_ge(s_evac, 2 + 84)
            pe.wait_ge(s_keys, 16)
            for t in range(NT):
                for c in range(DC):
                    q = t * 4 + c // 4
                    if q >= 4 and c % 4 == 0:
                        pe.wait_ge(s_psc, q - 3)
                    last = pe.matmul(ps[:, q % 4, (c % 4) * P:(c % 4 + 1) * P], pq[:, c, t * P:(t + 1) * P],
                                     keys[:, c, :], start=True, stop=True)
                    if c % 4 == 3:
                        last.then_inc(s_ps, 1)
            def experts(first, n):
                g1, e0 = BASE["u"] + first, evac_index["u"] + first
                with pe.Fori(0, n // RING) as i:
                    for s in range(RING):
                        r = ring_t()[s]
                        pe.wait_ge(s_ring[s], i * 16 + (g1 // RING + 1) * 16)
                        pe.wait_ge(s_evac, i * RING + (e0 + s + 1))
                        for c in range(DC):
                            last = pe.matmul(ps[:, 4 + s % 2, 0:T], r[:, c, :], xt[:, c, :],
                                             start=c == 0, stop=c == DC - 1)
                        last.then_inc(s_chunk, 1)

            experts(0, NKEYS // 2)
            pe.wait_ge(s_psc, 8)
            pe.wait_ge(s_nat, 1)
            for k in range(3):
                for t in range(NT):
                    last = pe.transpose(ps[:, k, t * P:(t + 1) * P], nat[:, t, k, :], ident)
                last.then_inc(s_natt, 1)
            experts(NKEYS // 2, NKEYS // 2)
            pe.wait_ge(s_pick, 3)
            with pe.Fori(0, T // 8) as i:
                for b in range(2):
                    pe.wait_ge(s_hot, i * 2 + b + 1)
                    pe.wait_ge(s_w, i * 2 + b + 1)
                    for a in range(4):
                        last = pe.matmul(ps[:, b, a * P:(a + 1) * P], hot[:, b, 0, a, :], hot[:, b, 1, a, :],
                                         start=True, stop=True)
                    last.then_inc(s_g, 1)
            pe.wait_ge(s_evac, 2 + 84 + NKEYS)
            pe.wait_ge(s_w, 2 + T // 4)
            wide("v_tab", NKEYS, 16)

        @block.vector
        def _(dve):
            chain = [0]

            def link(ins):
                chain[0] += 1
                ins.then_inc(s_v, 1)
                dve.wait_ge(s_v, chain[0])

            dve.sem_inc(s_mul, 2)
            dve.sem_inc(s_gsig, 2)
            dve.sem_inc(s_y, 2)
            dve.sem_inc(s_w, 2)
            dve.memset(rows_sb[:, T:384], NEG).then_inc(s_rowc, 1)
            dve.wait_ge(s_wg, 5 * 16)
            for n in range(2):
                last = dve.tensor_tensor_reduce(ee[2][:, n * 64:(n + 1) * 64], lam_in[:, n * 128:n * 128 + 64],
                                                lam_in[:, n * 128 + 64:n * 128 + 128], 1.0, 0.0,
                                                ALU.mult, ALU.add, lam_tmp[:, n:n + 1])
            last.then_inc(s_lam, 1)
            dve.wait_ge(s_flip, 12)
            dve.wait_ge(s_evac, 2 + 56)
            for kv in range(2):
                for g in range(B_GROUPS):
                    c, h0 = (RAW_K, RAW_V)[kv] + g // 2, 64 * (g % 2)
                    dve.tensor_copy(rawp[0:64, kv, g, :], qk[h0:h0 + 64, c, :])
                    last = dve.tensor_copy(rawp[64:128, kv, g, 0:T - 1], qk[h0:h0 + 64, c, 1:T])
            last.then_inc(s_raw, 1)
            dve.wait_ge(s_raw, 1)
            dve.memset(at(O_QK + RAW_K * T, 512), 0.0).then_inc(s_bd, 1)
            dve.wait_ge(s_lame, 1)
            link(dve.tensor_tensor(lam_sb, lam_tmp[:, 2:3], lam_tmp[:, 3:4], ALU.subtract))
            link(dve.tensor_scalar(lam_sb, lam_sb, BETA_LAM, None, ALU.add))
            dve.wait_ge(s_cs, 1)
            for t in range(NT):
                dst = pc[:, t, :, :].rearrange("p c n -> p (c n)")
                for q in range(2):
                    link(dve.tensor_copy(dst[:, q * 512:(q + 1) * 512], ps[:, 2 * t + q, :]))
            for t in range(NT):
                v = pc[:, t, :, :].rearrange("p c (e n) -> p (c e) n", e=2)
                real = v[:, :, 0:N_CMP]
                add_m = cmask[:, 0, t, :].unsqueeze(1).to_broadcast([P, 16, N_CMP])
                link(dve.tensor_scalar(real, real, B_DH ** 0.0, None, ALU.mult))
                link(dve.tensor_tensor(real, real, add_m, ALU.add))
                link(dve.tensor_reduce(cst[:, t, :], real, AX.X, ALU.max))
                ins = dve.tensor_tensor(real, real, cst[:, t, :].unsqueeze(2).to_broadcast([P, 16, N_CMP]),
                                        ALU.subtract)
                if t == NT - 1:
                    ins.then_inc(s_csx, 1)
                else:
                    link(ins)
            dve.wait_ge(s_cex, 1)
            dve.wait_ge(s_gates, 1)
            for t in range(NT):
                v = pc[:, t, :, :].rearrange("p c (e n) -> p (c e) n", e=2)
                real = v[:, :, 0:N_CMP]
                link(dve.memset(v[:, :, N_CMP:64], 0.0))
                link(dve.tensor_tensor(real, real, cmask[:, 1, t, :].unsqueeze(1).to_broadcast([P, 16, N_CMP]),
                                       ALU.mult))
                link(dve.tensor_reduce(cst[:, 2 + t, :], real, AX.X, ALU.add))
                link(dve.tensor_scalar(cst[:, 2 + t, :], cst[:, 2 + t, :], 1e-30, None, ALU.max))
                link(dve.reciprocal(cst[:, 2 + t, :], cst[:, 2 + t, :]))
                for j in range(2):
                    g4 = gates[:, t, 8 * j:8 * j + 8].rearrange("p (e i) -> p i e", e=2)
                    r4 = cst[:, 2 + t, 8 * j:8 * j + 8].rearrange("p (i e) -> p i e", e=2)
                    link(dve.tensor_tensor(r4, r4, g4, ALU.mult))
                ins = dve.tensor_tensor(real, real, cst[:, 2 + t, :].unsqueeze(2).to_broadcast([P, 16, N_CMP]),
                                        ALU.mult)
                if t == NT - 1:
                    ins.then_inc(s_cp, 1)
                else:
                    link(ins)

            def head_of(k):
                kind, c, br, half = maps[k]
                return c if kind == "diff" else 8 * (c // 4) + 4 * half + c % 4

            def stage1(k):
                kind, c, br, half = maps[k]
                e, b = ee[k % 3], k % 3
                dve.wait_ge(s_sc, k + 1)
                if kind == "mem":
                    dve.tensor_reduce(nmx[b], ps[:, b, :].rearrange("p (t n) -> p t n", t=NT), AX.X, ALU.max,
                                      negate=True).then_inc(s_st1, 1)
                    return
                if k >= 3 and k - 3 in unit_of:
                    dve.wait_ge(s_tr, unit_of[k - 3] + 1)
                elif k >= 3:
                    dve.wait_ge(s_p, unit_of[k - 2] + 1)
                hb = head_of(k) + (0 if kind == "diff" else A_HEADS)
                if k == 0:
                    dve.wait_ge(s_bias, 12)
                dve.tensor_tensor_reduce(e[:, 0:P], ps[:, b, 0:P], bias[:, hb, P:T], 1.0, NEG, ALU.add,
                                         ALU.max, mxs[b][:, 0:1])
                link(dve.tensor_tensor_reduce(e[:, P:3 * P], ps[:, b, P:3 * P], bias[:, hb, :], 1.0, NEG,
                                              ALU.add, ALU.max, mxs[b][:, 1:2]))
                dve.tensor_scalar(nmx[b], mxs[b], -1.0, None, ALU.mult).then_inc(s_st1, 1)

            def stage2(k):
                kind, c, br, half = maps[k]
                e, b = ee[k % 3], k % 3
                dve.wait_ge(s_exp, k + 1)
                link(dve.reciprocal(rec[b], sums[b]))
                if kind == "nsa":
                    col = (br + 1) * B_HEADS + head_of(k)
                    link(dve.tensor_tensor(rec[b], rec[b], gates[:, :, col], ALU.mult))
                cut = [(0, T), (T, 2 * T)] if kind == "mem" else [(0, P), (P, 3 * P)]
                if kind != "diff":
                    for t, (a, z) in enumerate(cut):
                        last = dve.tensor_scalar(e[:, a:z], e[:, a:z], rec[b][:, t:t + 1], None, ALU.mult)
                    last.then_inc(s_p, 1)
                elif br == 0:
                    for t, (a, z) in enumerate(cut):
                        ins = dve.tensor_scalar(e[:, a:z], e[:, a:z], rec[b][:, t:t + 1], None, ALU.mult)
                    link(ins)
                else:
                    link(dve.tensor_scalar(rec[b], rec[b], lam_sb, -1.0, ALU.mult, ALU.mult))
                    e0 = ee[(k - 1) % 3]
                    for t, (a, z) in enumerate(cut):
                        last = dve.scalar_tensor_tensor(e[:, a:z], e[:, a:z], rec[b][:, t:t + 1], e0[:, a:z],
                                                        ALU.mult, ALU.add)
                    last.then_inc(s_p, 1)

            dve.wait_ge(s_ctc, 4)
            stage1(0)
            for k in range(NM):
                if k + 1 < NM:
                    stage1(k + 1)
                stage2(k)
            dve.wait_ge(s_oev, len(jobs))
            o_a = at(O_OT, A_HEADS * T)
            dve.tensor_tensor(at(O_BIAS, A_HEADS * T), o_a, o_a, ALU.mult).then_inc(s_sq, 1)
            dve.wait_ge(s_rt, 1)
            link(dve.reciprocal(rms, rms))
            link(dve.tensor_tensor(o_a, o_a, rms, ALU.mult))
            dve.tensor_scalar(o_a, o_a, subln_sb, 1.0 - BETA_LAM, ALU.mult, ALU.mult).then_inc(s_da, 1)
            dve.wait_ge(s_da, 1)
            link(dve.memset(yt_flat, 0.0))
            for n in range(3):
                with dve.Fori(0, 4) as i:
                    for s in range(RING):
                        dve.wait_ge(s_umm, i * RING + (16 * n + s + 1))
                        dve.wait_ge(s_gsig, i * RING + (16 * n + s + 3))
                        dve.tensor_tensor(prod_t[s % 2], ps[:, 2 + s % 2, 0:T], gate_t[s % 2],
                                          ALU.mult).then_inc(s_mul, 1)
                        dve.wait_ge(s_mul, i * RING + (16 * n + s + 3))
                        if n:
                            dve.wait_ge(s_yacc, i * RING + (16 * (n - 1) + s + 1))
                        dst = yt_flat[:, bass.ds((i * RING + s) * T, T)]
                        dve.tensor_tensor(dst, dst, prod_t[s % 2], ALU.add).then_inc(s_yacc, 1)

            def norm(base, res, params, s_params, s_var, s_root, s_done, s_res):
                dve.wait_ge(s_chunk, base)
                dve.wait_ge(s_res, 16)
                for t in range(NT):
                    for q in range(4):
                        part = res[:, t, q * 512:(q + 1) * 512]
                        ins = dve.scalar_tensor_tensor(part, part, ALPHA, ps[:, 4 * t + q, :], ALU.mult, ALU.add)
                link(ins)
                for t in range(NT):
                    for q in range(4):
                        ins = dve.bn_stats(bn[:, t, q, :], res[:, t, q * 512:(q + 1) * 512])
                link(ins)
                for t in range(NT):
                    ins = dve.bn_aggr(mean_var[:, t, :], bn[:, t, :, :].rearrange("p c s -> p (c s)"))
                ins.then_inc(s_var, 1)
                dve.wait_ge(s_root, 1)
                link(dve.reciprocal(rstd, rstd))
                dve.wait_ge(s_params, 32)
                for t in range(NT):
                    row = res[:, t, :]
                    link(dve.tensor_scalar(row, row, mean_var[:, t, 0:1], rstd[:, t:t + 1],
                                           ALU.subtract, ALU.mult))
                    link(dve.tensor_tensor(row, row, params[:, 0, :], ALU.mult))
                    dve.tensor_tensor(row, row, params[:, 1, :], ALU.add).then_inc(s_done, 1)

            norm(BASE["wq"], xn, gb, s_gb, s_lnv, s_lnr, s_x1, s_xn)

            BIG = -3e38
            ones16 = iota[:, 0:TOPK]
            for t in range(NT):
                dve.wait_ge(s_psc, 4 * (t + 1))
                idx = idx_u.rearrange("p (h c k) -> p h c k", h=PEER_HEADS, c=2)
                for h in range(PEER_HEADS):
                    for c in range(2):
                        src = sc[:, t, (2 * h + c) * P:(2 * h + c + 1) * P]
                        link(dve.max(vals[:, h, c, 0:8], src))
                        dve.max_index(idx[:, h, c, 0:8], vals[:, h, c, 0:8], src)
                        link(dve.match_replace(seg, vals[:, h, c, 0:8], src, BIG))
                        link(dve.max(vals[:, h, c, 8:16], seg))
                        link(dve.max_index(idx[:, h, c, 8:16], vals[:, h, c, 8:16], seg))
                posv = pos_u
                for h in range(PEER_HEADS):
                    cv = comb.rearrange("p (a b) -> p a b", a=TOPK)
                    link(dve.tensor_tensor(cv, vals[:, h, 0, :].unsqueeze(2).to_broadcast([P, TOPK, TOPK]),
                                           vals[:, h, 1, :].unsqueeze(1).to_broadcast([P, TOPK, TOPK]), ALU.add))
                    f, z = fin[:, h * TOPK:(h + 1) * TOPK], posv[:, h * TOPK:(h + 1) * TOPK]
                    link(dve.max(f[:, 0:8], comb))
                    dve.max_index(z[:, 0:8], f[:, 0:8], comb)
                    link(dve.match_replace(comb2, f[:, 0:8], comb, BIG))
                    link(dve.max(f[:, 8:16], comb2))
                    link(dve.max_index(z[:, 8:16], f[:, 8:16], comb2))
                link(dve.tensor_copy(idx_f.rearrange("p h c k -> p (h c k)"), idx_u))
                work = sc[:, t, :]
                for c in range(2):
                    if c == 0:
                        link(dve.tensor_scalar(pab_u, pos_u, 4, None, ALU.logical_shift_right))
                    else:
                        link(dve.tensor_scalar(pab_u, pos_u, 15, None, ALU.bitwise_and))
                    link(dve.tensor_copy(pab_f, pab_u))
                    wv = work.rearrange("p (n a) -> p n a", a=TOPK)
                    link(dve.tensor_tensor(wv, pab_f.unsqueeze(2).to_broadcast([P, PICKS, TOPK]),
                                           ones16.unsqueeze(1).to_broadcast([P, PICKS, TOPK]), ALU.is_equal))
                    w4 = work.rearrange("p (h k a) -> p h k a", h=PEER_HEADS, k=TOPK)
                    link(dve.tensor_tensor(w4, w4, idx_f[:, :, c, :].unsqueeze(2)
                                           .to_broadcast([P, PEER_HEADS, TOPK, TOPK]), ALU.mult))
                    link(dve.tensor_reduce(nat[:, t, c, :], wv, AX.X, ALU.add))
                f3 = fin.rearrange("p (h k) -> p h k", h=PEER_HEADS)
                ins = dve.tensor_tensor(nat[:, t, 2, :].rearrange("p (h k) -> p h k", h=PEER_HEADS), f3,
                                        f3[:, :, 0:1].to_broadcast([P, PEER_HEADS, TOPK]), ALU.subtract)
                if t == NT - 1:
                    ins.then_inc(s_tke, 1)
                else:
                    link(ins)
            dve.wait_ge(s_tkx, 1)
            for t in range(NT):
                g3 = nat[:, t, 2, :].rearrange("p (h k) -> p h k", h=PEER_HEADS)
                link(dve.tensor_reduce(den[:, t * 8:t * 8 + 8], g3, AX.X, ALU.add))
                link(dve.reciprocal(den[:, t * 8:t * 8 + 8], den[:, t * 8:t * 8 + 8]))
                ins = dve.tensor_tensor(g3, g3, den[:, t * 8:t * 8 + 8].unsqueeze(2)
                                        .to_broadcast([P, PEER_HEADS, TOPK]), ALU.mult)
            ins.then_inc(s_nat, 1)

            dve.wait_ge(s_pick, 3)
            dve.wait_ge(s_evac, 2 + 84 + NKEYS)
            pick_flat = at(w + 1024, 3 * T)

            def one_hots(i, b, first):
                if not first:
                    dve.wait_ge(s_g, i * 2 + (b - 1))
                for a in range(4):
                    tok = i * 8 + 4 * b + a
                    dve.tensor_scalar(hot[:, b, 0, a, :], iota, pick_flat[:, bass.ds(tok, 1)],
                                      pick_flat[:, bass.ds(tok + 2 * T, 1)], ALU.is_equal, ALU.mult)
                    last = dve.tensor_scalar(hot[:, b, 1, a, :], iota, pick_flat[:, bass.ds(tok + T, 1)], None,
                                             ALU.is_equal)
                last.then_inc(s_hot, 1)

            def weigh(i, b):
                dve.wait_ge(s_g, i * 2 + (b + 1))
                part = hx[:, :, bass.ds(i * 8 + 4 * b, 4)].rearrange("p j a -> p a j")
                dve.tensor_tensor(part, ps[:, b, :].rearrange("p (a j) -> p a j", a=4), part,
                                  ALU.mult).then_inc(s_w, 1)

            one_hots(0, 0, True)
            one_hots(0, 1, True)
            with dve.Fori(1, T // 8) as i:
                for b in range(2):
                    weigh(i - 1, b)
                    one_hots(i, b, False)
            weigh(T // 8 - 1, 0)
            weigh(T // 8 - 1, 1)

            norm(CHUNKS, x1n, gb2, s_gb2, s_lnv2, s_lnr2, s_fin, s_x1l)


def _column_chunks(w):
    n = w.shape[1] // P
    return np.ascontiguousarray(w.reshape(DC, P, n, P).transpose(2, 1, 0, 3)).reshape(n, P, CW)


def kernel(**inputs):
    import concourse.bacc as bacc
    from concourse.bass_utils import run_bass_kernel_spmd

    a = {k: np.asarray(v) for k, v in inputs.items()}
    w_in = a["w_in"][0]
    widths = [1024, 1024, 1024, 1024, 1536, 48, 1024, 3 * D]
    edge = np.concatenate([[0], np.cumsum(widths)])
    aq, ak, av, bq, bkv, bg, mq, merge = (slice(edge[i], edge[i + 1]) for i in range(8))
    order = [8 * j + 4 * e + i for j in range(2) for i in range(B_HPG) for e in range(2)]
    perm = np.concatenate([np.arange(B_DH) + B_DH * h for h in order])
    kv = w_in[:, bkv].reshape(D, 3, 2, 256)
    qk_w = np.concatenate([w_in[:, aq], w_in[:, bq][:, perm], w_in[:, mq], w_in[:, ak],
                           kv[:, 1, 0], kv[:, 2, 0], kv[:, 0, 0], kv[:, 0, 1]], axis=1)
    v_w = np.concatenate([w_in[:, av], kv[:, 1, 1], kv[:, 2, 1]], axis=1)
    w1 = a["cmp_w1"][0].reshape(2, 2, 8, P, CMP_HIDDEN).transpose(0, 1, 3, 2, 4).reshape(4, P, CW)
    u = a["peer_u"][0].reshape(NKEYS, NKEYS, DC, P).transpose(1, 3, 2, 0).reshape(NKEYS, P, CW)
    v = a["peer_v"][0].reshape(NKEYS, NKEYS, D).transpose(1, 0, 2)
    mem_kv = a["w_mem_kv"][0]
    stream = np.concatenate([
        _column_chunks(mem_kv[:, 0:1024]), _column_chunks(mem_kv[:, 1024:2048]),
        _column_chunks(qk_w), _column_chunks(v_w), w1, _column_chunks(w_in[:, merge]),
        a["w_out"][0].reshape(DC, P, D), _column_chunks(a["peer_wq"][0]), u, v])
    wbr = a["w_branch"][0].copy()
    wbr[1] = wbr[1][perm]
    w_branch = wbr.reshape(3, MIX_C, P, DC, P).transpose(0, 3, 2, 1, 4).reshape(48, P, MIX_C * P)

    def rows_to_parts(m2):
        return np.ascontiguousarray(m2.reshape(DC, P, -1).transpose(1, 0, 2)).reshape(P, -1)

    onehot = np.zeros((BUCKETS, T), np.float32)
    onehot[rel_buckets()[::-1], np.arange(T)] = 1.0
    tpos = np.arange(T)
    ok = (np.arange(N_CMP) * CMP_STRIDE + CMP_LEN - 1)[None, :] <= tpos[:, None]
    ok = ok.reshape(NT, P, N_CMP).transpose(1, 0, 2)
    mask = np.stack([np.where(ok, 0.0, NEG), np.where(ok, 1.0, 0.0)], axis=1).astype(np.float32)
    arrays = {
        "x": a["x"], "x_t": rows_to_parts(a["x"][0].T), "mem_t": rows_to_parts(a["mem"][0].T),
        "stream": stream, "w_gate": rows_to_parts(w_in[:, bg]).reshape(P, DC, 48), "w_branch": w_branch,
        "tab": a["rel_bias"], "buckets_rev": onehot, "lam": a["diff_lambda"].reshape(1, 256),
        "subln": a["diff_subln"].reshape(P, 1),
        "pe_cols": a["cmp_pe"][0].reshape(2, 16, P).transpose(2, 0, 1),
        "w2": a["cmp_w2"][0].reshape(2, 2, P, B_DH).transpose(2, 0, 1, 3),
        "keys_t": a["peer_keys"][0].reshape(DC, NKEYS, P).transpose(2, 0, 1),
        "ln1_g": a["ln1_g"], "ln1_b": a["ln1_b"], "ln2_g": a["ln2_g"], "ln2_b": a["ln2_b"],
        "identity": np.eye(P, dtype=np.float32), "flip": np.eye(P, dtype=np.float32)[::-1],
        "cmp_mask": mask, "iotas": np.broadcast_to(np.arange(P, dtype=np.float32), (P, P)),
    }
    arrays = {k: np.ascontiguousarray(val) for k, val in arrays.items()}
    nc = bacc.Bacc("TRN2", target_bir_lowering=False, num_devices=1)
    args = [nc.dram_tensor(f"in_{k}", val.shape, mybir.dt.from_np(val.dtype), kind="ExternalInput").ap()
            for k, val in arrays.items()]
    args.append(nc.dram_tensor("out", (1, T, D), F32, kind="ExternalOutput").ap())
    build(nc, *args)
    r = run_bass_kernel_spmd(nc, [{f"in_{k}": val for k, val in arrays.items()}], core_ids=[0])
    return r.results[0]["out"]
```

```python
import math
from contextlib import ExitStack

import numpy as np

import concourse.bass as bass
from concourse import mybir

F32 = mybir.dt.float32
F32R = mybir.dt.float32r
U32 = mybir.dt.uint32
ALU = mybir.AluOpType
ACT = mybir.ActivationFunctionType
AX = mybir.AxisListType

P = 128
T = 256
NT = T // P
D = 2048
DC = D // P
A_HEADS, A_DQK, A_DV = 8, 64, 128
B_HEADS, B_GROUPS, B_DH = 16, 4, 64
B_HPG = B_HEADS // B_GROUPS
CMP_LEN, CMP_STRIDE, CMP_HIDDEN = 32, 16, 256
N_CMP = (T - CMP_LEN) // CMP_STRIDE + 1
M_HEADS, M_DH = 4, 256
BUCKETS, MAX_DIST = 32, 1024
HEADS = A_HEADS + B_HEADS
MIX_C = 1024 // P
PEER_HEADS, NKEYS, TOPK = 8, 128, 16
PICKS = PEER_HEADS * TOPK
LN_EPS = 1e-5
ALPHA = 2.0 ** 0.25
BETA_LAM = 0.8 - 0.6
NEG = -1e30
POOL_HALVES = NKEYS

RING = 3
PHASES = [("mem_k", 8, 2), ("mem_v", 8, 2), ("q", 16, 2), ("q_mem", 8, 2), ("k", 16, 2), ("v", 12, 2), ("cmp_w1", 4, 2),
          ("merge", 48, 3),
          ("w_out", 16, 2), ("wq", 16, 2), ("u", NKEYS, 2), ("v_tab", NKEYS, 2)]
HW = 1024
BASE, HALVES = {}, 0
for _name, _count, _h in PHASES:
    BASE[_name] = HALVES
    HALVES += _count * _h
W1_END = BASE["merge"]
W1_HALVES = 8


EVAC = {"mem_k": 0, "mem_v": 8, "q": 16, "q_mem": 32, "k": 40, "v": 56, "wq": 68, "u": 84}
PER = {name: h for name, _, h in PHASES}
NEXT = {a[0]: b[0] for a, b in zip(PHASES, PHASES[1:]) if "cmp_w1" not in (a[0], b[0])}


class Half:

    def __init__(self, name, i, s, k):
        at = BASE[name] + s * PER[name] + k
        self.h = i * (RING * PER[name]) + at
        self.slot = at % RING
        self.landed = i * (16 * PER[name]) + 16 * (at // RING + 1)
        skip = W1_HALVES if BASE[name] >= W1_END else 0
        self.split = self.h + (1 - skip)
        self.free = self.h + 1
        self.done = self.h + (1 + RING)


def halves(name, i, s):
    return [Half(name, i, s, k) for k in range(PER[name])]


def ahead(name, i, s, last):
    if not last:
        return [Half(name, i, s, PER[name] + k) for k in range(PER[name])]
    return halves(NEXT[name], 0, 0) if name in NEXT else []


Q_A, Q_B, Q_M, K_A, K_SEL, K_WIN, RAW_K, RAW_V = 0, 8, 16, 24, 32, 34, 36, 38
V_A, V_SEL, V_WIN, NV_W = 0, 1024, 1280, 1536

SB = 53184
O_RING = 0
O_W = O_RING + RING * HW
O_X = O_W + RING * 2 * HW
XW = DC * T
O_MISC = O_X + 2 * XW
O_H = SB - NKEYS * T
O_QK = O_H
O_RAWP = O_QK + 40 * T
O_KM = O_RAWP + 2 * B_GROUPS * T
O_NV = O_KM + 8 * T
O_MV = O_NV + NT * NV_W
O_BIAS = O_MV + NT * 1024
O_OT = O_BIAS + HEADS * T
O_LEFT = O_OT + 24 * T
assert O_LEFT + 1024 == SB


def rel_buckets():
    n = np.arange(T)
    nf = np.maximum(n, 1).astype(np.float32)
    half = BUCKETS // 2
    large = half + (np.log(nf / np.float32(half)) / np.float32(math.log(MAX_DIST / half))
                    * np.float32(BUCKETS - half)).astype(np.int32)
    return np.where(n < half, n, np.minimum(large, BUCKETS - 1))


def build(nc, x, x_t, mem_t, stream, w_gate, tab, buckets_rev, lam, subln, pe_cols, w2,
          keys_t, ln1_g, ln1_b, ln2_g, ln2_b, identity, flip, cmp_mask, iotas, out):
    ctx = ExitStack()
    with ctx:
        def sem(name):
            return ctx.enter_context(nc.semaphore(name))

        floor = (nc.sbuf_base + 31) // 32 * 32

        def place(name, dt, first, end):
            return first, end, nc.alloc_sbuf_tensor_at(name, [P, end - first], dt, offset=floor + 4 * first)

        f32_parts = [place("raw_ring", F32, O_RING, O_W), place("turns", F32, O_X, O_MISC),
                     place("small", F32, O_MISC, O_H), place("main", F32, O_H, SB)]
        f32r_parts = [place("split_ring", F32R, O_W, O_X), place("split_x", F32R, O_X, O_MISC),
                      place("split_mix", F32R, O_QK, O_QK + 2 * 24 * T),
                      place("split_mem", F32R, O_BIAS, O_BIAS + 2 * XW)]

        def cut(parts, off, n, height):
            first, _, tensor = next(x for x in parts if x[0] <= off and off + n <= x[1])
            return tensor[0:height, off - first:off - first + n]
        ps = ctx.enter_context(nc.psum_tensor("ps", [P, 8, 512], F32))
        bias_rows = nc.dram_tensor("bias_rows", [HEADS, 384], F32, kind="Internal")
        x1_dram = nc.dram_tensor("x1_dram", [P, NT * D], F32, kind="Internal")

        def at(off, n, height=P):
            return cut(f32_parts, off, n, height)

        def at_r(off, n):
            return cut(f32r_parts, off, n, P)

        def split_at(off, n):
            return at_r(off, n), at_r(off + n, n)

        ring = [at(O_RING + s * HW, HW) for s in range(RING)]
        w_hl = [split_at(O_W + s * 2 * HW, HW) for s in range(RING)]
        x_hl = split_at(O_X, XW)
        mem_hl = split_at(O_BIAS, XW)
        mem_raw, x_raw = at(O_QK, XW), at(O_QK + XW, XW)
        ot_hl = split_at(O_QK, 24 * T)

        def by_chunk(pair, c=DC):
            return [a.rearrange("p (c t) -> p c t", c=c) for a in pair]

        qk = at(O_QK, 40 * T).rearrange("p (c t) -> p c t", c=40)
        rawp = at(O_RAWP, 2 * B_GROUPS * T).rearrange("p (k g t) -> p k g t", k=2, g=B_GROUPS)
        cmp_pe_ps = ps[:, 4:8, 0:1]
        km = at(O_KM, 8 * T).rearrange("p (c t) -> p c t", c=8)
        nv = at(O_NV, NT * NV_W).rearrange("p (t n) -> p t n", t=NT)
        mv = at(O_MV, NT * 1024).rearrange("p (t n) -> p t n", t=NT)
        bias = at(O_BIAS, HEADS * T).rearrange("p (h k) -> p h k", h=HEADS)
        ot = at(O_OT, 24 * T).rearrange("p (c t) -> p c t", c=24)
        hank_a = at(O_OT, 16 * T)
        hank_b = at(O_OT + 16 * T, 8 * T)
        pc = at(O_OT, NT * 1024).rearrange("p (t c n) -> p t c n", t=NT, c=8)
        pct = at(O_RAWP, 8 * T).rearrange("p (c t) -> p c t", c=8)
        pt = [at(O_LEFT + 512 * i, 512) for i in range(2)]
        ee = [at(O_MISC + 816 + 512 * i, 512) for i in range(3)]
        m = O_MISC
        ident = at(m, P)
        ones = at(m + 128, P)
        iota = at(m + 256, P)
        gates = at(m + 384, NT * 48).rearrange("p (t n) -> p t n", t=NT)
        small = m + 480
        nmx = [at(small + 4 * i, 2) for i in range(3)]
        mxs = [at(small + 12 + 4 * i, 2) for i in range(3)]
        sums = [at(small + 24 + 4 * i, 2) for i in range(3)]
        rec = [at(small + 36 + 4 * i, 2) for i in range(3)]
        lam_sb = at(small + 48, 1)
        lam_tmp = at(small + 49, 4)
        subln_sb = at(small + 53, 1)
        bn = at(small + 56, 48).rearrange("p (t c s) -> p t c s", t=NT, c=4)
        mean_var = at(small + 104, 4).rearrange("p (t s) -> p t s", t=NT)
        rstd = at(small + 108, 2)
        eps_sb = at(small + 110, 1)
        flip_sb = at(m + 592, P)
        pe_sb = at(m + 720, 32).rearrange("p (k l) -> p k l", k=2)
        cmask = at(m + 752, 60).rearrange("p (k t n) -> p k t n", k=2, t=NT)
        w2_sb = at(m + 2352, 256).rearrange("p (k h n) -> p k h n", k=2, h=2)
        hid = at(m + 2608, 2 * 2 * 60).rearrange("p (k h n) -> p k h n", k=2, h=2)
        hid_pe = at(m + 2848, 4).rearrange("p (k h) -> p k h", k=2)
        cst = at(m + 2852, 64).rearrange("p (a b) -> p a b", a=4)
        assert m + 2916 <= O_H
        w = O_BIAS + 2 * XW
        wgate_sb = at(w, DC * 48).rearrange("p (c n) -> p c n", c=DC)
        lam_in = at(w + 768, 256)
        tab_sb = at(w + 1024, HEADS, BUCKETS)
        rows_sb = at(w + 1056, 384, HEADS)
        brev_sb = at(w + 1440, T, BUCKETS)
        lam_scratch = at(w + 1696, P)
        assert w + 1824 <= SB
        kbd = at(O_QK + RAW_K * T, 256).rearrange("p (j n) -> p j n", j=2)
        vbd = at(O_QK + RAW_K * T + 256, 256).rearrange("p (j n) -> p j n", j=2)
        def st_hl(off, s):
            return split_at(off + 2 * T * (s % RING), T)

        rms = at(O_BIAS + 2048, 2048)
        yt_flat = at(O_OT, DC * T)
        gate_t = [at(O_OT + 4096 + 256 * i, T) for i in range(RING)]
        prod_t = [at(O_OT + 4096 + 256 * (RING + i), T) for i in range(RING)]
        xn = at(O_KM, NT * D).rearrange("p (t n) -> p t n", t=NT)
        gb = [at(O_KM + NT * D + D * k, D) for k in range(2)]
        pq = at(O_H + 28672, DC * T).rearrange("p (c t) -> p c t", c=DC)
        keys = at(O_H + 26624, DC * NKEYS).rearrange("p (c n) -> p c n", c=DC)
        sc = at(O_H + 20480, NT * D).rearrange("p (t n) -> p t n", t=NT)
        hx = at(O_H, NKEYS * T).rearrange("p (j t) -> p j t", j=NKEYS)
        w = O_H + 24576
        vals = at(w, 256).rearrange("p (h c k) -> p h c k", h=PEER_HEADS, c=2)
        idx_u = at(w + 256, 256).bitcast(U32)
        idx_f = at(w + 512, 256).rearrange("p (h c k) -> p h c k", h=PEER_HEADS, c=2)
        comb = at(w + 768, 256)
        comb2 = at(w + 1024, 256)
        seg = at(w + 1024, P)
        fin = at(w + 1280, PICKS)
        pos_u = at(w + 1408, PICKS).bitcast(U32)
        pab_u = at(w + 1536, PICKS).bitcast(U32)
        pab_f = at(w + 1664, PICKS)
        den = at(w + 1792, 16)
        nat = at(m + 720, NT * 3 * P).rearrange("p (t k n) -> p t k n", t=NT, k=3)
        pick_t = at(O_X + 3072, 3 * T).rearrange("p (k t) -> p k t", k=3)
        pick_lo = at(O_X + 3840, T)
        pick_hi = at_r(O_X + 4096, T)
        hot = at_r(O_X, 3072).rearrange("p (b k a n) -> p b k a n", b=2, k=3, a=4)
        x1n = at(O_X + XW, NT * D).rearrange("p (t n) -> p t n", t=NT)
        gb2 = [at(O_X + 2048, D), at(m + 720, D)]

        s_ring = [sem(f"chunk_landed_{s}") for s in range(RING)]
        s_xt, s_mem, s_first, s_wg, s_w2 = (sem(n) for n in (
            "x_t_landed", "mem_t_landed", "constants_landed", "gate_weights_landed", "w2_landed"))
        s_small = sem("small_inputs_landed")
        s_hi, s_lo = sem("high_part_ready"), sem("low_part_ready")
        s_half = sem("half_multiplied")
        s_w1 = sem("compression_half_used")
        s_xhi, s_xlo = sem("operand_high_ready"), sem("operand_low_ready")
        s_sthi = sem("staged_high_ready")
        s_xn, s_gb, s_x1s, s_keys, s_x1l, s_gb2, s_out = (sem(n) for n in (
            "x_landed", "ln1_params_landed", "x1_stored", "keys_landed", "x1_reloaded",
            "ln2_params_landed", "out_stored"))
        s_chunk = sem("projection_ready")
        s_evac = sem("projection_evacuated")
        s_rows, s_rowc, s_rowd, s_hank, s_flip, s_bias = (sem(n) for n in (
            "bias_rows_ready", "bias_rows_copied", "bias_rows_stored", "hankel_landed",
            "bias_flipped", "bias_copied"))
        s_bg, s_gates = sem("gate_logits_ready"), sem("gates_ready")
        s_raw, s_hid, s_hidc, s_w2mm, s_bd = (sem(n) for n in (
            "raw_paired", "cmp_hidden_ready", "cmp_hidden_copied", "cmp_kv_ready", "cmp_kv_copied"))
        s_cs, s_csx, s_cex, s_cp, s_ct, s_ctc = (sem(n) for n in (
            "cmp_scores_ready", "cmp_scores_shifted", "cmp_exp_done", "cmp_probs_ready",
            "cmp_probs_transposed", "cmp_probs_t_copied"))
        s_sc, s_st1, s_exp, s_p, s_tr, s_ptc, s_pv, s_oev = (sem(n) for n in (
            "scores_ready", "scores_biased", "exp_done", "probs_ready", "probs_transposed",
            "probs_t_copied", "values_mixed", "mixed_copied"))
        s_lam, s_lame = sem("lambda_sums_ready"), sem("lambda_exp_done")
        s_sq, s_ss, s_rt, s_da = (sem(n) for n in (
            "squares_ready", "square_sums_ready", "rms_root_ready", "diff_heads_scaled"))
        s_gmm, s_umm, s_gsig, s_mul, s_yacc = (sem(n) for n in (
            "merge_logits_ready", "branch_up_ready", "merge_gate_ready", "gated_product_ready",
            "gated_sum_ready"))
        s_stage, s_y = sem("weights_staged"), sem("wide_product_ready")
        s_v = sem("vector_chain")
        s_a = sem("scalar_chain")
        s_lnv, s_lnr, s_x1, s_x1t, s_x1tc = (sem(n) for n in (
            "variance_ready", "deviation_ready", "x1_ready", "x1_transposed", "x1_t_copied"))
        s_ps, s_psc, s_tke, s_tkx, s_nat, s_natt, s_pick = (sem(n) for n in (
            "key_scores_ready", "key_scores_copied", "topk_shifted", "topk_exp_done",
            "picks_ready", "picks_transposed", "picks_t_copied"))
        s_hot, s_g, s_w = sem("one_hots_ready"), sem("gate_matrix_ready"), sem("expert_weights_ready")
        s_lnv2, s_lnr2, s_fin = sem("variance2_ready"), sem("deviation2_ready"), sem("out_ready")

        maps = [("diff", h, mm, 0) for h in range(A_HEADS) for mm in range(2)]
        maps += [("nsa", c, br, half) for c in range(8) for br in range(2) for half in range(2)]
        maps += [("mem", h, 0, 0) for h in range(M_HEADS)]
        NM = len(maps)
        unit_of, units = {}, []
        for k, (kind, _, b, _) in enumerate(maps):
            if kind != "diff" or b == 1:
                unit_of[k] = len(units)
                units.append(k)
        jobs = [k for k, (kind, _, b, half) in enumerate(maps)
                if kind == "mem" or (kind == "diff" and b == 1) or (kind == "nsa" and b == 1 and half == 1)]
        job_of = {k: j for j, k in enumerate(jobs)}

        def job_at(k):
            return next(j for j, last in enumerate(jobs) if last >= k)

        def rolled(eng, n, body):
            full = (n - 1) // RING
            with eng.Fori(0, full) as i:
                for s in range(RING):
                    body(i, s, False)
            for k in range(full * RING, n):
                body(k // RING, k % RING, k == n - 1)

        block = ctx.enter_context(nc.Block())

        @block.sync
        def _(sp):
            sp.dma_start(mem_raw, mem_t).then_inc(s_mem, 16)

            def load(h, s, used, count):
                if used is not None:
                    sp.wait_ge(used, count)
                sp.dma_start(ring[s], stream[h]).then_inc(s_ring[s], 16)

            for h in range(RING):
                load(h, h, None, 0)
            w1_first = BASE["cmp_w1"]
            rows = w1_first // RING
            with sp.Fori(1, rows + 1) as i:
                for s in range(RING):
                    load(i * RING + s, s, s_lo, i * RING + (s - RING + 1))
            for h in range((rows + 1) * RING, W1_END + RING):
                if h - RING < w1_first:
                    load(h, h % RING, s_lo, h - RING + 1)
                else:
                    load(h, h % RING, s_w1, h - RING + 1 - w1_first)
            assert (W1_END + RING) % RING == 0
            with sp.Fori((W1_END + RING) // RING, HALVES // RING) as i:
                for s in range(RING):
                    load(i * RING + s, s, s_lo, i * RING + (s - RING + 1 - W1_HALVES))
            for t in range(NT):
                sp.wait_ge(s_fin, t + 1)
                sp.dma_start(out[0, t * P:(t + 1) * P, :], x1n[:, t, :]).then_inc(s_out, 16)
            sp.wait_ge(s_out, NT * 16)

        @block.gpsimd
        def _(pool):
            pool.memset(ones, 1.0)
            pool.memset(eps_sb, LN_EPS).then_inc(s_first, 1)
            pool.wait_ge(s_rowd, 16)
            pool.wait_ge(s_half, BASE["q"] + RING)
            pool.wait_ge(s_bg, 1)
            pool.wait_ge(s_lam, 1)
            pool.dma_start(hank_a, bass.AP(bias_rows, 0, [[1, P], [384, 16], [1, T]])).then_inc(s_hank, 16)
            pool.dma_start(hank_b, bass.AP(bias_rows, 16 * 384, [[1, P], [384, 8], [1, T]])).then_inc(s_hank, 16)
            pool.wait_ge(s_da, 1)
            pool.dma_start(xn, x.rearrange("b (t p) n -> p (b t) n", p=P)).then_inc(s_xn, 16)
            pool.dma_start(gb[0], ln1_g.to_broadcast([P, D])).then_inc(s_gb, 16)
            pool.dma_start(gb[1], ln1_b.to_broadcast([P, D])).then_inc(s_gb, 16)
            pool.wait_ge(s_half, BASE["wq"] + RING)
            pool.dma_start(keys, keys_t).then_inc(s_keys, 16)
            pool.wait_ge(s_x1, NT)
            pool.dma_start(x1_dram.ap(), xn.rearrange("p t n -> p (t n)")).then_inc(s_x1s, 16)
            pool.wait_ge(s_lo, Half("u", 0, 0, 1).split)

            def low(i, s, last):
                n = BASE["u"] + 2 + s
                w_hi, w_lo = w_hl[n % RING]
                pool.wait_ge(s_hi, i * RING + (n + 1 - W1_HALVES))
                pool.tensor_tensor(w_lo, ring[n % RING], w_hi.bitcast(F32), ALU.subtract).then_inc(s_lo, 1)

            rolled(pool, POOL_HALVES, low)
            pool.wait_ge(s_g, T // 4)
            pool.wait_ge(s_w, 2 + T // 4)
            pool.dma_start(gb2[0], ln2_g.to_broadcast([P, D])).then_inc(s_gb2, 16)
            pool.dma_start(gb2[1], ln2_b.to_broadcast([P, D])).then_inc(s_gb2, 16)
            pool.wait_ge(s_x1s, 16)
            pool.dma_start(x1n.rearrange("p t n -> p (t n)"), x1_dram.ap()).then_inc(s_x1l, 16)

        @block.scalar
        def _(act):
            chain = [0]

            def link(ins):
                chain[0] += 1
                ins.then_inc(s_a, 1)
                act.wait_ge(s_a, chain[0])

            act.dma_start(x_raw, x_t).then_inc(s_xt, 16)
            for dst, src in ((ident, identity), (iota, iotas), (flip_sb, flip),
                             (tab_sb, tab), (brev_sb, buckets_rev)):
                act.dma_start(dst, src).then_inc(s_small, 16)
            act.dma_start(wgate_sb, w_gate).then_inc(s_wg, 16)
            for dst, src in ((lam_in, lam.to_broadcast([P, 256])),
                             (subln_sb, subln), (pe_sb, pe_cols), (cmask, cmp_mask)):
                act.dma_start(dst, src).then_inc(s_wg, 16)
            act.wait_ge(s_rows, 1)
            act.activation(rows_sb[:, 0:T], ps[0:HEADS, 7, 0:T], ACT.Copy).then_inc(s_rowc, 1)
            act.wait_ge(s_rowc, 2)
            act.dma_start(bias_rows.ap(), rows_sb).then_inc(s_rowd, 16)
            act.wait_ge(s_rowd, 16)
            act.dma_start(w2_sb, w2).then_inc(s_w2, 16)
            act.sem_inc(s_evac, RING)
            act.sem_inc(s_half, RING)

            def highs(todo):
                for x in todo:
                    act.wait_ge(s_ring[x.slot], x.landed)
                    act.wait_ge(s_half, x.free)
                    act.activation(w_hl[x.slot][0], ring[x.slot], ACT.Copy).then_inc(s_hi, 1)

            highs(halves("mem_k", 0, 0))
            for raw, pair, landed in ((mem_raw, mem_hl, s_mem), (x_raw, x_hl, s_xt)):
                act.wait_ge(landed, 16)
                for q in range(4):
                    act.activation(pair[0][:, q * 1024:(q + 1) * 1024], raw[:, q * 1024:(q + 1) * 1024],
                                   ACT.Copy).then_inc(s_xhi, 1)

            def evac_t(name, n, dst, scale=1.0, func=ACT.Copy, off=0, bank0=0, to_next=True):
                def body(i, s, last):
                    highs(ahead(name, i, s + off, last and to_next))
                    act.wait_ge(s_half, Half(name, i, s + off, 1).done)
                    act.activation(dst[:, bass.ds(i * (RING * T) + (s + off) * T, T)],
                                   ps[:, bank0 + (EVAC[name] + off + s) % RING, 0:T],
                                   func, scale=scale).then_inc(s_evac, 1)
                rolled(act, n, body)

            def evac_n(name, n, dst):
                def body(i, s, last):
                    highs(ahead(name, i, s, last))
                    act.wait_ge(s_half, Half(name, i, s, 1).done)
                    act.activation(dst[:, :, bass.ds(i * (RING * P) + s * P, P)],
                                   ps[:, (EVAC[name] + s) % RING, 0:T].rearrange("p (t n) -> p t n", t=NT),
                                   ACT.Copy).then_inc(s_evac, 1)
                rolled(act, n, body)

            evac_t("mem_k", 8, at(O_KM, 8 * T))
            evac_n("mem_v", 8, mv)
            evac_t("q", 16, at(O_QK, 16 * T), A_DQK ** -0.5)
            evac_t("q_mem", 8, at(O_QK + Q_M * T, 8 * T), M_DH ** -0.5)
            evac_t("k", 16, at(O_QK + K_A * T, 16 * T))
            evac_n("v", 12, nv)
            act.wait_ge(s_bg, 1)
            act.activation(gates, ps[:, 7, 0:96].rearrange("p (t n) -> p t n", t=NT),
                           ACT.Sigmoid).then_inc(s_gates, 1)
            for q in range(12):
                act.wait_ge(s_flip, q + 1)
                act.activation(at(O_BIAS + 512 * q, 512), ps[:, 4 + q % 2, :], ACT.Copy).then_inc(s_bias, 1)
            act.wait_ge(s_lam, 1)
            act.activation(lam_tmp[:, 2:4], lam_tmp[:, 0:2], ACT.Exp).then_inc(s_lame, 1)
            act.wait_ge(s_hid, 1)
            link(act.activation(hid_pe.rearrange("p k h -> p (k h)").unsqueeze(2), cmp_pe_ps, ACT.Copy))
            for kv in range(2):
                for hh in range(2):
                    last = act.activation(hid[:, kv, hh, :], ps[:, 2 * kv + hh, 0:60],
                                          ACT.Gelu_apprx_tanh, bias=hid_pe[:, kv, hh:hh + 1])
            last.then_inc(s_hidc, 1)
            act.wait_ge(s_w2mm, 1)
            act.wait_ge(s_bd, 1)
            for g in range(B_GROUPS):
                j, e = g // 2, g % 2
                act.activation(kbd[64 * e:64 * e + 64, j, 64 * e:64 * e + N_CMP],
                               ps[0:64, 5, g * N_CMP:(g + 1) * N_CMP], ACT.Copy)
                last = act.activation(vbd[64 * e:64 * e + N_CMP, j, 64 * e:64 * e + 64],
                                      ps[0:N_CMP, 6, g * 64:(g + 1) * 64], ACT.Copy)
            last.then_inc(s_bd, 1)
            highs(halves("merge", 0, 0))
            act.wait_ge(s_csx, 1)
            act.activation(pc.rearrange("p t c n -> p (t c n)"), pc.rearrange("p t c n -> p (t c n)"),
                           ACT.Exp).then_inc(s_cex, 1)
            for q in range(4):
                act.wait_ge(s_ct, q + 1)
                act.activation(at(O_RAWP + 512 * q, 512), ps[:, q, :], ACT.Copy).then_inc(s_ctc, 1)

            def exp(k):
                kind = maps[k][0]
                e = ee[k % 3]
                act.wait_ge(s_st1, k + 1)
                if kind == "mem":
                    if k >= 3:
                        act.wait_ge(s_tr, unit_of[k - 3] + 1)
                    parts = [(e[:, t * T:(t + 1) * T], ps[:, k % 3, t * T:(t + 1) * T]) for t in range(NT)]
                else:
                    parts = [(e[:, 0:P],) * 2, (e[:, P:3 * P],) * 2]
                for t, (dst, src) in enumerate(parts):
                    last = act.activation(dst, src, ACT.Exp, bias=nmx[k % 3][:, t:t + 1],
                                          accum_out=sums[k % 3][:, t:t + 1])
                last.then_inc(s_exp, 1)

            def pt_copy(k):
                u = unit_of[k]
                wid = 512 if maps[k][0] == "mem" else 384
                act.wait_ge(s_tr, u + 1)
                if u >= 2:
                    act.wait_ge(s_pv, u - 1)
                act.activation(pt[u % 2][:, 0:wid], ps[:, 3 + u % 2, 0:wid], ACT.Copy).then_inc(s_ptc, 1)

            def o_copy(k):
                kind, c = maps[k][0], maps[k][1]
                j = job_of[k]
                act.wait_ge(s_pv, unit_of[k] + 1)
                b = 5 + j % 2
                if kind == "mem":
                    act.activation(at(O_OT + (16 + 2 * c) * T, 512), ps[:, b, :], ACT.Copy).then_inc(s_oev, 1)
                else:
                    first = 0 if kind == "diff" else 8
                    act.activation(ot[:, first + c, :], ps[:, b, 0:T], ACT.Copy).then_inc(s_oev, 1)

            for k in range(-1, NM + 1):
                if k + 1 < NM:
                    exp(k + 1)
                if k in unit_of:
                    pt_copy(k)
                if k - 1 in job_of:
                    o_copy(k - 1)
            act.wait_ge(s_ss, 1)
            for q in range(4):
                last = act.activation(rms[:, 512 * q:512 * q + 512], ps[:, q, :], ACT.Sqrt,
                                      bias=eps_sb, scale=1.0 / A_DV)
            last.then_inc(s_rt, 1)
            act.wait_ge(s_da, 1)
            for q in range(3):
                act.activation(ot_hl[0][:, q * 2048:(q + 1) * 2048], at(O_OT + q * 2048, 2048),
                               ACT.Copy).then_inc(s_xhi, 1)
            for n in range(3):
                def body(i, s, last):
                    highs(ahead("merge", i, 16 * n + s, last and n == 2))
                    act.wait_ge(s_half, Half("merge", i, 16 * n + s, 1).done)
                    act.wait_ge(s_mul, i * RING + (16 * n + s + 1))
                    b = (16 * n + s) % RING
                    act.activation(gate_t[b], ps[:, b, 0:T], ACT.Sigmoid).then_inc(s_gsig, 1)
                rolled(act, 16, body)

            def wide(name, n, src, off):
                def stage(i, s):
                    act.activation(st_hl(off, s)[0], src[:, bass.ds(i * (RING * T) + s * T, T)],
                                   ACT.Copy).then_inc(s_sthi, 1)

                stage(0, 0)
                def body(i, s, last):
                    highs(ahead(name, i, s, last))
                    if not last:
                        if not isinstance(i, int) or i * RING + s >= 2:
                            act.wait_ge(s_half, i * (2 * RING) + (BASE[name] + RING + 2 * (s - 1)))
                        stage(i, s + 1)
                rolled(act, n, body)

            act.wait_ge(s_yacc, 48)
            wide("w_out", 16, yt_flat, O_QK)
            act.wait_ge(s_lnv, 1)
            act.activation(rstd, mean_var[:, :, 1], ACT.Sqrt, bias=eps_sb).then_inc(s_lnr, 1)
            for q in range(8):
                act.wait_ge(s_x1t, q + 1)
                act.activation(x_hl[0][:, 512 * q:512 * q + 512], ps[:, q % 4, :], ACT.Copy).then_inc(s_xhi, 1)
            evac_t("wq", 16, at(O_H + 28672, DC * T), bank0=3)
            for q in range(8):
                act.wait_ge(s_ps, q + 1)
                act.activation(at(O_H + 20480 + 512 * q, 512), ps[:, (0, 1, 2, 6)[q % 4], :], ACT.Copy).then_inc(s_psc, 1)
            act.wait_ge(s_x1s, 16)
            evac_t("u", 64, at(O_H, NKEYS * T), func=ACT.Gelu_apprx_tanh, bank0=3, to_next=False)
            act.wait_ge(s_tke, 1)
            act.activation(nat[:, :, 2, :], nat[:, :, 2, :], ACT.Exp).then_inc(s_tkx, 1)
            act.wait_ge(s_nat, 1)
            evac_t("u", 64, at(O_H, NKEYS * T), func=ACT.Gelu_apprx_tanh, off=64, bank0=3)
            for q in range(3):
                act.wait_ge(s_natt, q + 1)
                link(act.activation(pick_t[:, q, :], ps[:, q, 0:T], ACT.Copy))
            act.activation(pick_hi, pick_t[:, 2, :], ACT.Copy).then_inc(s_pick, 1)
            act.wait_ge(s_w, 2 + T // 4)
            wide("v_tab", NKEYS, at(O_H, NKEYS * T), O_X)
            act.wait_ge(s_lnv2, 1)
            act.activation(rstd, mean_var[:, :, 1], ACT.Sqrt, bias=eps_sb).then_inc(s_lnr2, 1)

        @block.tensor
        def _(pe):
            def product(out, w, x, first, final):
                pe.matmul(out, w[0], x[0], start=first, stop=False, skip_group_check=True)
                pe.matmul(out, w[0], x[1], start=False, stop=False, skip_group_check=True)
                return pe.matmul(out, w[1], x[0], start=False, stop=final, skip_group_check=True)

            def columns_stationary(name, n, pair, bank0, off=0):
                mv_c = by_chunk(pair)
                def body(i, s, last):
                    out_b = ps[:, bank0 + (EVAC[name] + off + s) % RING, 0:T]
                    for k in range(2):
                        x = Half(name, i, s + off, k)
                        pe.wait_ge(s_lo, x.split)
                        if k == 0:
                            pe.wait_ge(s_evac, i * RING + (EVAC[name] + off + s + 1))
                        w = by_chunk(w_hl[x.slot], 8)
                        for c in range(8):
                            end = product(out_b, [a[:, c, :] for a in w], [a[:, 8 * k + c, :] for a in mv_c],
                                          k == 0 and c == 0, k == 1 and c == 7)
                        end.then_inc(s_half, 1)
                rolled(pe, n, body)

            def tokens_stationary(name, n, pair):
                st_c = by_chunk(pair)
                def body(i, s, last):
                    b = (EVAC[name] + s) % RING
                    for k in range(2):
                        x = Half(name, i, s, k)
                        pe.wait_ge(s_lo, x.split)
                        if k == 0:
                            pe.wait_ge(s_evac, i * RING + (EVAC[name] + s + 1))
                        w = by_chunk(w_hl[x.slot], 8)
                        for t in range(NT):
                            for c in range(8):
                                end = product(ps[:, b, t * P:(t + 1) * P],
                                              [a[:, 8 * k + c, t * P:(t + 1) * P] for a in st_c],
                                              [a[:, c, :] for a in w],
                                              k == 0 and c == 0 and t == 0, k == 1 and c == 7)
                        end.then_inc(s_half, 1)
                rolled(pe, n, body)

            pe.wait_ge(s_small, 5 * 16)
            pe.wait_ge(s_first, 1)
            pe.matmul(ps[0:HEADS, 7, 0:T], tab_sb, brev_sb, start=True, stop=True).then_inc(s_rows, 1)
            pe.wait_ge(s_xlo, 4)
            columns_stationary("mem_k", 8, mem_hl, 0)
            tokens_stationary("mem_v", 8, mem_hl)
            pe.wait_ge(s_xt, 16)
            pe.wait_ge(s_wg, 5 * 16)
            pe.wait_ge(s_rowc, 2)
            for t in range(NT):
                for c in range(DC):
                    last = pe.matmul(ps[:, 7, t * 48:(t + 1) * 48], x_raw[:, c * T + t * P:c * T + (t + 1) * P],
                                     wgate_sb[:, c, :], start=c == 0, stop=c == DC - 1)
            last.then_inc(s_bg, 1)
            pe.wait_ge(s_xlo, 8)
            columns_stationary("q", 16, x_hl, 0)
            columns_stationary("q_mem", 8, x_hl, 0)
            columns_stationary("k", 16, x_hl, 0)
            tokens_stationary("v", 12, x_hl)
            pe.wait_ge(s_hank, 32)
            for q in range(12):
                if q >= 2:
                    pe.wait_ge(s_bias, q - 1)
                src = hank_a[:, q * 512:(q + 1) * 512] if q < 8 else hank_b[:, (q - 8) * 512:(q - 7) * 512]
                pe.matmul(ps[:, 4 + q % 2, :], flip_sb, src, start=True, stop=True).then_inc(s_flip, 1)
            pe.wait_ge(s_raw, 1)
            pe.wait_ge(s_evac, RING + 68)
            pe.wait_ge(s_bias, 12)
            pe.wait_ge(s_gates, 1)
            for n in range(W1_HALVES):
                kv, x = n // 4, Half("cmp_w1", 0, 0, n)
                pe.wait_ge(s_ring[x.slot], x.landed)
                w1 = ring[x.slot].rearrange("p (l n) -> p l n", l=4)
                for l in range(4):
                    l2 = (n % 4) * 4 + l
                    for hh in range(2):
                        lhs = w1[:, l, hh * P:(hh + 1) * P]
                        mov = rawp[:, kv, :, 2 * l2:2 * l2 + 16 * (N_CMP - 1) + 1:16]
                        pe.matmul(ps[:, 2 * kv + hh, 0:60].rearrange("p (g c) -> p g c", g=4), lhs, mov,
                                  start=l2 == 0, stop=l2 == 15)
                        last = pe.matmul(ps[:, 4 + 2 * kv + hh, 0:1], lhs, pe_sb[:, kv, l2:l2 + 1],
                                         start=l2 == 0, stop=l2 == 15)
                last.then_inc(s_w1, 1)
            pe.wait_ge(s_w1, W1_HALVES)
            pe.sem_inc(s_hid, 1)
            pe.sem_inc(s_half, W1_HALVES)
            pe.wait_ge(s_hidc, 1)
            pe.wait_ge(s_w2, 16)
            for hh in range(2):
                pe.matmul(ps[0:64, 5, 0:60], w2_sb[:, 0, hh, :], hid[:, 0, hh, :], start=hh == 0, stop=hh == 1)
            for g in range(B_GROUPS):
                for hh in range(2):
                    last = pe.matmul(ps[0:N_CMP, 6, g * 64:(g + 1) * 64],
                                     hid[:, 1, hh, g * N_CMP:(g + 1) * N_CMP], w2_sb[:, 1, hh, :],
                                     start=hh == 0, stop=hh == 1)
            last.then_inc(s_w2mm, 1)
            pe.wait_ge(s_bd, 2)
            for t in range(NT):
                for c in range(8):
                    b = 2 * t + c // 4
                    last = pe.matmul(ps[:, b, (c % 4) * P:(c % 4 + 1) * P],
                                     qk[:, Q_B + c, t * P:(t + 1) * P], kbd[:, c // 4, :], start=True, stop=True)
            last.then_inc(s_cs, 1)
            pe.wait_ge(s_cp, 1)
            for c in range(8):
                for t in range(NT):
                    last = pe.transpose(ps[:, c // 2, (c % 2) * T + t * P:(c % 2) * T + (t + 1) * P],
                                        pc[:, t, c, :], ident)
                if c % 2:
                    last.then_inc(s_ct, 1)

            def scores(k):
                kind, c, br, half = maps[k]
                if k >= 3:
                    pe.wait_ge(s_exp, k - 2)
                else:
                    pe.wait_ge(s_ctc, 4)
                b = k % 3
                if kind == "mem":
                    for t in range(NT):
                        for d in range(2):
                            last = pe.matmul(ps[:, b, t * T:(t + 1) * T], qk[:, Q_M + 2 * c + d, t * P:(t + 1) * P],
                                             km[:, 2 * c + d, :], start=d == 0, stop=d == 1)
                else:
                    if kind == "diff":
                        q, kk, h0 = qk[:, Q_A + c, :], qk[:, K_A + c, :], 64 * br
                    else:
                        q, kk, h0 = qk[:, Q_B + c, :], qk[:, (K_SEL, K_WIN)[br] + c // 4, :], 64 * half
                    pe.matmul(ps[:, b, 0:P], q[h0:h0 + 64, 0:P], kk[h0:h0 + 64, 0:P], start=True, stop=True)
                    last = pe.matmul(ps[:, b, P:3 * P], q[h0:h0 + 64, P:T], kk[h0:h0 + 64, 0:T],
                                     start=True, stop=True)
                last.then_inc(s_sc, 1)

            def transposes(k):
                u = unit_of[k]
                pe.wait_ge(s_p, u + 1)
                if u >= 2:
                    pe.wait_ge(s_ptc, u - 1)
                e, b = ee[k % 3], 3 + u % 2
                if maps[k][0] == "mem":
                    pairs = [(t * T + kb * P, kb * T + t * P) for t in range(NT) for kb in range(2)]
                else:
                    pairs = [(i * P, i * P) for i in range(3)]
                for a, z in pairs:
                    last = pe.transpose(ps[:, b, z:z + P], e[:, a:a + P], ident)
                last.then_inc(s_tr, 1)

            def mix(k):
                kind, c, br, half = maps[k]
                u, j = unit_of[k], job_at(k)
                b = 5 + j % 2
                pe.wait_ge(s_ptc, u + 1)
                if j >= 2:
                    pe.wait_ge(s_oev, j - 1)
                p_t = pt[u % 2]
                if kind == "mem":
                    for dd in range(2):
                        for kb in range(2):
                            last = pe.matmul(ps[:, b, dd * T:(dd + 1) * T],
                                             mv[:, kb, c * 256 + dd * P:c * 256 + (dd + 1) * P],
                                             p_t[:, kb * T:(kb + 1) * T], start=kb == 0, stop=kb == 1)
                elif kind == "diff":
                    v = nv[:, :, V_A + c * P:V_A + (c + 1) * P]
                    pe.matmul(ps[:, b, 0:T], v[:, 0, :], p_t[:, 0:T], start=True, stop=False)
                    last = pe.matmul(ps[:, b, P:T], v[:, 1, :], p_t[:, T:T + P], start=False, stop=True)
                else:
                    if br == 0 and half == 0:
                        pe.matmul(ps[:, b, 0:T], vbd[:, c // 4, :], pct[:, c, :], start=True, stop=False,
                                  skip_group_check=True)
                    g = 2 * (c // 4) + half
                    v = nv[:, :, (V_SEL, V_WIN)[br] + g * 64:(V_SEL, V_WIN)[br] + (g + 1) * 64]
                    h0 = 64 * half
                    pe.matmul(ps[h0:h0 + 64, b, 0:T], v[:, 0, :], p_t[:, 0:T], start=False, stop=False,
                              skip_group_check=True)
                    last = pe.matmul(ps[h0:h0 + 64, b, P:T], v[:, 1, :], p_t[:, T:T + P], start=False,
                                     stop=br == 1, skip_group_check=True)
                last.then_inc(s_pv, 1)

            scores(0)
            scores(1)
            for k in range(NM + 1):
                if k + 2 < NM:
                    scores(k + 2)
                if k in unit_of:
                    transposes(k)
                if k - 1 in unit_of:
                    mix(k - 1)
            for h in range(A_HEADS):
                if h == 0:
                    pe.wait_ge(s_sq, 1)
                last = pe.matmul(ps[:, h // 2, (h % 2) * T:(h % 2 + 1) * T], ones,
                                 at(O_BIAS + h * T, T), start=True, stop=True)
            last.then_inc(s_ss, 1)
            pe.wait_ge(s_da, 1)
            pe.wait_ge(s_oev, len(jobs))
            pe.wait_ge(s_xlo, 8 + 3)
            x_c, o_c = by_chunk(x_hl), by_chunk(ot_hl, 24)
            for n in range(3):
                def body(i, s, last):
                    b = (16 * n + s) % RING
                    for k in range(3):
                        x = Half("merge", i, 16 * n + s, k)
                        pe.wait_ge(s_lo, x.split)
                        if k == 0:
                            pe.wait_ge(s_gsig, i * RING + (16 * n + s + 1))
                        if k == 2:
                            pe.wait_ge(s_mul, i * RING + (16 * n + s + 1))
                        w = by_chunk(w_hl[x.slot], 8)
                        for c in range(8):
                            mov = o_c if k == 2 else x_c
                            cc = 8 * n + c if k == 2 else 8 * k + c
                            end = product(ps[:, (RING if k == 2 else 0) + b, 0:T], [a[:, c, :] for a in w],
                                          [a[:, cc, :] for a in mov], k != 1 and c == 0, k != 0 and c == 7)
                        end.then_inc(s_half, 1)
                rolled(pe, 16, body)

            def wide(name, n, staged, off):
                def step(i, s, first, final):
                    st = st_hl(off, s)
                    for k in range(2):
                        x = Half(name, i, s, k)
                        pe.wait_ge(s_lo, x.split)
                        if k == 0:
                            pe.wait_ge(s_stage, i * RING + (staged + s + 1))
                        w = w_hl[x.slot]
                        for t in range(NT):
                            for part, others in ((0, (0, 1)), (1, (0,))):
                                for q in range(2):
                                    for o in others:
                                        end = pe.matmul(ps[:, 4 * t + 2 * k + q, :],
                                                        st[part][:, t * P:(t + 1) * P],
                                                        w[o][:, q * 512:(q + 1) * 512],
                                                        start=first and part == 0 and o == 0,
                                                        stop=final and part == 1, skip_group_check=True)
                        end.then_inc(s_half, 1)
                for s in range(RING):
                    step(0, s, s == 0, False)
                full = (n - 1) // RING
                with pe.Fori(1, full) as i:
                    for s in range(RING):
                        step(i, s, False, False)
                for m_ in range(full * RING, n):
                    step(m_ // RING, m_ % RING, False, m_ == n - 1)

            pe.wait_ge(s_mul, RING + 48)
            pe.wait_ge(s_gsig, RING + 48)
            wide("w_out", 16, 0, O_QK)
            pe.wait_ge(s_x1, NT)
            for c in range(DC):
                if c >= 8 and c % 2 == 0:
                    pe.wait_ge(s_xlo, 11 + c // 2 - 3)
                for t in range(NT):
                    last = pe.transpose(ps[:, (c // 2) % 4, (c % 2) * T + t * P:(c % 2) * T + (t + 1) * P],
                                        xn[:, t, c * P:(c + 1) * P], ident)
                if c % 2:
                    last.then_inc(s_x1t, 1)
            pe.wait_ge(s_xlo, 11 + 8)
            columns_stationary("wq", 16, x_hl, 3)
            pe.wait_ge(s_evac, RING + 84)
            pe.wait_ge(s_keys, 16)
            for t in range(NT):
                for c in range(DC):
                    q = t * 4 + c // 4
                    if q >= 4 and c % 4 == 0:
                        pe.wait_ge(s_psc, q - 3)
                    last = pe.matmul(ps[:, (0, 1, 2, 6)[q % 4], (c % 4) * P:(c % 4 + 1) * P], pq[:, c, t * P:(t + 1) * P],
                                     keys[:, c, :], start=True, stop=True)
                    if c % 4 == 3:
                        last.then_inc(s_ps, 1)
            columns_stationary("u", NKEYS, x_hl, 3)
            pe.wait_ge(s_psc, 8)
            pe.wait_ge(s_nat, 1)
            for k in range(3):
                for t in range(NT):
                    last = pe.transpose(ps[:, k, t * P:(t + 1) * P], nat[:, t, k, :], ident)
                last.then_inc(s_natt, 1)
            pe.wait_ge(s_pick, 1)
            with pe.Fori(0, T // 8) as i:
                for b in range(2):
                    pe.wait_ge(s_hot, i * 2 + b + 1)
                    pe.wait_ge(s_w, i * 2 + b + 1)
                    for a in range(4):
                        for part in range(2):
                            last = pe.matmul(ps[:, b, a * P:(a + 1) * P], hot[:, b, part, a, :],
                                             hot[:, b, 2, a, :], start=part == 0, stop=part == 1)
                    last.then_inc(s_g, 1)
            pe.wait_ge(s_evac, RING + 84 + NKEYS)
            pe.wait_ge(s_w, 2 + T // 4)
            wide("v_tab", NKEYS, 16, O_X)

        @block.vector
        def _(dve):
            chain = [0]

            def link(ins):
                chain[0] += 1
                ins.then_inc(s_v, 1)
                dve.wait_ge(s_v, chain[0])

            dve.sem_inc(s_mul, RING)
            dve.sem_inc(s_gsig, RING)
            dve.sem_inc(s_w, 2)
            dve.memset(rows_sb[:, T:384], NEG).then_inc(s_rowc, 1)
            dve.wait_ge(s_wg, 5 * 16)
            for n in range(2):
                last = dve.tensor_tensor_reduce(lam_scratch[:, n * 64:(n + 1) * 64], lam_in[:, n * 128:n * 128 + 64],
                                                lam_in[:, n * 128 + 64:n * 128 + 128], 1.0, 0.0,
                                                ALU.mult, ALU.add, lam_tmp[:, n:n + 1])
            last.then_inc(s_lam, 1)

            def lows(todo):
                for x in todo:
                    dve.wait_ge(s_hi, x.split)
                    w_hi, w_lo = w_hl[x.slot]
                    dve.tensor_tensor(w_lo, ring[x.slot], w_hi.bitcast(F32), ALU.subtract).then_inc(s_lo, 1)

            def lows_of(name, n, off=0):
                rolled(dve, n, lambda i, s, last: lows(ahead(name, i, s + off, last)))

            def low_of(pair, raw, a, z, count):
                dve.wait_ge(s_xhi, count)
                dve.tensor_tensor(pair[1][:, a:z], raw, pair[0][:, a:z].bitcast(F32),
                                  ALU.subtract).then_inc(s_xlo, 1)

            lows(halves("mem_k", 0, 0))
            for m_, (raw, pair) in enumerate(((mem_raw, mem_hl), (x_raw, x_hl))):
                for q in range(4):
                    low_of(pair, raw[:, q * 1024:(q + 1) * 1024], q * 1024, (q + 1) * 1024, 4 * m_ + q + 1)
            for name, n in (("mem_k", 8), ("mem_v", 8), ("q", 16), ("q_mem", 8), ("k", 16), ("v", 12)):
                lows_of(name, n)
            dve.wait_ge(s_flip, 12)
            dve.wait_ge(s_evac, RING + 56)
            for kv in range(2):
                for g in range(B_GROUPS):
                    c, h0 = (RAW_K, RAW_V)[kv] + g // 2, 64 * (g % 2)
                    dve.tensor_copy(rawp[0:64, kv, g, :], qk[h0:h0 + 64, c, :])
                    last = dve.tensor_copy(rawp[64:128, kv, g, 0:T - 1], qk[h0:h0 + 64, c, 1:T])
            last.then_inc(s_raw, 1)
            dve.wait_ge(s_raw, 1)
            dve.memset(at(O_QK + RAW_K * T, 512), 0.0).then_inc(s_bd, 1)
            dve.wait_ge(s_lame, 1)
            link(dve.tensor_tensor(lam_sb, lam_tmp[:, 2:3], lam_tmp[:, 3:4], ALU.subtract))
            link(dve.tensor_scalar(lam_sb, lam_sb, BETA_LAM, None, ALU.add))
            dve.wait_ge(s_cs, 1)
            for t in range(NT):
                dst = pc[:, t, :, :].rearrange("p c n -> p (c n)")
                for q in range(2):
                    link(dve.tensor_copy(dst[:, q * 512:(q + 1) * 512], ps[:, 2 * t + q, :]))
            for t in range(NT):
                v = pc[:, t, :, :].rearrange("p c (e n) -> p (c e) n", e=2)
                real = v[:, :, 0:N_CMP]
                add_m = cmask[:, 0, t, :].unsqueeze(1).to_broadcast([P, 16, N_CMP])
                link(dve.tensor_scalar(real, real, B_DH ** 0.0, None, ALU.mult))
                link(dve.tensor_tensor(real, real, add_m, ALU.add))
                link(dve.tensor_reduce(cst[:, t, :], real, AX.X, ALU.max))
                ins = dve.tensor_tensor(real, real, cst[:, t, :].unsqueeze(2).to_broadcast([P, 16, N_CMP]),
                                        ALU.subtract)
                if t == NT - 1:
                    ins.then_inc(s_csx, 1)
                else:
                    link(ins)
            dve.wait_ge(s_cex, 1)
            dve.wait_ge(s_gates, 1)
            for t in range(NT):
                v = pc[:, t, :, :].rearrange("p c (e n) -> p (c e) n", e=2)
                real = v[:, :, 0:N_CMP]
                link(dve.memset(v[:, :, N_CMP:64], 0.0))
                link(dve.tensor_tensor(real, real, cmask[:, 1, t, :].unsqueeze(1).to_broadcast([P, 16, N_CMP]),
                                       ALU.mult))
                link(dve.tensor_reduce(cst[:, 2 + t, :], real, AX.X, ALU.add))
                link(dve.tensor_scalar(cst[:, 2 + t, :], cst[:, 2 + t, :], 1e-30, None, ALU.max))
                link(dve.reciprocal(cst[:, 2 + t, :], cst[:, 2 + t, :]))
                for j in range(2):
                    g4 = gates[:, t, 8 * j:8 * j + 8].rearrange("p (e i) -> p i e", e=2)
                    r4 = cst[:, 2 + t, 8 * j:8 * j + 8].rearrange("p (i e) -> p i e", e=2)
                    link(dve.tensor_tensor(r4, r4, g4, ALU.mult))
                ins = dve.tensor_tensor(real, real, cst[:, 2 + t, :].unsqueeze(2).to_broadcast([P, 16, N_CMP]),
                                        ALU.mult)
                if t == NT - 1:
                    ins.then_inc(s_cp, 1)
                else:
                    link(ins)

            def head_of(k):
                kind, c, br, half = maps[k]
                return c if kind == "diff" else 8 * (c // 4) + 4 * half + c % 4

            def stage1(k):
                kind, c, br, half = maps[k]
                e, b = ee[k % 3], k % 3
                dve.wait_ge(s_sc, k + 1)
                if kind == "mem":
                    dve.tensor_reduce(nmx[b], ps[:, b, :].rearrange("p (t n) -> p t n", t=NT), AX.X, ALU.max,
                                      negate=True).then_inc(s_st1, 1)
                    return
                if k >= 3 and k - 3 in unit_of:
                    dve.wait_ge(s_tr, unit_of[k - 3] + 1)
                elif k >= 3:
                    dve.wait_ge(s_p, unit_of[k - 2] + 1)
                hb = head_of(k) + (0 if kind == "diff" else A_HEADS)
                if k == 0:
                    dve.wait_ge(s_bias, 12)
                dve.tensor_tensor_reduce(e[:, 0:P], ps[:, b, 0:P], bias[:, hb, P:T], 1.0, NEG, ALU.add,
                                         ALU.max, mxs[b][:, 0:1])
                link(dve.tensor_tensor_reduce(e[:, P:3 * P], ps[:, b, P:3 * P], bias[:, hb, :], 1.0, NEG,
                                              ALU.add, ALU.max, mxs[b][:, 1:2]))
                dve.tensor_scalar(nmx[b], mxs[b], -1.0, None, ALU.mult).then_inc(s_st1, 1)

            def stage2(k):
                kind, c, br, half = maps[k]
                e, b = ee[k % 3], k % 3
                dve.wait_ge(s_exp, k + 1)
                link(dve.reciprocal(rec[b], sums[b]))
                if kind == "nsa":
                    col = (br + 1) * B_HEADS + head_of(k)
                    link(dve.tensor_tensor(rec[b], rec[b], gates[:, :, col], ALU.mult))
                cut = [(0, T), (T, 2 * T)] if kind == "mem" else [(0, P), (P, 3 * P)]
                if kind != "diff":
                    for t, (a, z) in enumerate(cut):
                        last = dve.tensor_scalar(e[:, a:z], e[:, a:z], rec[b][:, t:t + 1], None, ALU.mult)
                    last.then_inc(s_p, 1)
                elif br == 0:
                    for t, (a, z) in enumerate(cut):
                        ins = dve.tensor_scalar(e[:, a:z], e[:, a:z], rec[b][:, t:t + 1], None, ALU.mult)
                    link(ins)
                else:
                    link(dve.tensor_scalar(rec[b], rec[b], lam_sb, -1.0, ALU.mult, ALU.mult))
                    e0 = ee[(k - 1) % 3]
                    for t, (a, z) in enumerate(cut):
                        last = dve.scalar_tensor_tensor(e[:, a:z], e[:, a:z], rec[b][:, t:t + 1], e0[:, a:z],
                                                        ALU.mult, ALU.add)
                    last.then_inc(s_p, 1)

            lows(halves("merge", 0, 0))
            dve.wait_ge(s_ctc, 4)
            stage1(0)
            for k in range(NM):
                if k + 1 < NM:
                    stage1(k + 1)
                stage2(k)
            dve.wait_ge(s_oev, len(jobs))
            o_a = at(O_OT, A_HEADS * T)
            dve.tensor_tensor(at(O_BIAS, A_HEADS * T), o_a, o_a, ALU.mult).then_inc(s_sq, 1)
            dve.wait_ge(s_rt, 1)
            link(dve.reciprocal(rms, rms))
            link(dve.tensor_tensor(o_a, o_a, rms, ALU.mult))
            dve.tensor_scalar(o_a, o_a, subln_sb, 1.0 - BETA_LAM, ALU.mult, ALU.mult).then_inc(s_da, 1)
            for q in range(3):
                low_of(ot_hl, at(O_OT + q * 2048, 2048), q * 2048, (q + 1) * 2048, 8 + q + 1)
            dve.wait_ge(s_xlo, 8 + 3)
            link(dve.memset(yt_flat, 0.0))
            for n in range(3):
                def body(i, s, last):
                    b = (16 * n + s) % RING
                    lows(ahead("merge", i, 16 * n + s, last and n == 2))
                    dve.wait_ge(s_half, Half("merge", i, 16 * n + s, 2).done)
                    dve.wait_ge(s_gsig, i * RING + (16 * n + s + 1 + RING))
                    dve.tensor_tensor(prod_t[b], ps[:, RING + b, 0:T], gate_t[b], ALU.mult).then_inc(s_mul, 1)
                    dve.wait_ge(s_mul, i * RING + (16 * n + s + 1 + RING))
                    if n:
                        dve.wait_ge(s_yacc, i * RING + (16 * (n - 1) + s + 1))
                    dst = yt_flat[:, bass.ds(i * (RING * T) + s * T, T)]
                    dve.tensor_tensor(dst, dst, prod_t[b], ALU.add).then_inc(s_yacc, 1)
                rolled(dve, 16, body)

            def wide(name, n, src, off, staged):
                def stage(i, s):
                    hi, lo = st_hl(off, s)
                    dve.wait_ge(s_sthi, i * RING + (staged + s + 1))
                    dve.tensor_tensor(lo, src[:, bass.ds(i * (RING * T) + s * T, T)], hi.bitcast(F32),
                                      ALU.subtract).then_inc(s_stage, 1)

                stage(0, 0)
                def body(i, s, last):
                    lows(ahead(name, i, s, last))
                    if not last:
                        stage(i, s + 1)
                rolled(dve, n, body)

            dve.wait_ge(s_yacc, 48)
            wide("w_out", 16, yt_flat, O_QK, 0)

            def norm(base, res, params, s_params, s_var, s_root, s_done, s_res):
                dve.wait_ge(s_half, base + RING)
                dve.wait_ge(s_res, 16)
                for t in range(NT):
                    for q in range(4):
                        part = res[:, t, q * 512:(q + 1) * 512]
                        ins = dve.scalar_tensor_tensor(part, part, ALPHA, ps[:, 4 * t + q, :], ALU.mult, ALU.add)
                link(ins)
                for t in range(NT):
                    for q in range(4):
                        ins = dve.bn_stats(bn[:, t, q, :], res[:, t, q * 512:(q + 1) * 512])
                link(ins)
                for t in range(NT):
                    ins = dve.bn_aggr(mean_var[:, t, :], bn[:, t, :, :].rearrange("p c s -> p (c s)"))
                ins.then_inc(s_var, 1)
                dve.wait_ge(s_root, 1)
                link(dve.reciprocal(rstd, rstd))
                dve.wait_ge(s_params, 32)
                for t in range(NT):
                    row = res[:, t, :]
                    link(dve.tensor_scalar(row, row, mean_var[:, t, 0:1], rstd[:, t:t + 1],
                                           ALU.subtract, ALU.mult))
                    link(dve.tensor_tensor(row, row, params[0], ALU.mult))
                    dve.tensor_tensor(row, row, params[1], ALU.add).then_inc(s_done, 1)

            norm(BASE["wq"], xn, gb, s_gb, s_lnv, s_lnr, s_x1, s_xn)

            for q in range(8):
                dve.wait_ge(s_x1t, q + 1)
                low_of(x_hl, ps[:, q % 4, :], 512 * q, 512 * q + 512, 11 + q + 1)
            lows_of("wq", 16)

            BIG = -3e38
            ones16 = iota[:, 0:TOPK]
            for t in range(NT):
                dve.wait_ge(s_psc, 4 * (t + 1))
                idx = idx_u.rearrange("p (h c k) -> p h c k", h=PEER_HEADS, c=2)
                for h in range(PEER_HEADS):
                    for c in range(2):
                        src = sc[:, t, (2 * h + c) * P:(2 * h + c + 1) * P]
                        link(dve.max(vals[:, h, c, 0:8], src))
                        dve.max_index(idx[:, h, c, 0:8], vals[:, h, c, 0:8], src)
                        link(dve.match_replace(seg, vals[:, h, c, 0:8], src, BIG))
                        link(dve.max(vals[:, h, c, 8:16], seg))
                        link(dve.max_index(idx[:, h, c, 8:16], vals[:, h, c, 8:16], seg))
                posv = pos_u
                for h in range(PEER_HEADS):
                    cv = comb.rearrange("p (a b) -> p a b", a=TOPK)
                    link(dve.tensor_tensor(cv, vals[:, h, 0, :].unsqueeze(2).to_broadcast([P, TOPK, TOPK]),
                                           vals[:, h, 1, :].unsqueeze(1).to_broadcast([P, TOPK, TOPK]), ALU.add))
                    f, z = fin[:, h * TOPK:(h + 1) * TOPK], posv[:, h * TOPK:(h + 1) * TOPK]
                    link(dve.max(f[:, 0:8], comb))
                    dve.max_index(z[:, 0:8], f[:, 0:8], comb)
                    link(dve.match_replace(comb2, f[:, 0:8], comb, BIG))
                    link(dve.max(f[:, 8:16], comb2))
                    link(dve.max_index(z[:, 8:16], f[:, 8:16], comb2))
                link(dve.tensor_copy(idx_f.rearrange("p h c k -> p (h c k)"), idx_u))
                work = sc[:, t, :]
                for c in range(2):
                    if c == 0:
                        link(dve.tensor_scalar(pab_u, pos_u, 4, None, ALU.logical_shift_right))
                    else:
                        link(dve.tensor_scalar(pab_u, pos_u, 15, None, ALU.bitwise_and))
                    link(dve.tensor_copy(pab_f, pab_u))
                    wv = work.rearrange("p (n a) -> p n a", a=TOPK)
                    link(dve.tensor_tensor(wv, pab_f.unsqueeze(2).to_broadcast([P, PICKS, TOPK]),
                                           ones16.unsqueeze(1).to_broadcast([P, PICKS, TOPK]), ALU.is_equal))
                    w4 = work.rearrange("p (h k a) -> p h k a", h=PEER_HEADS, k=TOPK)
                    link(dve.tensor_tensor(w4, w4, idx_f[:, :, c, :].unsqueeze(2)
                                           .to_broadcast([P, PEER_HEADS, TOPK, TOPK]), ALU.mult))
                    link(dve.tensor_reduce(nat[:, t, c, :], wv, AX.X, ALU.add))
                f3 = fin.rearrange("p (h k) -> p h k", h=PEER_HEADS)
                ins = dve.tensor_tensor(nat[:, t, 2, :].rearrange("p (h k) -> p h k", h=PEER_HEADS), f3,
                                        f3[:, :, 0:1].to_broadcast([P, PEER_HEADS, TOPK]), ALU.subtract)
                if t == NT - 1:
                    ins.then_inc(s_tke, 1)
                else:
                    link(ins)
            dve.wait_ge(s_tkx, 1)
            for t in range(NT):
                g3 = nat[:, t, 2, :].rearrange("p (h k) -> p h k", h=PEER_HEADS)
                link(dve.tensor_reduce(den[:, t * 8:t * 8 + 8], g3, AX.X, ALU.add))
                link(dve.reciprocal(den[:, t * 8:t * 8 + 8], den[:, t * 8:t * 8 + 8]))
                ins = dve.tensor_tensor(g3, g3, den[:, t * 8:t * 8 + 8].unsqueeze(2)
                                        .to_broadcast([P, PEER_HEADS, TOPK]), ALU.mult)
            ins.then_inc(s_nat, 1)

            dve.wait_ge(s_lo, Half("u", 0, 0, 1).split + POOL_HALVES)
            lows_of("u", 64, 64)
            dve.wait_ge(s_pick, 1)
            dve.wait_ge(s_evac, RING + 84 + NKEYS)
            link(dve.tensor_tensor(pick_lo, pick_t[:, 2, :], pick_hi.bitcast(F32), ALU.subtract))

            def one_hots(i, b, first):
                if not first:
                    dve.wait_ge(s_g, i * 2 + (b - 1))
                for a in range(4):
                    tok = i * 8 + 4 * b + a
                    first_key = at(O_X + 3072, T)[:, bass.ds(tok, 1)]
                    for part, gate in enumerate((pick_hi.bitcast(F32), pick_lo)):
                        dve.tensor_scalar(hot[:, b, part, a, :], iota, first_key, gate[:, bass.ds(tok, 1)],
                                          ALU.is_equal, ALU.mult)
                    last = dve.tensor_scalar(hot[:, b, 2, a, :], iota, at(O_X + 3072 + T, T)[:, bass.ds(tok, 1)],
                                             None, ALU.is_equal)
                last.then_inc(s_hot, 1)

            def weigh(i, b):
                dve.wait_ge(s_g, i * 2 + (b + 1))
                part = hx[:, :, bass.ds(i * 8 + 4 * b, 4)].rearrange("p j a -> p a j")
                dve.tensor_tensor(part, ps[:, b, :].rearrange("p (a j) -> p a j", a=4), part,
                                  ALU.mult).then_inc(s_w, 1)

            one_hots(0, 0, True)
            one_hots(0, 1, True)
            with dve.Fori(1, T // 8) as i:
                for b in range(2):
                    weigh(i - 1, b)
                    one_hots(i, b, False)
            weigh(T // 8 - 1, 0)
            weigh(T // 8 - 1, 1)

            dve.wait_ge(s_w, 2 + T // 4)
            wide("v_tab", NKEYS, at(O_H, NKEYS * T), O_X, 16)

            norm(HALVES, x1n, gb2, s_gb2, s_lnv2, s_lnr2, s_fin, s_x1l)


def _column_chunks(w):
    n = w.shape[1] // P
    return w.reshape(2, DC // 2, P, n, P).transpose(3, 0, 2, 1, 4).reshape(2 * n, P, HW)


def kernel(**inputs):
    import concourse.bacc as bacc
    from concourse.bass_utils import run_bass_kernel_spmd

    a = {k: np.asarray(v) for k, v in inputs.items()}
    w_in = a["w_in"][0]
    widths = [1024, 1024, 1024, 1024, 1536, 48, 1024, 3 * D]
    edge = np.concatenate([[0], np.cumsum(widths)])
    aq, ak, av, bq, bkv, bg, mq, merge = (slice(edge[i], edge[i + 1]) for i in range(8))
    order = [8 * j + 4 * e + i for j in range(2) for i in range(B_HPG) for e in range(2)]
    perm = np.concatenate([np.arange(B_DH) + B_DH * h for h in order])
    kv = w_in[:, bkv].reshape(D, 3, 2, 256)
    qk_w = np.concatenate([w_in[:, aq], w_in[:, bq][:, perm], w_in[:, mq], w_in[:, ak],
                           kv[:, 1, 0], kv[:, 2, 0], kv[:, 0, 0], kv[:, 0, 1]], axis=1)
    v_w = np.concatenate([w_in[:, av], kv[:, 1, 1], kv[:, 2, 1]], axis=1)
    w1 = a["cmp_w1"][0].reshape(2, 4, 4, P, CMP_HIDDEN).transpose(0, 1, 3, 2, 4).reshape(8, P, HW)
    u = a["peer_u"][0].reshape(NKEYS, NKEYS, 2, 8, P).transpose(1, 2, 4, 3, 0).reshape(2 * NKEYS, P, HW)
    v = a["peer_v"][0].reshape(NKEYS, NKEYS, 2, HW).transpose(1, 2, 0, 3).reshape(2 * NKEYS, P, HW)
    mem_kv = a["w_mem_kv"][0]
    wbr = a["w_branch"][0].copy()
    wbr[1] = wbr[1][perm]
    w_up = wbr.reshape(3, MIX_C, P, DC, P).transpose(0, 3, 2, 1, 4).reshape(48, 1, P, HW)
    merged = np.concatenate([_column_chunks(w_in[:, merge]).reshape(48, 2, P, HW), w_up], axis=1)
    stream = np.concatenate([
        _column_chunks(mem_kv[:, 0:1024]), _column_chunks(mem_kv[:, 1024:2048]),
        _column_chunks(qk_w), _column_chunks(v_w), w1, merged.reshape(144, P, HW),
        a["w_out"][0].reshape(DC, P, 2, HW).transpose(0, 2, 1, 3).reshape(2 * DC, P, HW),
        _column_chunks(a["peer_wq"][0]), u, v])

    def rows_to_parts(m2):
        return np.ascontiguousarray(m2.reshape(DC, P, -1).transpose(1, 0, 2)).reshape(P, -1)

    onehot = np.zeros((BUCKETS, T), np.float32)
    onehot[rel_buckets()[::-1], np.arange(T)] = 1.0
    tpos = np.arange(T)
    ok = (np.arange(N_CMP) * CMP_STRIDE + CMP_LEN - 1)[None, :] <= tpos[:, None]
    ok = ok.reshape(NT, P, N_CMP).transpose(1, 0, 2)
    mask = np.stack([np.where(ok, 0.0, NEG), np.where(ok, 1.0, 0.0)], axis=1).astype(np.float32)
    arrays = {
        "x": a["x"], "x_t": rows_to_parts(a["x"][0].T), "mem_t": rows_to_parts(a["mem"][0].T),
        "stream": stream, "w_gate": rows_to_parts(w_in[:, bg]).reshape(P, DC, 48),
        "tab": a["rel_bias"], "buckets_rev": onehot, "lam": a["diff_lambda"].reshape(1, 256),
        "subln": a["diff_subln"].reshape(P, 1),
        "pe_cols": a["cmp_pe"][0].reshape(2, 16, P).transpose(2, 0, 1),
        "w2": a["cmp_w2"][0].reshape(2, 2, P, B_DH).transpose(2, 0, 1, 3),
        "keys_t": a["peer_keys"][0].reshape(DC, NKEYS, P).transpose(2, 0, 1),
        "ln1_g": a["ln1_g"], "ln1_b": a["ln1_b"], "ln2_g": a["ln2_g"], "ln2_b": a["ln2_b"],
        "identity": np.eye(P, dtype=np.float32), "flip": np.eye(P, dtype=np.float32)[::-1],
        "cmp_mask": mask, "iotas": np.broadcast_to(np.arange(P, dtype=np.float32), (P, P)),
    }
    arrays = {k: np.ascontiguousarray(val) for k, val in arrays.items()}
    nc = bacc.Bacc("TRN2", target_bir_lowering=False, num_devices=1)
    args = [nc.dram_tensor(f"in_{k}", val.shape, mybir.dt.from_np(val.dtype), kind="ExternalInput").ap()
            for k, val in arrays.items()]
    args.append(nc.dram_tensor("out", (1, T, D), F32, kind="ExternalOutput").ap())
    build(nc, *args)
    r = run_bass_kernel_spmd(nc, [{f"in_{k}": val for k, val in arrays.items()}], core_ids=[0])
    return r.results[0]["out"]
```

```python
import math
from contextlib import ExitStack

import numpy as np

import concourse.bass as bass
from concourse import mybir

F32 = mybir.dt.float32
F32R = mybir.dt.float32r
U32 = mybir.dt.uint32
ALU = mybir.AluOpType
ACT = mybir.ActivationFunctionType
AX = mybir.AxisListType

P = 128
T = 256
NT = T // P
D = 2048
DC = D // P
A_HEADS, A_DQK, A_DV = 8, 64, 128
B_HEADS, B_GROUPS, B_DH = 16, 4, 64
B_HPG = B_HEADS // B_GROUPS
CMP_LEN, CMP_STRIDE, CMP_HIDDEN = 32, 16, 256
N_CMP = (T - CMP_LEN) // CMP_STRIDE + 1
M_HEADS, M_DH = 4, 256
BUCKETS, MAX_DIST = 32, 1024
HEADS = A_HEADS + B_HEADS
MIX_C = 1024 // P
PEER_HEADS, NKEYS, TOPK = 8, 128, 16
PICKS = PEER_HEADS * TOPK
LN_EPS = 1e-5
ALPHA = 2.0 ** 0.25
BETA_LAM = 0.8 - 0.6
NEG = -1e30
POOL_HALVES = NKEYS
HOT = 4
HB = 4

RING = 3
PHASES = [("mem_k", 8, 2), ("mem_v", 16, 1), ("q", 16, 2), ("q_mem", 8, 2), ("k", 16, 2), ("cmp_w1", 4, 2),
          ("v_diff", 16, 1), ("v_nsa", 8, 1),
          ("merge", 48, 3),
          ("w_out", 16, 2), ("wq", 16, 2), ("u", NKEYS, 2), ("v_tab", NKEYS, 2)]
HW = 1024
BASE, HALVES = {}, 0
for _name, _count, _h in PHASES:
    BASE[_name] = HALVES
    HALVES += _count * _h
W1_END = BASE["v_diff"]
W1_HALVES = 8


EVAC = {"mem_k": 0, "q": 8, "q_mem": 24, "k": 32, "wq": 48, "u": 64}
PER = {name: h for name, _, h in PHASES}
COUNT = {name: n * h for name, n, h in PHASES}
NEXT = {a[0]: b[0] for a, b in zip(PHASES, PHASES[1:]) if "cmp_w1" not in (a[0], b[0])}


class Half:

    def __init__(self, name, i, s, k):
        at = BASE[name] + s * PER[name] + k
        self.h = i * (RING * PER[name]) + at
        self.slot = at % RING
        self.landed = i * (16 * PER[name]) + 16 * (at // RING + 1)
        skip = W1_HALVES if BASE[name] >= W1_END else 0
        self.split = self.h + (1 - skip)
        self.free = self.h + 1
        self.done = self.h + (1 + RING)


def halves(name, i, s):
    return [Half(name, i, s, k) for k in range(PER[name])]


def ahead(name, i, s, last):
    if not last:
        return [Half(name, i, s, PER[name] + k) for k in range(PER[name])]
    return halves(NEXT[name], 0, 0) if name in NEXT else []


Q_A, Q_B, Q_M, K_A, K_SEL, K_WIN, RAW_K, RAW_V = 0, 8, 16, 24, 32, 34, 36, 38
V_A, V_SEL, V_WIN, NV_W = 0, 1024, 1280, 1536

SB = 53184
O_RING = 0
O_W = O_RING + RING * HW
O_X = O_W + RING * 2 * HW
XW = DC * T
O_MISC = O_X + 2 * XW
O_H = SB - NKEYS * T
O_QK = O_H
O_RAWP = O_QK + 40 * T
O_KM = O_RAWP + 2 * B_GROUPS * T
O_NV = O_KM + 8 * T
O_MV = O_NV + NT * NV_W
O_BIAS = O_MV + NT * 1024
O_OT = O_BIAS + HEADS * T
O_LEFT = O_OT + 24 * T
assert O_LEFT + 1024 == SB


def rel_buckets():
    n = np.arange(T)
    nf = np.maximum(n, 1).astype(np.float32)
    half = BUCKETS // 2
    large = half + (np.log(nf / np.float32(half)) / np.float32(math.log(MAX_DIST / half))
                    * np.float32(BUCKETS - half)).astype(np.int32)
    return np.where(n < half, n, np.minimum(large, BUCKETS - 1))


def build(nc, x, x_t, mem_t, stream, w_gate, tab, buckets_rev, lam, subln, pe_cols, w2,
          keys_t, ln1_g, ln1_b, ln2_g, ln2_b, identity, flip, cmp_mask, iotas, out):
    ctx = ExitStack()
    with ctx:
        def sem(name):
            return ctx.enter_context(nc.semaphore(name))

        floor = (nc.sbuf_base + 31) // 32 * 32

        def place(name, dt, first, end):
            return first, end, nc.alloc_sbuf_tensor_at(name, [P, end - first], dt, offset=floor + 4 * first)

        f32_parts = [place("raw_ring", F32, O_RING, O_W), place("turns", F32, O_X, O_MISC),
                     place("small", F32, O_MISC, O_H), place("main", F32, O_H, SB)]
        f32r_parts = [place("split_ring", F32R, O_W, O_X), place("split_x", F32R, O_X, O_MISC),
                      place("split_mix", F32R, O_QK, O_QK + 2 * 24 * T),
                      place("split_mem", F32R, O_BIAS, O_BIAS + 2 * XW)]

        def cut(parts, off, n, height):
            first, _, tensor = next(x for x in parts if x[0] <= off and off + n <= x[1])
            return tensor[0:height, off - first:off - first + n]
        ps = ctx.enter_context(nc.psum_tensor("ps", [P, 8, 512], F32))
        bias_rows = nc.dram_tensor("bias_rows", [HEADS, 384], F32, kind="Internal")
        x1_dram = nc.dram_tensor("x1_dram", [P, NT * D], F32, kind="Internal")

        def at(off, n, height=P):
            return cut(f32_parts, off, n, height)

        def at_r(off, n):
            return cut(f32r_parts, off, n, P)

        def split_at(off, n):
            return at_r(off, n), at_r(off + n, n)

        ring = [at(O_RING + s * HW, HW) for s in range(RING)]
        w_hl = [split_at(O_W + s * 2 * HW, HW) for s in range(RING)]
        x_hl = split_at(O_X, XW)
        mem_hl = split_at(O_BIAS, XW)
        mem_raw, x_raw = at(O_QK, XW), at(O_QK + XW, XW)
        ot_hl = split_at(O_QK, 24 * T)

        def by_chunk(pair, c=DC):
            return [a.rearrange("p (c t) -> p c t", c=c) for a in pair]

        qk = at(O_QK, 40 * T).rearrange("p (c t) -> p c t", c=40)
        rawp = at(O_RAWP, 2 * B_GROUPS * T).rearrange("p (k g t) -> p k g t", k=2, g=B_GROUPS)
        windows = at(O_NV, 2 * 16 * B_GROUPS * N_CMP).rearrange("p (k l n) -> p k l n", k=2, l=16)
        km = at(O_KM, 8 * T).rearrange("p (c t) -> p c t", c=8)
        nv = at(O_NV, NT * NV_W).rearrange("p (t n) -> p t n", t=NT)
        mv = at(O_MV, NT * 1024).rearrange("p (t n) -> p t n", t=NT)
        bias = at(O_BIAS, HEADS * T).rearrange("p (h k) -> p h k", h=HEADS)
        ot = at(O_OT, 24 * T).rearrange("p (c t) -> p c t", c=24)
        hank_a = at(O_OT, 16 * T)
        hank_b = at(O_OT + 16 * T, 8 * T)
        pc = at(O_OT, NT * 1024).rearrange("p (t c n) -> p t c n", t=NT, c=8)
        pct = at(O_RAWP, 8 * T).rearrange("p (c t) -> p c t", c=8)
        pt = [at(O_LEFT + 512 * i, 512) for i in range(2)]
        ee = [at(O_MISC + 816 + 512 * i, 512) for i in range(3)]
        m = O_MISC
        ident = at(m, P)
        strip = at(m + 128, 2 * A_HEADS - 1)
        iota = at(m + 256, P)
        gates = at(m + 384, NT * 48).rearrange("p (t n) -> p t n", t=NT)
        small = m + 480
        nmx = [at(small + 4 * i, 2) for i in range(3)]
        mxs = [at(small + 12 + 4 * i, 2) for i in range(3)]
        sums = [at(small + 24 + 4 * i, 2) for i in range(3)]
        rec = [at(small + 36 + 4 * i, 2) for i in range(3)]
        lam_sb = at(small + 48, 1)
        lam_tmp = at(small + 49, 4)
        subln_sb = at(small + 53, 1)
        row_sums = at(small + 56, 4 * NT)
        row_sum, neg_mean, sq_sum, rstd = (at(small + 64 + 2 * i, NT) for i in range(4))
        eps_sb = at(small + 110, 1)
        flip_sb = at(m + 592, P)
        pe_sb = at(m + 720, 32).rearrange("p (k l) -> p k l", k=2)
        cmask = at(m + 752, 60).rearrange("p (k t n) -> p k t n", k=2, t=NT)
        w2_sb = at(m + 2352, 256).rearrange("p (k h n) -> p k h n", k=2, h=2)
        hid = at(m + 2608, 2 * 2 * 60).rearrange("p (k h n) -> p k h n", k=2, h=2)
        cst = at(m + 2852, 64).rearrange("p (a b) -> p a b", a=4)
        assert m + 2916 <= O_H
        w = O_BIAS + 2 * XW
        wgate_sb = at(w, DC * 48).rearrange("p (c n) -> p c n", c=DC)
        lam_in = at(w + 768, 256)
        tab_sb = at(w + 1024, HEADS, BUCKETS)
        rows_sb = at(w + 1056, 384, HEADS)
        brev_sb = at(w + 1440, T, BUCKETS)
        lam_scratch = at(w + 1696, P)
        assert w + 1824 <= SB
        kbd = at(O_QK + RAW_K * T, 256).rearrange("p (j n) -> p j n", j=2)
        vbd = at(O_QK + RAW_K * T + 256, 256).rearrange("p (j n) -> p j n", j=2)
        def st_hl(off, s):
            return split_at(off + 2 * T * (s % RING), T)

        squares = at(O_BIAS, A_HEADS * T)
        rows_of = at(O_BIAS, A_HEADS * P, A_HEADS).rearrange("p (h n) -> p h n", h=A_HEADS)
        root = at(O_BIAS + A_HEADS * P, T, A_HEADS)
        root_inv = at(O_BIAS + A_HEADS * P + T, T, A_HEADS)
        yt_flat = at(O_OT, DC * T)
        gate_t = [at(O_OT + 4096 + 256 * i, T) for i in range(RING)]
        prod_t = [at(O_OT + 4096 + 256 * (RING + i), T) for i in range(RING)]
        xn = at(O_KM, NT * D).rearrange("p (t n) -> p t n", t=NT)
        gb = [at(O_KM + NT * D + D * k, D) for k in range(2)]
        norm_sq = at(O_H + 2048, D)
        norm_mid = [at(O_H + 4096 + D * t, D) for t in range(NT)]
        pq = at(O_H + 28672, DC * T).rearrange("p (c t) -> p c t", c=DC)
        keys = at(O_H + 26624, DC * NKEYS).rearrange("p (c n) -> p c n", c=DC)
        sc = at(O_H + 20480, NT * D).rearrange("p (t n) -> p t n", t=NT)
        hx = at(O_H, NKEYS * T).rearrange("p (j t) -> p j t", j=NKEYS)
        w = O_H + 24576
        vals = at(w, 256).rearrange("p (h c k) -> p h c k", h=PEER_HEADS, c=2)
        idx_u = at(w + 256, 256).bitcast(U32)
        idx_f = at(w + 512, 256).rearrange("p (h c k) -> p h c k", h=PEER_HEADS, c=2)
        comb = at(w + 768, 256)
        comb2 = at(w + 1024, 256)
        seg = at(w + 1024, P)
        fin = at(w + 1280, PICKS)
        pos_u = at(w + 1408, PICKS).bitcast(U32)
        pab_u = at(w + 1536, PICKS).bitcast(U32)
        pab_f = at(w + 1664, PICKS)
        den = at(w + 1792, 16)
        nat = at(m + 720, NT * 3 * P).rearrange("p (t k n) -> p t k n", t=NT, k=3)
        hot1, gated, hot2 = ([at(O_X + (HB * k + b) * HOT * P, HOT * P) for b in range(HB)] for k in range(3))
        pick_t = at(O_X + 3 * HB * HOT * P, 3 * T).rearrange("p (k t) -> p k t", k=3)
        x1n = at(O_X + XW, NT * D).rearrange("p (t n) -> p t n", t=NT)
        gb2 = [at(O_X + 2048, D), at(m + 720, D)]

        s_ring = [sem(f"chunk_landed_{s}") for s in range(RING)]
        s_mem = [sem(f"mem_t_landed_{q}") for q in range(4)]
        s_xt, s_first, s_wg, s_w2 = (sem(n) for n in (
            "x_t_landed", "constants_landed", "gate_weights_landed", "w2_landed"))
        s_small = sem("small_inputs_landed")
        s_hi, s_lo = sem("high_part_ready"), sem("low_part_ready")
        s_half = sem("half_multiplied")
        s_w1 = sem("compression_half_used")
        s_xhi, s_xlo = sem("operand_high_ready"), sem("operand_low_ready")
        s_sthi = sem("staged_high_ready")
        s_xn, s_gb, s_x1s, s_keys, s_x1l, s_gb2, s_out = (sem(n) for n in (
            "x_landed", "ln1_params_landed", "x1_stored", "keys_landed", "x1_reloaded",
            "ln2_params_landed", "out_stored"))
        s_evac = sem("projection_evacuated")
        s_vev = sem("values_evacuated")
        s_rows, s_rowc, s_rowd, s_hank, s_flip, s_bias = (sem(n) for n in (
            "bias_rows_ready", "bias_rows_copied", "bias_rows_stored", "hankel_landed",
            "bias_flipped", "bias_copied"))
        s_bg, s_gates = sem("gate_logits_ready"), sem("gates_ready")
        s_win = sem("windows_ready")
        s_raw, s_hid, s_hidc, s_w2mm, s_bd = (sem(n) for n in (
            "raw_paired", "cmp_hidden_ready", "cmp_hidden_copied", "cmp_kv_ready", "cmp_kv_copied"))
        s_cs, s_csx, s_cex, s_cp, s_ct, s_ctc = (sem(n) for n in (
            "cmp_scores_ready", "cmp_scores_shifted", "cmp_exp_done", "cmp_probs_ready",
            "cmp_probs_transposed", "cmp_probs_t_copied"))
        s_sc, s_st1, s_exp, s_p, s_tr, s_ptc, s_pv, s_oev = (sem(n) for n in (
            "scores_ready", "scores_biased", "exp_done", "probs_ready", "probs_transposed",
            "probs_t_copied", "values_mixed", "mixed_copied"))
        s_lam, s_lame = sem("lambda_sums_ready"), sem("lambda_exp_done")
        s_sq, s_ss, s_rt, s_ri, s_rb, s_da = (sem(n) for n in (
            "squares_ready", "square_sums_ready", "rms_root_ready", "rms_inverse_ready",
            "rms_broadcast_ready", "diff_heads_scaled"))
        s_gsig, s_mul, s_yacc = (sem(n) for n in (
            "merge_gate_ready", "gated_product_ready", "gated_sum_ready"))
        s_stage = sem("staged_low_ready")
        s_v = sem("vector_chain")
        s_a = sem("scalar_chain")
        s_lnv, s_lnr, s_x1, s_x1t = (sem(n) for n in (
            "mean_ready", "deviation_ready", "x1_ready", "x1_transposed"))
        s_ps, s_psc, s_tke, s_tkx, s_nat, s_natt, s_pick = (sem(n) for n in (
            "key_scores_ready", "key_scores_copied", "topk_shifted", "topk_exp_done",
            "picks_ready", "picks_transposed", "picks_t_copied"))
        s_hot1, s_hotg, s_hotgp, s_hot2v, s_hot2 = (sem(n) for n in (
            "first_keys_ready", "odd_gated_keys_ready", "even_gated_keys_ready", "second_keys_0_ready",
            "second_keys_ready"))
        s_dist, s_dsq = sem("key_distances_ready"), sem("squared_distances_ready")
        s_g, s_w = sem("gate_matrix_ready"), sem("expert_weights_ready")
        s_lnv2, s_lnr2, s_fin = sem("mean2_ready"), sem("deviation2_ready"), sem("out_ready")

        maps = [("diff", h, mm, 0) for h in range(A_HEADS) for mm in range(2)]
        maps += [("nsa", c, br, half) for c in range(8) for br in range(2) for half in range(2)]
        maps += [("mem", h, 0, 0) for h in range(M_HEADS)]
        NM = len(maps)
        unit_of, units = {}, []
        for k, (kind, _, b, _) in enumerate(maps):
            if kind != "diff" or b == 1:
                unit_of[k] = len(units)
                units.append(k)
        jobs = [k for k, (kind, _, b, half) in enumerate(maps)
                if kind == "mem" or (kind == "diff" and b == 1) or (kind == "nsa" and b == 1 and half == 1)]
        job_of = {k: j for j, k in enumerate(jobs)}

        RMS = 4 * 5

        def job_at(k):
            return next(j for j, last in enumerate(jobs) if last >= k)

        def rolled(eng, n, body, rounds=1):
            full = (n - 1) // (RING * rounds)
            with eng.Fori(0, full) as i:
                for s in range(RING * rounds):
                    body(i * rounds if rounds > 1 else i, s, False)
            for k in range(full * RING * rounds, n):
                body(k // RING, k % RING, k == n - 1)

        def lows(eng, todo):
            for x in todo:
                eng.wait_ge(s_hi, x.split)
                w_hi, w_lo = w_hl[x.slot]
                eng.tensor_tensor(w_lo, ring[x.slot], w_hi.bitcast(F32), ALU.subtract).then_inc(s_lo, 1)

        block = ctx.enter_context(nc.Block())

        @block.sync
        def _(sp):
            def load(h, s, used, count):
                if used is not None:
                    sp.wait_ge(used, count)
                sp.dma_start(ring[s], stream[h]).then_inc(s_ring[s], 16)

            load(0, 0, None, 0)
            for q in range(4):
                part = slice(q * 1024, (q + 1) * 1024)
                sp.dma_start(mem_raw[:, part], mem_t[:, part]).then_inc(s_mem[q], 16)
            for h in range(1, RING):
                load(h, h, None, 0)
            w1_first = BASE["cmp_w1"]
            rows = w1_first // RING
            with sp.Fori(1, rows + 1) as i:
                for s in range(RING):
                    load(i * RING + s, s, s_lo, i * RING + (s - RING + 1))
            for h in range((rows + 1) * RING, W1_END + RING):
                if h - RING < w1_first:
                    load(h, h % RING, s_lo, h - RING + 1)
                else:
                    load(h, h % RING, s_w1, h - RING + 1 - w1_first)
            assert (W1_END + RING) % RING == 0
            with sp.Fori((W1_END + RING) // RING, HALVES // RING) as i:
                for s in range(RING):
                    load(i * RING + s, s, s_lo, i * RING + (s - RING + 1 - W1_HALVES))
            for n in range(2 * NT):
                t, cols = n // 2, slice(n % 2 * 1024, n % 2 * 1024 + 1024)
                sp.wait_ge(s_fin, n + 1)
                sp.dma_start(out[0, t * P:(t + 1) * P, cols], x1n[:, t, cols]).then_inc(s_out, 16)
            sp.wait_ge(s_out, 2 * NT * 16)

        @block.gpsimd
        def _(pool):
            pool.memset(strip[:, 0:A_HEADS - 1], 0.0)
            pool.memset(strip[:, A_HEADS - 1:A_HEADS], 1.0)
            pool.memset(strip[:, A_HEADS:2 * A_HEADS - 1], 0.0)
            pool.memset(eps_sb, LN_EPS).then_inc(s_first, 1)
            pool.wait_ge(s_rowd, 16)
            pool.wait_ge(s_half, BASE["q"] + RING)
            pool.wait_ge(s_bg, 1)
            pool.wait_ge(s_lam, 1)
            pool.dma_start(hank_a, bass.AP(bias_rows, 0, [[1, P], [384, 16], [1, T]])).then_inc(s_hank, 16)
            pool.dma_start(hank_b, bass.AP(bias_rows, 16 * 384, [[1, P], [384, 8], [1, T]])).then_inc(s_hank, 16)
            pool.wait_ge(s_lo, BASE["cmp_w1"])
            lows(pool, halves("v_diff", 0, 0))
            for name, n in (("v_diff", 16), ("v_nsa", 8)):
                rolled(pool, n, lambda i, s, last: lows(pool, ahead(name, i, s, last)))
            for p in range(4):
                pool.wait_ge(s_oev, 2 * (p + 1))
                pool.tensor_tensor(squares[:, 512 * p:512 * (p + 1)], at(O_OT + 512 * p, 512),
                                   at(O_OT + 512 * p, 512), ALU.mult).then_inc(s_sq, 1)
            pool.wait_ge(s_oev, len(jobs))
            pool.wait_ge(s_da, 4)
            pool.dma_start(xn, x.rearrange("b (t p) n -> p (b t) n", p=P)).then_inc(s_xn, 16)
            pool.dma_start(gb[0], ln1_g.to_broadcast([P, D])).then_inc(s_gb, 16)
            pool.dma_start(gb[1], ln1_b.to_broadcast([P, D])).then_inc(s_gb, 16)
            pool.wait_ge(s_half, BASE["wq"] + RING)
            pool.dma_start(keys, keys_t).then_inc(s_keys, 16)
            pool.wait_ge(s_x1, 2 * NT)
            pool.dma_start(x1_dram.ap(), xn.rearrange("p t n -> p (t n)")).then_inc(s_x1s, 16)
            pool.wait_ge(s_lo, Half("u", 0, 0, 1).split)

            def low(i, s, last):
                n = BASE["u"] + 2 + s
                w_hi, w_lo = w_hl[n % RING]
                pool.wait_ge(s_hi, i * RING + (n + 1 - W1_HALVES))
                pool.tensor_tensor(w_lo, ring[n % RING], w_hi.bitcast(F32), ALU.subtract).then_inc(s_lo, 1)

            rolled(pool, POOL_HALVES, low, rounds=4)
            pool.wait_ge(s_pick, 3)

            def keys_part(i, first):
                for b in range(HB):
                    here = i * (HB * HOT) + b * HOT
                    if not first:
                        pool.wait_ge(s_g, i * HB + (b + 1 - HB))
                    if b:
                        keys_of = pick_t[:, 1, :][:, bass.ds(here, HOT)]
                        pool.tensor_tensor(hot2[b].rearrange("p (a n) -> p a n", a=HOT),
                                           iota.unsqueeze(1).to_broadcast([P, HOT, P]),
                                           keys_of.unsqueeze(2).to_broadcast([P, HOT, P]),
                                           ALU.subtract).then_inc(s_dist, 1)
                    if b % 2 == 0:
                        pool.wait_ge(s_hot1, i * HB + (b + 1))
                        gate_of = pick_t[:, 2, :][:, bass.ds(here, HOT)]
                        pool.tensor_tensor(gated[b].rearrange("p (a n) -> p a n", a=HOT),
                                           hot1[b].rearrange("p (a n) -> p a n", a=HOT),
                                           gate_of.unsqueeze(2).to_broadcast([P, HOT, P]),
                                           ALU.mult).then_inc(s_hotgp, 1)

            keys_part(0, True)
            with pool.Fori(1, T // (HB * HOT)) as i:
                keys_part(i, False)
            pool.wait_ge(s_g, T // HOT)
            pool.wait_ge(s_w, HB + T // HOT)
            pool.dma_start(gb2[0], ln2_g.to_broadcast([P, D])).then_inc(s_gb2, 16)
            pool.dma_start(gb2[1], ln2_b.to_broadcast([P, D])).then_inc(s_gb2, 16)
            pool.wait_ge(s_x1s, 16)
            pool.dma_start(x1n.rearrange("p t n -> p (t n)"), x1_dram.ap()).then_inc(s_x1l, 16)

        @block.scalar
        def _(act):
            chain = [0]

            def link(ins):
                chain[0] += 1
                ins.then_inc(s_a, 1)
                act.wait_ge(s_a, chain[0])

            act.sem_inc(s_evac, RING)
            act.sem_inc(s_half, RING)

            def highs(todo):
                for x in todo:
                    act.wait_ge(s_ring[x.slot], x.landed)
                    act.wait_ge(s_half, x.free)
                    act.activation(w_hl[x.slot][0], ring[x.slot], ACT.Copy).then_inc(s_hi, 1)

            highs(halves("mem_k", 0, 0))
            for q in range(4):
                act.wait_ge(s_mem[q], 16)
                act.activation(mem_hl[0][:, q * 1024:(q + 1) * 1024], mem_raw[:, q * 1024:(q + 1) * 1024],
                               ACT.Copy).then_inc(s_xhi, 1)
            act.dma_start(x_raw, x_t).then_inc(s_xt, 16)
            for dst, src in ((ident, identity), (iota, iotas), (flip_sb, flip),
                             (tab_sb, tab), (brev_sb, buckets_rev)):
                act.dma_start(dst, src).then_inc(s_small, 16)
            act.dma_start(wgate_sb, w_gate).then_inc(s_wg, 16)
            for dst, src in ((lam_in, lam.to_broadcast([P, 256])),
                             (subln_sb, subln), (pe_sb, pe_cols), (cmask, cmp_mask)):
                act.dma_start(dst, src).then_inc(s_wg, 16)
            act.dma_start(w2_sb, w2).then_inc(s_w2, 16)

            def evac_t(name, n, dst, scale=1.0, func=ACT.Copy, off=0, bank0=0, to_next=True,
                       rounds=1):
                def body(i, s, last):
                    highs(ahead(name, i, s + off, last and to_next))
                    act.wait_ge(s_half, Half(name, i, s + off, 1).done)
                    act.activation(dst[:, bass.ds(i * (RING * T) + (s + off) * T, T)],
                                   ps[:, bank0 + (EVAC[name] + off + s) % RING, 0:T],
                                   func, scale=scale).then_inc(s_evac, 1)
                rolled(act, n, body, rounds)

            def evac_values(name, dst, first, banks):
                act.wait_ge(s_half, BASE[name] + COUNT[name] + RING)
                for n, b in enumerate(banks):
                    t, q = n // (len(banks) // NT), n % (len(banks) // NT)
                    act.activation(dst[:, t, first + 512 * q:first + 512 * (q + 1)], ps[:, b, :],
                                   ACT.Copy).then_inc(s_vev, 1)

            evac_t("mem_k", 8, at(O_KM, 8 * T))
            act.wait_ge(s_rows, 1)
            act.activation(rows_sb[:, 0:T], ps[0:HEADS, 7, 0:T], ACT.Copy).then_inc(s_rowc, 1)
            act.wait_ge(s_rowc, 2)
            act.dma_start(bias_rows.ap(), rows_sb).then_inc(s_rowd, 16)
            act.wait_ge(s_xt, 16)
            for q in range(4):
                rolled(act, 4, lambda i, s, last: highs(ahead("mem_v", i, s + 4 * q, last and q == 3)))
                act.activation(x_hl[0][:, q * 1024:(q + 1) * 1024], x_raw[:, q * 1024:(q + 1) * 1024],
                               ACT.Copy).then_inc(s_xhi, 1)
            evac_values("mem_v", mv, 0, (3, 4, 5, 6))
            evac_t("q", 16, at(O_QK, 16 * T), A_DQK ** -0.5)
            evac_t("q_mem", 8, at(O_QK + Q_M * T, 8 * T), M_DH ** -0.5)
            evac_t("k", 16, at(O_QK + K_A * T, 16 * T))
            act.wait_ge(s_bg, 1)
            act.activation(gates, ps[:, 7, 0:96].rearrange("p (t n) -> p t n", t=NT),
                           ACT.Sigmoid).then_inc(s_gates, 1)
            for q in range(12):
                act.wait_ge(s_flip, q + 1)
                act.activation(at(O_BIAS + 512 * q, 512), ps[:, 4 + q % 2, :], ACT.Copy).then_inc(s_bias, 1)
            act.wait_ge(s_lam, 1)
            act.activation(lam_tmp[:, 2:4], lam_tmp[:, 0:2], ACT.Exp).then_inc(s_lame, 1)
            highs(halves("v_diff", 0, 0))
            act.wait_ge(s_hid, 1)
            for kv in range(2):
                for hh in range(2):
                    last = act.activation(hid[:, kv, hh, :], ps[:, 2 * kv + hh, 0:60], ACT.Gelu_apprx_tanh)
            last.then_inc(s_hidc, 1)
            act.wait_ge(s_w2mm, 1)
            act.wait_ge(s_bd, 1)
            for g in range(B_GROUPS):
                j, e = g // 2, g % 2
                act.activation(kbd[64 * e:64 * e + 64, j, 64 * e:64 * e + N_CMP],
                               ps[0:64, 5, g * N_CMP:(g + 1) * N_CMP], ACT.Copy)
                last = act.activation(vbd[64 * e:64 * e + N_CMP, j, 64 * e:64 * e + 64],
                                      ps[0:N_CMP, 6, g * 64:(g + 1) * 64], ACT.Copy)
            last.then_inc(s_bd, 1)
            rolled(act, 8, lambda i, s, last: highs(ahead("v_diff", i, s, False)))
            act.wait_ge(s_csx, 1)
            act.activation(pc.rearrange("p t c n -> p (t c n)"), pc.rearrange("p t c n -> p (t c n)"),
                           ACT.Exp).then_inc(s_cex, 1)
            rolled(act, 8, lambda i, s, last: highs(ahead("v_diff", i, s + 8, last)))
            for q in range(4):
                act.wait_ge(s_ct, q + 1)
                act.activation(at(O_RAWP + 512 * q, 512), ps[:, q, :], ACT.Copy).then_inc(s_ctc, 1)
            rolled(act, 4, lambda i, s, last: highs(ahead("v_nsa", i, s, False)))
            evac_values("v_diff", nv, V_A, (4, 5, 6, 7))
            rolled(act, 4, lambda i, s, last: highs(ahead("v_nsa", i, s + 4, last)))
            evac_values("v_nsa", nv, V_SEL, (0, 1))

            def exp(k):
                kind = maps[k][0]
                e = ee[k % 3]
                act.wait_ge(s_st1, k + 1)
                if kind == "mem":
                    if k >= 3:
                        act.wait_ge(s_tr, unit_of[k - 3] + 1)
                    parts = [(e[:, t * T:(t + 1) * T], ps[:, k % 3, t * T:(t + 1) * T]) for t in range(NT)]
                else:
                    parts = [(e[:, 0:P],) * 2, (e[:, P:3 * P],) * 2]
                for t, (dst, src) in enumerate(parts):
                    last = act.activation(dst, src, ACT.Exp, bias=nmx[k % 3][:, t:t + 1],
                                          accum_out=sums[k % 3][:, t:t + 1])
                last.then_inc(s_exp, 1)

            def pt_copy(k):
                u = unit_of[k]
                wid = 512 if maps[k][0] == "mem" else 384
                act.wait_ge(s_tr, u + 1)
                if u >= 2:
                    act.wait_ge(s_pv, u - 1)
                act.activation(pt[u % 2][:, 0:wid], ps[:, 3 + u % 2, 0:wid], ACT.Copy).then_inc(s_ptc, 1)

            def o_copy(k):
                kind, c = maps[k][0], maps[k][1]
                j = job_of[k]
                act.wait_ge(s_pv, unit_of[k] + 1)
                b = 5 + j % 2
                if kind == "mem":
                    act.activation(at(O_OT + (16 + 2 * c) * T, 512), ps[:, b, :], ACT.Copy).then_inc(s_oev, 1)
                else:
                    first = 0 if kind == "diff" else 8
                    act.activation(ot[:, first + c, :], ps[:, b, 0:T], ACT.Copy).then_inc(s_oev, 1)

            def branch_high(p):
                act.activation(ot_hl[0][:, 512 * p:512 * (p + 1)], at(O_OT + 512 * p, 512),
                               ACT.Copy).then_inc(s_xhi, 1)

            for k in range(-1, NM + 1):
                if k + 1 < NM:
                    exp(k + 1)
                if k in unit_of:
                    pt_copy(k)
                if k - 1 in job_of:
                    o_copy(k - 1)
                if k == RMS + 1:
                    act.wait_ge(s_ss, 1)
                    act.activation(root, ps[0:A_HEADS, 7, 0:T], ACT.Sqrt, bias=eps_sb[0:A_HEADS],
                                   scale=1.0 / A_DV).then_inc(s_rt, 1)
                p = k - (RMS + 7)
                if 0 <= p < 4:
                    act.wait_ge(s_da, p + 1)
                    branch_high(p)
                if k in (NM - 2, NM - 1):
                    act.wait_ge(s_oev, A_HEADS + 8)
                    for p in (4, 5) if k == NM - 2 else (6, 7):
                        branch_high(p)
            act.wait_ge(s_oev, len(jobs))
            for p in range(8, 12):
                branch_high(p)
            act.wait_ge(s_xlo, 8 + 12)
            for n in range(3):
                def body(i, s, last):
                    highs(ahead("merge", i, 16 * n + s, last and n == 2))
                    act.wait_ge(s_half, Half("merge", i, 16 * n + s, 1).done)
                    act.wait_ge(s_mul, i * RING + (16 * n + s + 1))
                    b = (16 * n + s) % RING
                    act.activation(gate_t[b], ps[:, b, 0:T], ACT.Sigmoid).then_inc(s_gsig, 1)
                rolled(act, 16, body)

            def wide(name, n, src, off):
                def stage(i, s):
                    act.activation(st_hl(off, s)[0], src[:, bass.ds(i * (RING * T) + s * T, T)],
                                   ACT.Copy).then_inc(s_sthi, 1)

                stage(0, 0)
                def body(i, s, last):
                    if not last:
                        if not isinstance(i, int) or i * RING + s >= 2:
                            act.wait_ge(s_half, i * (2 * RING) + (BASE[name] + RING + 2 * (s - 1)))
                        stage(i, s + 1)
                    highs(ahead(name, i, s, last))
                rolled(act, n, body)

            def deviations(res, s_mean, s_root):
                for t in range(NT):
                    act.wait_ge(s_mean, t + 1)
                    link(act.activation(norm_sq, res[:, t, :], ACT.Square, bias=neg_mean[:, t:t + 1],
                                        accum_out=sq_sum[:, t:t + 1]))
                    act.activation(rstd[:, t:t + 1], sq_sum[:, t:t + 1], ACT.Sqrt, bias=eps_sb,
                                   scale=1.0 / D).then_inc(s_root, 1)

            act.wait_ge(s_yacc, 32)
            wide("w_out", 16, yt_flat, O_QK)
            deviations(xn, s_lnv, s_lnr)
            for q in range(8):
                act.wait_ge(s_x1t, q + 1)
                act.activation(x_hl[0][:, 512 * q:512 * q + 512], ps[:, q % 4, :], ACT.Copy).then_inc(s_xhi, 1)
            evac_t("wq", 16, at(O_H + 28672, DC * T), bank0=3)
            for q in range(8):
                act.wait_ge(s_ps, q + 1)
                act.activation(at(O_H + 20480 + 512 * q, 512), ps[:, (0, 1, 2, 6)[q % 4], :], ACT.Copy).then_inc(s_psc, 1)
            act.wait_ge(s_x1s, 16)
            evac_t("u", 64, at(O_H, NKEYS * T), func=ACT.Gelu_apprx_tanh, bank0=3, to_next=False,
                   rounds=4)
            act.wait_ge(s_tke, 1)
            act.activation(nat[:, :, 2, :], nat[:, :, 2, :], ACT.Exp).then_inc(s_tkx, 1)
            act.wait_ge(s_nat, 1)
            evac_t("u", 64, at(O_H, NKEYS * T), func=ACT.Gelu_apprx_tanh, off=64, bank0=3,
                   rounds=4)
            for q in range(3):
                act.wait_ge(s_natt, q + 1)
                act.activation(pick_t[:, q, :], ps[:, q, 0:T], ACT.Copy).then_inc(s_pick, 1)
            act.wait_ge(s_pick, 3)

            def gate(i, b, first):
                act.wait_ge(s_dist, i * (HB - 1) + b)
                act.activation(hot2[b], hot2[b], ACT.Square).then_inc(s_dsq, 1)
                if b % 2:
                    act.wait_ge(s_hot1, i * HB + (b + 1))
                    if not first:
                        act.wait_ge(s_g, i * HB + (b + 1 - HB))
                    for a in range(HOT):
                        g = pick_t[:, 2, :][:, bass.ds(i * (HB * HOT) + (b * HOT + a), 1)]
                        last = act.activation(gated[b][:, a * P:(a + 1) * P], hot1[b][:, a * P:(a + 1) * P],
                                              ACT.Copy, scale=g)
                    last.then_inc(s_hotg, 1)
                act.wait_ge(s_dsq, i * (HB - 1) + b)
                act.activation(hot2[b], hot2[b], ACT.Relu, bias=1.0, scale=-1.0).then_inc(s_hot2, 1)

            for b in range(1, HB):
                gate(0, b, True)
            with act.Fori(1, T // (HB * HOT)) as i:
                for b in range(1, HB):
                    gate(i, b, False)
            act.wait_ge(s_w, HB + T // HOT)
            wide("v_tab", NKEYS, at(O_H, NKEYS * T), O_X)
            deviations(x1n, s_lnv2, s_lnr2)

        @block.tensor
        def _(pe):
            def product(out, w, x, first, final):
                pe.matmul(out, w[0], x[0], start=first, stop=False, skip_group_check=True)
                pe.matmul(out, w[0], x[1], start=False, stop=False, skip_group_check=True)
                return pe.matmul(out, w[1], x[0], start=False, stop=final, skip_group_check=True)

            def columns_stationary(name, n, pair, bank0, rounds=1):
                mv_c = by_chunk(pair)
                def body(i, s, last):
                    out_b = ps[:, bank0 + (EVAC[name] + s) % RING, 0:T]
                    for k in range(2):
                        x = Half(name, i, s, k)
                        pe.wait_ge(s_lo, x.split)
                        if k == 0:
                            pe.wait_ge(s_evac, i * RING + (EVAC[name] + s + 1))
                        w = by_chunk(w_hl[x.slot], 8)
                        for c in range(8):
                            end = product(out_b, [a[:, c, :] for a in w], [a[:, 8 * k + c, :] for a in mv_c],
                                          k == 0 and c == 0, k == 1 and c == 7)
                        end.then_inc(s_half, 1)
                rolled(pe, n, body, rounds)

            def tokens_stationary(name, pair, banks):
                x_c = by_chunk(pair)
                per_tile = len(banks) // NT
                rows = 2 // per_tile
                for n in range(COUNT[name]):
                    x = Half(name, n // RING, n % RING, 0)
                    pe.wait_ge(s_lo, x.split)
                    w = [a.rearrange("p (r q n) -> p r q n", r=rows, n=512) for a in w_hl[x.slot]]
                    for r in range(rows):
                        c = n * rows + r
                        for t in range(NT):
                            for part, other in ((0, 0), (0, 1), (1, 0)):
                                for q in range(per_tile):
                                    end = pe.matmul(ps[:, banks[t * per_tile + q], :],
                                                    x_c[part][:, c, t * P:(t + 1) * P], w[other][:, r, q, :],
                                                    start=c == 0 and part == 0 and other == 0,
                                                    stop=c == DC - 1 and part == 1, skip_group_check=True)
                    end.then_inc(s_half, 1)

            pe.wait_ge(s_xlo, 4)
            columns_stationary("mem_k", 8, mem_hl, 0)
            pe.wait_ge(s_small, 5 * 16)
            pe.wait_ge(s_first, 1)
            pe.matmul(ps[0:HEADS, 7, 0:T], tab_sb, brev_sb, start=True, stop=True).then_inc(s_rows, 1)
            tokens_stationary("mem_v", mem_hl, (3, 4, 5, 6))
            pe.wait_ge(s_xt, 16)
            pe.wait_ge(s_wg, 5 * 16)
            pe.wait_ge(s_rowc, 2)
            for t in range(NT):
                for c in range(DC):
                    last = pe.matmul(ps[:, 7, t * 48:(t + 1) * 48], x_raw[:, c * T + t * P:c * T + (t + 1) * P],
                                     wgate_sb[:, c, :], start=c == 0, stop=c == DC - 1)
            last.then_inc(s_bg, 1)
            pe.wait_ge(s_xlo, 8)
            columns_stationary("q", 16, x_hl, 0)
            columns_stationary("q_mem", 8, x_hl, 0)
            columns_stationary("k", 16, x_hl, 0)
            pe.wait_ge(s_hank, 32)
            pe.wait_ge(s_vev, 4)
            for q in range(12):
                if q >= 2:
                    pe.wait_ge(s_bias, q - 1)
                src = hank_a[:, q * 512:(q + 1) * 512] if q < 8 else hank_b[:, (q - 8) * 512:(q - 7) * 512]
                pe.matmul(ps[:, 4 + q % 2, :], flip_sb, src, start=True, stop=True).then_inc(s_flip, 1)
            pe.wait_ge(s_win, 2 * B_GROUPS)
            pe.wait_ge(s_evac, RING + EVAC["wq"])
            for n in range(W1_HALVES):
                kv, x = n // 4, Half("cmp_w1", 0, 0, n)
                pe.wait_ge(s_ring[x.slot], x.landed)
                w1 = ring[x.slot].rearrange("p (l n) -> p l n", l=4)
                for l in range(4):
                    l2 = (n % 4) * 4 + l
                    for hh in range(2):
                        lhs = w1[:, l, hh * P:(hh + 1) * P]
                        last = pe.matmul(ps[:, 2 * kv + hh, 0:60], lhs, windows[:, kv, l2, :],
                                         start=l2 == 0, stop=l2 == 15)
                last.then_inc(s_w1, 1)
            pe.wait_ge(s_w1, W1_HALVES)
            pe.sem_inc(s_hid, 1)
            pe.sem_inc(s_half, W1_HALVES)
            pe.wait_ge(s_hidc, 1)
            pe.wait_ge(s_w2, 16)
            pe.wait_ge(s_bias, 12)
            pe.wait_ge(s_gates, 1)
            for hh in range(2):
                pe.matmul(ps[0:64, 5, 0:60], w2_sb[:, 0, hh, :], hid[:, 0, hh, :], start=hh == 0, stop=hh == 1)
            for g in range(B_GROUPS):
                for hh in range(2):
                    last = pe.matmul(ps[0:N_CMP, 6, g * 64:(g + 1) * 64],
                                     hid[:, 1, hh, g * N_CMP:(g + 1) * N_CMP], w2_sb[:, 1, hh, :],
                                     start=hh == 0, stop=hh == 1)
            last.then_inc(s_w2mm, 1)
            pe.wait_ge(s_bd, 2)
            for t in range(NT):
                for c in range(8):
                    b = 2 * t + c // 4
                    last = pe.matmul(ps[:, b, (c % 4) * P:(c % 4 + 1) * P],
                                     qk[:, Q_B + c, t * P:(t + 1) * P], kbd[:, c // 4, :], start=True, stop=True)
            last.then_inc(s_cs, 1)
            tokens_stationary("v_diff", x_hl, (4, 5, 6, 7))
            pe.wait_ge(s_cp, 1)
            for c in range(8):
                for t in range(NT):
                    last = pe.transpose(ps[:, c // 2, (c % 2) * T + t * P:(c % 2) * T + (t + 1) * P],
                                        pc[:, t, c, :], ident)
                if c % 2:
                    last.then_inc(s_ct, 1)

            def scores(k):
                kind, c, br, half = maps[k]
                if k >= 3:
                    pe.wait_ge(s_exp if maps[k - 3][0] == "mem" else s_st1, k - 2)
                b = k % 3
                if kind == "mem":
                    for t in range(NT):
                        for d in range(2):
                            last = pe.matmul(ps[:, b, t * T:(t + 1) * T], qk[:, Q_M + 2 * c + d, t * P:(t + 1) * P],
                                             km[:, 2 * c + d, :], start=d == 0, stop=d == 1)
                else:
                    if kind == "diff":
                        q, kk, h0 = qk[:, Q_A + c, :], qk[:, K_A + c, :], 64 * br
                    else:
                        q, kk, h0 = qk[:, Q_B + c, :], qk[:, (K_SEL, K_WIN)[br] + c // 4, :], 64 * half
                    pe.matmul(ps[:, b, 0:P], q[h0:h0 + 64, 0:P], kk[h0:h0 + 64, 0:P], start=True, stop=True)
                    last = pe.matmul(ps[:, b, P:3 * P], q[h0:h0 + 64, P:T], kk[h0:h0 + 64, 0:T],
                                     start=True, stop=True)
                last.then_inc(s_sc, 1)

            def transposes(k):
                u = unit_of[k]
                pe.wait_ge(s_p, u + 1)
                if u >= 2:
                    pe.wait_ge(s_ptc, u - 1)
                e, b = ee[k % 3], 3 + u % 2
                if maps[k][0] == "mem":
                    pairs = [(t * T + kb * P, kb * T + t * P) for t in range(NT) for kb in range(2)]
                else:
                    pairs = [(i * P, i * P) for i in range(3)]
                for a, z in pairs:
                    last = pe.transpose(ps[:, b, z:z + P], e[:, a:a + P], ident)
                last.then_inc(s_tr, 1)

            def mix(k):
                kind, c, br, half = maps[k]
                u, j = unit_of[k], job_at(k)
                b = 5 + j % 2
                pe.wait_ge(s_ptc, u + 1)
                if j >= 2:
                    pe.wait_ge(s_oev, j - 1)
                p_t = pt[u % 2]
                if kind == "mem":
                    for dd in range(2):
                        for kb in range(2):
                            last = pe.matmul(ps[:, b, dd * T:(dd + 1) * T],
                                             mv[:, kb, c * 256 + dd * P:c * 256 + (dd + 1) * P],
                                             p_t[:, kb * T:(kb + 1) * T], start=kb == 0, stop=kb == 1)
                elif kind == "diff":
                    v = nv[:, :, V_A + c * P:V_A + (c + 1) * P]
                    pe.matmul(ps[:, b, 0:T], v[:, 0, :], p_t[:, 0:T], start=True, stop=False)
                    last = pe.matmul(ps[:, b, P:T], v[:, 1, :], p_t[:, T:T + P], start=False, stop=True)
                else:
                    if br == 0 and half == 0:
                        pe.matmul(ps[:, b, 0:T], vbd[:, c // 4, :], pct[:, c, :], start=True, stop=False,
                                  skip_group_check=True)
                    g = 2 * (c // 4) + half
                    v = nv[:, :, (V_SEL, V_WIN)[br] + g * 64:(V_SEL, V_WIN)[br] + (g + 1) * 64]
                    h0 = 64 * half
                    pe.matmul(ps[h0:h0 + 64, b, 0:T], v[:, 0, :], p_t[:, 0:T], start=False, stop=False,
                              skip_group_check=True)
                    last = pe.matmul(ps[h0:h0 + 64, b, P:T], v[:, 1, :], p_t[:, T:T + P], start=False,
                                     stop=br == 1, skip_group_check=True)
                last.then_inc(s_pv, 1)

            pe.wait_ge(s_ctc, 4)
            tokens_stationary("v_nsa", x_hl, (0, 1))
            pe.wait_ge(s_vev, 4 + 4 + 2)
            for k in range(3):
                scores(k)
            for k in range(NM + 1):
                if k + 3 < NM:
                    scores(k + 3)
                if k in unit_of:
                    transposes(k)
                if k - 1 in unit_of:
                    mix(k - 1)
                if k == RMS:
                    pe.wait_ge(s_sq, 4)
                    for h in range(A_HEADS):
                        last = pe.matmul(ps[0:A_HEADS, 7, 0:T], strip[:, A_HEADS - 1 - h:2 * A_HEADS - 1 - h],
                                         squares[:, h * T:(h + 1) * T], start=h == 0, stop=h == A_HEADS - 1)
                    last.then_inc(s_ss, 1)
                p = k - (RMS + 4)
                if 0 <= p < 4:
                    pe.wait_ge(s_ri, 1)
                    if p:
                        pe.wait_ge(s_da, p)
                    for e in range(2):
                        last = pe.matmul(ps[:, 7, e * T:(e + 1) * T], rows_of[:, 2 * p + e, :], root_inv,
                                         start=True, stop=True)
                    last.then_inc(s_rb, 1)
            pe.wait_ge(s_oev, len(jobs))
            x_c, o_c = by_chunk(x_hl), by_chunk(ot_hl, 24)
            for n in range(3):
                pe.wait_ge(s_xlo, 8 + 4 * (n + 1))

                def body(i, s, last):
                    b = (16 * n + s) % RING
                    for k in range(3):
                        x = Half("merge", i, 16 * n + s, k)
                        pe.wait_ge(s_lo, x.split)
                        if k == 0:
                            pe.wait_ge(s_gsig, i * RING + (16 * n + s + 1))
                        if k == 2:
                            pe.wait_ge(s_mul, i * RING + (16 * n + s + 1))
                        w = by_chunk(w_hl[x.slot], 8)
                        for c in range(8):
                            mov = o_c if k == 2 else x_c
                            cc = 8 * n + c if k == 2 else 8 * k + c
                            end = product(ps[:, (RING if k == 2 else 0) + b, 0:T], [a[:, c, :] for a in w],
                                          [a[:, cc, :] for a in mov], k != 1 and c == 0, k != 0 and c == 7)
                        end.then_inc(s_half, 1)
                rolled(pe, 16, body)

            def wide(name, n, staged, off):
                def step(i, s, first, final):
                    st = st_hl(off, s)
                    for k in range(2):
                        x = Half(name, i, s, k)
                        pe.wait_ge(s_lo, x.split)
                        if k == 0:
                            pe.wait_ge(s_stage, i * RING + (staged + s + 1))
                        w = w_hl[x.slot]
                        for t in range(NT):
                            for part, others in ((0, (0, 1)), (1, (0,))):
                                for q in range(2):
                                    for o in others:
                                        end = pe.matmul(ps[:, 4 * t + 2 * k + q, :],
                                                        st[part][:, t * P:(t + 1) * P],
                                                        w[o][:, q * 512:(q + 1) * 512],
                                                        start=first and part == 0 and o == 0,
                                                        stop=final and part == 1, skip_group_check=True)
                        end.then_inc(s_half, 1)
                for s in range(RING):
                    step(0, s, s == 0, False)
                full = (n - 1) // RING
                with pe.Fori(1, full) as i:
                    for s in range(RING):
                        step(i, s, False, False)
                for m_ in range(full * RING, n):
                    step(m_ // RING, m_ % RING, False, m_ == n - 1)

            pe.wait_ge(s_mul, RING + 48)
            pe.wait_ge(s_gsig, RING + 48)
            wide("w_out", 16, 0, O_QK)
            for c in range(DC):
                if c % 8 == 0:
                    pe.wait_ge(s_x1, 3 + c // 8)
                if c >= 8 and c % 2 == 0:
                    pe.wait_ge(s_xlo, 20 + c // 2 - 3)
                for t in range(NT):
                    last = pe.transpose(ps[:, (c // 2) % 4, (c % 2) * T + t * P:(c % 2) * T + (t + 1) * P],
                                        xn[:, t, c * P:(c + 1) * P], ident)
                if c % 2:
                    last.then_inc(s_x1t, 1)
            pe.wait_ge(s_xlo, 20 + 8)
            columns_stationary("wq", 16, x_hl, 3)
            pe.wait_ge(s_evac, RING + EVAC["u"])
            pe.wait_ge(s_keys, 16)
            for t in range(NT):
                for c in range(DC):
                    q = t * 4 + c // 4
                    if q >= 4 and c % 4 == 0:
                        pe.wait_ge(s_psc, q - 3)
                    last = pe.matmul(ps[:, (0, 1, 2, 6)[q % 4], (c % 4) * P:(c % 4 + 1) * P], pq[:, c, t * P:(t + 1) * P],
                                     keys[:, c, :], start=True, stop=True)
                    if c % 4 == 3:
                        last.then_inc(s_ps, 1)
            columns_stationary("u", NKEYS, x_hl, 3, rounds=2)
            pe.wait_ge(s_psc, 8)
            pe.wait_ge(s_nat, 1)
            for k in range(3):
                for t in range(NT):
                    last = pe.transpose(ps[:, k, t * P:(t + 1) * P], nat[:, t, k, :], ident)
                last.then_inc(s_natt, 1)
            pe.wait_ge(s_pick, 3)
            pe.wait_ge(s_evac, RING + EVAC["u"] + NKEYS)
            with pe.Fori(0, T // (HB * HOT)) as i:
                for b in range(HB):
                    pe.wait_ge(s_hotg if b % 2 else s_hotgp, i * 2 + (b // 2 + 1))
                    pe.wait_ge(s_hot2 if b else s_hot2v, i * (HB - 1) + b if b else i + 1)
                    pe.wait_ge(s_w, i * HB + (b + 1))
                    for a in range(HOT):
                        last = pe.matmul(ps[:, b, a * P:(a + 1) * P], gated[b][:, a * P:(a + 1) * P],
                                         hot2[b][:, a * P:(a + 1) * P], start=True, stop=True)
                    last.then_inc(s_g, 1)
            pe.wait_ge(s_w, HB + T // HOT)
            wide("v_tab", NKEYS, 16, O_X)

        @block.vector
        def _(dve):
            chain = [0]

            def link(ins):
                chain[0] += 1
                ins.then_inc(s_v, 1)
                dve.wait_ge(s_v, chain[0])

            dve.sem_inc(s_mul, RING)
            dve.sem_inc(s_gsig, RING)
            dve.sem_inc(s_w, HB)
            dve.memset(rows_sb[:, T:384], NEG).then_inc(s_rowc, 1)
            def lows_of(name, n, off=0):
                rolled(dve, n, lambda i, s, last: lows(dve, ahead(name, i, s + off, last)))

            def low_of(pair, raw, a, z, count):
                dve.wait_ge(s_xhi, count)
                dve.tensor_tensor(pair[1][:, a:z], raw, pair[0][:, a:z].bitcast(F32),
                                  ALU.subtract).then_inc(s_xlo, 1)

            lows(dve, halves("mem_k", 0, 0))
            for q in range(4):
                low_of(mem_hl, mem_raw[:, q * 1024:(q + 1) * 1024], q * 1024, (q + 1) * 1024, q + 1)
            lows_of("mem_k", 8)
            dve.wait_ge(s_wg, 5 * 16)
            for n in range(2):
                last = dve.tensor_tensor_reduce(lam_scratch[:, n * 64:(n + 1) * 64], lam_in[:, n * 128:n * 128 + 64],
                                                lam_in[:, n * 128 + 64:n * 128 + 128], 1.0, 0.0,
                                                ALU.mult, ALU.add, lam_tmp[:, n:n + 1])
            last.then_inc(s_lam, 1)
            for q in range(4):
                rolled(dve, 4, lambda i, s, last: lows(dve, ahead("mem_v", i, s + 4 * q, last and q == 3)))
                low_of(x_hl, x_raw[:, q * 1024:(q + 1) * 1024], q * 1024, (q + 1) * 1024, 4 + q + 1)
            for name, n in (("q", 16), ("q_mem", 8), ("k", 16)):
                lows_of(name, n)
            dve.wait_ge(s_evac, RING + EVAC["wq"])
            for kv in range(2):
                for g in range(B_GROUPS):
                    c, h0 = (RAW_K, RAW_V)[kv] + g // 2, 64 * (g % 2)
                    dve.tensor_copy(rawp[0:64, kv, g, :], qk[h0:h0 + 64, c, :])
                    last = dve.tensor_copy(rawp[64:128, kv, g, 0:T - 1], qk[h0:h0 + 64, c, 1:T])
            last.then_inc(s_raw, 1)
            dve.wait_ge(s_raw, 1)
            for kv in range(2):
                for g in range(B_GROUPS):
                    raw = bass.AP(rawp.tensor, rawp[:, kv, g, 0:1].offset,
                                  [list(rawp.ap[0]), [2, 16], [CMP_STRIDE, N_CMP]])
                    dst = windows[:, kv, :, g * N_CMP:(g + 1) * N_CMP]
                    dve.tensor_tensor(dst, raw, pe_sb[:, kv, :].unsqueeze(2).to_broadcast([P, 16, N_CMP]),
                                      ALU.add).then_inc(s_win, 1)
            dve.memset(at(O_QK + RAW_K * T, 512), 0.0).then_inc(s_bd, 1)
            dve.tensor_scalar(subln_sb, subln_sb, 1.0 - BETA_LAM, None, ALU.mult)
            dve.wait_ge(s_lame, 1)
            link(dve.tensor_tensor(lam_sb, lam_tmp[:, 2:3], lam_tmp[:, 3:4], ALU.subtract))
            link(dve.tensor_scalar(lam_sb, lam_sb, BETA_LAM, None, ALU.add))
            dve.wait_ge(s_cs, 1)
            for t in range(NT):
                dst = pc[:, t, :, :].rearrange("p c n -> p (c n)")
                for q in range(2):
                    link(dve.tensor_copy(dst[:, q * 512:(q + 1) * 512], ps[:, 2 * t + q, :]))
            for t in range(NT):
                v = pc[:, t, :, :].rearrange("p c (e n) -> p (c e) n", e=2)
                real = v[:, :, 0:N_CMP]
                add_m = cmask[:, 0, t, :].unsqueeze(1).to_broadcast([P, 16, N_CMP])
                link(dve.tensor_tensor(real, real, add_m, ALU.add))
                link(dve.tensor_reduce(cst[:, t, :], real, AX.X, ALU.max))
                ins = dve.tensor_tensor(real, real, cst[:, t, :].unsqueeze(2).to_broadcast([P, 16, N_CMP]),
                                        ALU.subtract)
                if t == NT - 1:
                    ins.then_inc(s_csx, 1)
                else:
                    link(ins)
            dve.wait_ge(s_cex, 1)
            dve.wait_ge(s_gates, 1)
            for t in range(NT):
                v = pc[:, t, :, :].rearrange("p c (e n) -> p (c e) n", e=2)
                real = v[:, :, 0:N_CMP]
                link(dve.memset(v[:, :, N_CMP:64], 0.0))
                link(dve.tensor_tensor(real, real, cmask[:, 1, t, :].unsqueeze(1).to_broadcast([P, 16, N_CMP]),
                                       ALU.mult))
                link(dve.tensor_reduce(cst[:, 2 + t, :], real, AX.X, ALU.add))
                link(dve.tensor_scalar(cst[:, 2 + t, :], cst[:, 2 + t, :], 1e-30, None, ALU.max))
                link(dve.reciprocal(cst[:, 2 + t, :], cst[:, 2 + t, :]))
                for j in range(2):
                    g4 = gates[:, t, 8 * j:8 * j + 8].rearrange("p (e i) -> p i e", e=2)
                    r4 = cst[:, 2 + t, 8 * j:8 * j + 8].rearrange("p (i e) -> p i e", e=2)
                    link(dve.tensor_tensor(r4, r4, g4, ALU.mult))
                ins = dve.tensor_tensor(real, real, cst[:, 2 + t, :].unsqueeze(2).to_broadcast([P, 16, N_CMP]),
                                        ALU.mult)
                if t == NT - 1:
                    ins.then_inc(s_cp, 1)
                else:
                    link(ins)

            def head_of(k):
                kind, c, br, half = maps[k]
                return c if kind == "diff" else 8 * (c // 4) + 4 * half + c % 4

            def stage1(k):
                kind, c, br, half = maps[k]
                e, b = ee[k % 3], k % 3
                dve.wait_ge(s_sc, k + 1)
                if kind == "mem":
                    dve.tensor_reduce(nmx[b], ps[:, b, :].rearrange("p (t n) -> p t n", t=NT), AX.X, ALU.max,
                                      negate=True).then_inc(s_st1, 1)
                    return
                if k >= 3 and k - 3 in unit_of:
                    dve.wait_ge(s_tr, unit_of[k - 3] + 1)
                elif k >= 3:
                    dve.wait_ge(s_p, unit_of[k - 2] + 1)
                hb = head_of(k) + (0 if kind == "diff" else A_HEADS)
                if k == 0:
                    dve.wait_ge(s_bias, 12)
                dve.tensor_tensor_reduce(e[:, 0:P], ps[:, b, 0:P], bias[:, hb, P:T], 1.0, NEG, ALU.add,
                                         ALU.max, mxs[b][:, 0:1])
                link(dve.tensor_tensor_reduce(e[:, P:3 * P], ps[:, b, P:3 * P], bias[:, hb, :], 1.0, NEG,
                                              ALU.add, ALU.max, mxs[b][:, 1:2]))
                dve.tensor_scalar(nmx[b], mxs[b], -1.0, None, ALU.mult).then_inc(s_st1, 1)

            def stage2(k):
                kind, c, br, half = maps[k]
                e, b = ee[k % 3], k % 3
                dve.wait_ge(s_exp, k + 1)
                link(dve.reciprocal(rec[b], sums[b]))
                if kind == "nsa":
                    col = (br + 1) * B_HEADS + head_of(k)
                    link(dve.tensor_tensor(rec[b], rec[b], gates[:, :, col], ALU.mult))
                cut = [(0, T), (T, 2 * T)] if kind == "mem" else [(0, P), (P, 3 * P)]
                if kind != "diff":
                    for t, (a, z) in enumerate(cut):
                        last = dve.tensor_scalar(e[:, a:z], e[:, a:z], rec[b][:, t:t + 1], None, ALU.mult)
                    last.then_inc(s_p, 1)
                elif br == 0:
                    for t, (a, z) in enumerate(cut):
                        ins = dve.tensor_scalar(e[:, a:z], e[:, a:z], rec[b][:, t:t + 1], None, ALU.mult)
                    link(ins)
                else:
                    link(dve.tensor_scalar(rec[b], rec[b], lam_sb, -1.0, ALU.mult, ALU.mult))
                    e0 = ee[(k - 1) % 3]
                    for t, (a, z) in enumerate(cut):
                        last = dve.scalar_tensor_tensor(e[:, a:z], e[:, a:z], rec[b][:, t:t + 1], e0[:, a:z],
                                                        ALU.mult, ALU.add)
                    last.then_inc(s_p, 1)

            dve.wait_ge(s_ctc, 4)
            stage1(0)
            def branch_low(p):
                low_of(ot_hl, at(O_OT + 512 * p, 512), 512 * p, 512 * (p + 1), 8 + p + 1)

            for k in range(NM):
                if k + 1 < NM:
                    stage1(k + 1)
                stage2(k)
                if k == RMS + 2:
                    dve.wait_ge(s_ss, 1)
                    dve.tensor_copy(rows_of, ident[0:A_HEADS, 0:A_HEADS].unsqueeze(2)
                                    .to_broadcast([A_HEADS, A_HEADS, P]))
                    dve.wait_ge(s_rt, 1)
                    dve.reciprocal(root_inv, root).then_inc(s_ri, 1)
                p = k - (RMS + 5)
                if 0 <= p < 4:
                    dve.wait_ge(s_rb, p + 1)
                    o2 = at(O_OT + 512 * p, 512)
                    dve.scalar_tensor_tensor(o2, o2, subln_sb, ps[:, 7, :], ALU.mult, ALU.mult).then_inc(s_da, 1)
                p = k - (RMS + 8)
                if 0 <= p < 4:
                    branch_low(p)
            for p in range(4, 12):
                branch_low(p)
            dve.wait_ge(s_xlo, 8 + 12)
            dve.wait_ge(s_lo, Half("merge", 0, 0, 2).split)
            for n in range(3):
                def body(i, s, last):
                    b = (16 * n + s) % RING
                    lows(dve, ahead("merge", i, 16 * n + s, last and n == 2))
                    dve.wait_ge(s_half, Half("merge", i, 16 * n + s, 2).done)
                    dve.wait_ge(s_gsig, i * RING + (16 * n + s + 1 + RING))
                    dst = yt_flat[:, bass.ds(i * (RING * T) + s * T, T)]
                    dve.tensor_tensor(prod_t[b] if n else dst, ps[:, RING + b, 0:T], gate_t[b],
                                      ALU.mult).then_inc(s_mul, 1)
                    if n:
                        dve.wait_ge(s_mul, i * RING + (16 * n + s + 1 + RING))
                        if n == 2:
                            dve.wait_ge(s_yacc, i * RING + (s + 1))
                        dve.tensor_tensor(dst, dst, prod_t[b], ALU.add).then_inc(s_yacc, 1)
                rolled(dve, 16, body)

            def wide(name, n, src, off, staged):
                def stage(i, s):
                    hi, lo = st_hl(off, s)
                    dve.wait_ge(s_sthi, i * RING + (staged + s + 1))
                    dve.tensor_tensor(lo, src[:, bass.ds(i * (RING * T) + s * T, T)], hi.bitcast(F32),
                                      ALU.subtract).then_inc(s_stage, 1)

                stage(0, 0)
                def body(i, s, last):
                    if not last:
                        stage(i, s + 1)
                    lows(dve, ahead(name, i, s, last))
                rolled(dve, n, body)

            dve.wait_ge(s_yacc, 32)
            wide("w_out", 16, yt_flat, O_QK, 0)

            def norm(base, res, params, s_params, s_mean, s_root, s_done, s_res):
                dve.wait_ge(s_half, base + RING)
                dve.wait_ge(s_res, 16)
                for t in range(NT):
                    for q in range(4):
                        part = res[:, t, q * 512:(q + 1) * 512]
                        ins = dve.scalar_tensor_tensor(part, part, ALPHA, ps[:, 4 * t + q, :], ALU.mult, ALU.add,
                                                       accum_out=row_sums[:, 4 * t + q:4 * t + q + 1])
                    link(ins)
                    link(dve.tensor_reduce(row_sum[:, t:t + 1], row_sums[:, 4 * t:4 * t + 4], AX.X, ALU.add))
                    dve.tensor_scalar(neg_mean[:, t:t + 1], row_sum[:, t:t + 1], -1.0 / D, None,
                                      ALU.mult).then_inc(s_mean, 1)
                dve.wait_ge(s_params, 32)
                for t in range(NT):
                    dve.wait_ge(s_mean, t + 1)
                    dve.scalar_tensor_tensor(norm_mid[t], res[:, t, :], neg_mean[:, t:t + 1], params[0],
                                             ALU.add, ALU.mult)
                    dve.wait_ge(s_root, t + 1)
                    link(dve.reciprocal(rstd[:, t:t + 1], rstd[:, t:t + 1]))
                    for h in range(2):
                        cols = slice(h * 1024, h * 1024 + 1024)
                        dve.scalar_tensor_tensor(res[:, t, cols], norm_mid[t][:, cols], rstd[:, t:t + 1],
                                                 params[1][:, cols], ALU.mult, ALU.add).then_inc(s_done, 1)

            norm(BASE["wq"], xn, gb, s_gb, s_lnv, s_lnr, s_x1, s_xn)

            for q in range(8):
                dve.wait_ge(s_x1t, q + 1)
                low_of(x_hl, ps[:, q % 4, :], 512 * q, 512 * q + 512, 20 + q + 1)
            lows_of("wq", 16)

            BIG = -3e38
            ones16 = iota[:, 0:TOPK]
            for t in range(NT):
                dve.wait_ge(s_psc, 4 * (t + 1))
                idx = idx_u.rearrange("p (h c k) -> p h c k", h=PEER_HEADS, c=2)
                for h in range(PEER_HEADS):
                    for c in range(2):
                        src = sc[:, t, (2 * h + c) * P:(2 * h + c + 1) * P]
                        link(dve.max(vals[:, h, c, 0:8], src))
                        dve.max_index(idx[:, h, c, 0:8], vals[:, h, c, 0:8], src)
                        link(dve.match_replace(seg, vals[:, h, c, 0:8], src, BIG))
                        link(dve.max(vals[:, h, c, 8:16], seg))
                        link(dve.max_index(idx[:, h, c, 8:16], vals[:, h, c, 8:16], seg))
                for h in range(PEER_HEADS):
                    cv = comb.rearrange("p (a b) -> p a b", a=TOPK)
                    link(dve.tensor_tensor(cv, vals[:, h, 0, :].unsqueeze(2).to_broadcast([P, TOPK, TOPK]),
                                           vals[:, h, 1, :].unsqueeze(1).to_broadcast([P, TOPK, TOPK]), ALU.add))
                    f, z = fin[:, h * TOPK:(h + 1) * TOPK], pos_u[:, h * TOPK:(h + 1) * TOPK]
                    link(dve.max(f[:, 0:8], comb))
                    dve.max_index(z[:, 0:8], f[:, 0:8], comb)
                    link(dve.match_replace(comb2, f[:, 0:8], comb, BIG))
                    link(dve.max(f[:, 8:16], comb2))
                    link(dve.max_index(z[:, 8:16], f[:, 8:16], comb2))
                link(dve.tensor_copy(idx_f.rearrange("p h c k -> p (h c k)"), idx_u))
                work = sc[:, t, :]
                for c in range(2):
                    if c == 0:
                        link(dve.tensor_scalar(pab_u, pos_u, 4, None, ALU.logical_shift_right))
                    else:
                        link(dve.tensor_scalar(pab_u, pos_u, 15, None, ALU.bitwise_and))
                    link(dve.tensor_copy(pab_f, pab_u))
                    wv = work.rearrange("p (n a) -> p n a", a=TOPK)
                    link(dve.tensor_tensor(wv, pab_f.unsqueeze(2).to_broadcast([P, PICKS, TOPK]),
                                           ones16.unsqueeze(1).to_broadcast([P, PICKS, TOPK]), ALU.is_equal))
                    w4 = work.rearrange("p (h k a) -> p h k a", h=PEER_HEADS, k=TOPK)
                    link(dve.tensor_tensor(w4, w4, idx_f[:, :, c, :].unsqueeze(2)
                                           .to_broadcast([P, PEER_HEADS, TOPK, TOPK]), ALU.mult))
                    link(dve.tensor_reduce(nat[:, t, c, :], wv, AX.X, ALU.add))
                f3 = fin.rearrange("p (h k) -> p h k", h=PEER_HEADS)
                ins = dve.tensor_tensor(nat[:, t, 2, :].rearrange("p (h k) -> p h k", h=PEER_HEADS), f3,
                                        f3[:, :, 0:1].to_broadcast([P, PEER_HEADS, TOPK]), ALU.subtract)
                if t == NT - 1:
                    ins.then_inc(s_tke, 1)
                else:
                    link(ins)
            dve.wait_ge(s_tkx, 1)
            for t in range(NT):
                g3 = nat[:, t, 2, :].rearrange("p (h k) -> p h k", h=PEER_HEADS)
                link(dve.tensor_reduce(den[:, t * 8:t * 8 + 8], g3, AX.X, ALU.add))
                link(dve.reciprocal(den[:, t * 8:t * 8 + 8], den[:, t * 8:t * 8 + 8]))
                ins = dve.tensor_tensor(g3, g3, den[:, t * 8:t * 8 + 8].unsqueeze(2)
                                        .to_broadcast([P, PEER_HEADS, TOPK]), ALU.mult)
            ins.then_inc(s_nat, 1)

            dve.wait_ge(s_lo, Half("u", 0, 0, 1).split + POOL_HALVES)
            lows_of("u", 64, 64)
            dve.wait_ge(s_pick, 3)
            dve.wait_ge(s_evac, RING + EVAC["u"] + NKEYS)

            def one_hots(dst, k, i, b):
                keys_of = pick_t[:, k, :][:, bass.ds(i * (HB * HOT) + b * HOT, HOT)]
                return dve.tensor_tensor(dst.rearrange("p (a n) -> p a n", a=HOT),
                                         iota.unsqueeze(1).to_broadcast([P, HOT, P]),
                                         keys_of.unsqueeze(2).to_broadcast([P, HOT, P]), ALU.is_equal)

            def make_keys(i, b, first):
                if not first:
                    dve.wait_ge(s_hotg if b % 2 else s_hotgp, i * 2 + (b // 2 - 1))
                one_hots(hot1[b], 0, i, b).then_inc(s_hot1, 1)
                if b == 0:
                    if not first:
                        dve.wait_ge(s_g, i * HB + (b + 1 - HB))
                    one_hots(hot2[b], 1, i, b).then_inc(s_hot2v, 1)

            def weigh(i, b):
                dve.wait_ge(s_g, i * HB + (b + 1))
                part = hx[:, :, bass.ds(i * (HB * HOT) + b * HOT, HOT)].rearrange("p j a -> p a j")
                dve.tensor_tensor(part, ps[:, b, :].rearrange("p (a j) -> p a j", a=HOT), part,
                                  ALU.mult).then_inc(s_w, 1)

            for b in range(HB):
                make_keys(0, b, True)
            with dve.Fori(1, T // (HB * HOT)) as i:
                for b in range(HB):
                    weigh(i - 1, b)
                    make_keys(i, b, False)
            for b in range(HB):
                weigh(T // (HB * HOT) - 1, b)

            dve.wait_ge(s_w, HB + T // HOT)
            wide("v_tab", NKEYS, at(O_H, NKEYS * T), O_X, 16)

            norm(HALVES, x1n, gb2, s_gb2, s_lnv2, s_lnr2, s_fin, s_x1l)


def _column_chunks(w):
    n = w.shape[1] // P
    return w.reshape(2, DC // 2, P, n, P).transpose(3, 0, 2, 1, 4).reshape(2 * n, P, HW)


def kernel(**inputs):
    import concourse.bacc as bacc
    from concourse.bass_utils import run_bass_kernel_spmd

    a = {k: np.asarray(v) for k, v in inputs.items()}
    w_in = a["w_in"][0]
    widths = [1024, 1024, 1024, 1024, 1536, 48, 1024, 3 * D]
    edge = np.concatenate([[0], np.cumsum(widths)])
    aq, ak, av, bq, bkv, bg, mq, merge = (slice(edge[i], edge[i + 1]) for i in range(8))
    order = [8 * j + 4 * e + i for j in range(2) for i in range(B_HPG) for e in range(2)]
    perm = np.concatenate([np.arange(B_DH) + B_DH * h for h in order])
    kv = w_in[:, bkv].reshape(D, 3, 2, 256)
    qk_w = np.concatenate([w_in[:, aq], w_in[:, bq][:, perm], w_in[:, mq], w_in[:, ak],
                           kv[:, 1, 0], kv[:, 2, 0], kv[:, 0, 0], kv[:, 0, 1]], axis=1)
    v_nsa = np.concatenate([kv[:, 1, 1], kv[:, 2, 1]], axis=1)
    w1 = a["cmp_w1"][0].reshape(2, 4, 4, P, CMP_HIDDEN).transpose(0, 1, 3, 2, 4).reshape(8, P, HW)
    u = a["peer_u"][0].reshape(NKEYS, NKEYS, 2, 8, P).transpose(1, 2, 4, 3, 0).reshape(2 * NKEYS, P, HW)
    v = a["peer_v"][0].reshape(NKEYS, NKEYS, 2, HW).transpose(1, 2, 0, 3).reshape(2 * NKEYS, P, HW)
    mem_kv = a["w_mem_kv"][0]
    wbr = a["w_branch"][0].copy()
    wbr[1] = wbr[1][perm]
    w_up = wbr.reshape(3, MIX_C, P, DC, P).transpose(0, 3, 2, 1, 4).reshape(48, 1, P, HW)
    merged = np.concatenate([_column_chunks(w_in[:, merge]).reshape(48, 2, P, HW), w_up], axis=1)
    stream = np.concatenate([
        _column_chunks(mem_kv[:, 0:1024]), mem_kv[:, 1024:2048].reshape(DC, P, HW), _column_chunks(qk_w), w1,
        w_in[:, av].reshape(DC, P, HW), v_nsa.reshape(DC // 2, 2, P, 512).transpose(0, 2, 1, 3).reshape(-1, P, HW),
        merged.reshape(144, P, HW),
        a["w_out"][0].reshape(DC, P, 2, HW).transpose(0, 2, 1, 3).reshape(2 * DC, P, HW),
        _column_chunks(a["peer_wq"][0]), u, v])

    def rows_to_parts(m2):
        return np.ascontiguousarray(m2.reshape(DC, P, -1).transpose(1, 0, 2)).reshape(P, -1)

    onehot = np.zeros((BUCKETS, T), np.float32)
    onehot[rel_buckets()[::-1], np.arange(T)] = 1.0
    tpos = np.arange(T)
    ok = (np.arange(N_CMP) * CMP_STRIDE + CMP_LEN - 1)[None, :] <= tpos[:, None]
    ok = ok.reshape(NT, P, N_CMP).transpose(1, 0, 2)
    mask = np.stack([np.where(ok, 0.0, NEG), np.where(ok, 1.0, 0.0)], axis=1).astype(np.float32)
    arrays = {
        "x": a["x"], "x_t": rows_to_parts(a["x"][0].T), "mem_t": rows_to_parts(a["mem"][0].T),
        "stream": stream, "w_gate": rows_to_parts(w_in[:, bg]).reshape(P, DC, 48),
        "tab": a["rel_bias"], "buckets_rev": onehot, "lam": a["diff_lambda"].reshape(1, 256),
        "subln": a["diff_subln"].reshape(P, 1),
        "pe_cols": a["cmp_pe"][0].reshape(2, 16, P).transpose(2, 0, 1),
        "w2": a["cmp_w2"][0].reshape(2, 2, P, B_DH).transpose(2, 0, 1, 3),
        "keys_t": a["peer_keys"][0].reshape(DC, NKEYS, P).transpose(2, 0, 1),
        "ln1_g": a["ln1_g"], "ln1_b": a["ln1_b"], "ln2_g": a["ln2_g"], "ln2_b": a["ln2_b"],
        "identity": np.eye(P, dtype=np.float32), "flip": np.eye(P, dtype=np.float32)[::-1],
        "cmp_mask": mask, "iotas": np.broadcast_to(np.arange(P, dtype=np.float32), (P, P)),
    }
    arrays = {k: np.ascontiguousarray(val) for k, val in arrays.items()}
    nc = bacc.Bacc("TRN2", target_bir_lowering=False, num_devices=1)
    args = [nc.dram_tensor(f"in_{k}", val.shape, mybir.dt.from_np(val.dtype), kind="ExternalInput").ap()
            for k, val in arrays.items()]
    args.append(nc.dram_tensor("out", (1, T, D), F32, kind="ExternalOutput").ap())
    build(nc, *args)
    r = run_bass_kernel_spmd(nc, [{f"in_{k}": val for k, val in arrays.items()}], core_ids=[0])
    return r.results[0]["out"]
```
